# Optimizing a Trainium2 kernel written in Bass

```python
import math
import jax, jax.numpy as jnp
from jax import lax
import numpy as np

D_MODEL = 1024
BATCH = 1
SEQ = 256
DEPTH = 1

EPS = 1e-6
A_GROUPS = 8
A_GROUP_DIM = D_MODEL // A_GROUPS
A_WIDTH = A_GROUPS * A_GROUP_DIM
CHUNK = 128
B_HEADS = 8
B_HEAD_DIM = D_MODEL // 16
B_V_DIM = 2 * B_HEAD_DIM
QK_WIDTH = B_HEADS * 2 * B_HEAD_DIM
B_WIDTH = B_HEADS * B_V_DIM
Q_BLOCK = 128
IN_COLS = 2 * A_WIDTH + 2 * QK_WIDTH + B_WIDTH
N_GROUPS = 4
EXPERTS_PER_GROUP = 8
N_EXPERTS = N_GROUPS * EXPERTS_PER_GROUP
TOP_K = 2
D_EXPERT = D_MODEL // 4
MOE_BLOCK = 128


def rmsnorm(x, g):
    xf = x.astype(jnp.float32)
    r = lax.rsqrt(jnp.mean(xf * xf, axis=-1, keepdims=True) + EPS)
    return (xf * r).astype(x.dtype) * g

def chunked_spatial_gating(u, v, g_v, w_s, b_s):
    bsz, s, _ = u.shape
    nc = s // CHUNK
    v = rmsnorm(v.reshape(bsz, s, A_GROUPS, A_GROUP_DIM), g_v)
    v = v.reshape(bsz, nc, CHUNK, A_GROUPS, A_GROUP_DIM)
    causal = jnp.tril(jnp.ones((CHUNK, CHUNK), dtype=bool))
    ws = jnp.where(causal[None], w_s, 0.0)
    z = jnp.einsum('gts,bcsgd->bctgd', ws, v) + b_s.T[None, None, :, :, None]
    return u * z.reshape(bsz, s, A_WIDTH)

def diff_attention(q, k, v, lam, slopes):
    bsz, nh, _, s, hd = q.shape
    nb = s // Q_BLOCK
    key_pos = jnp.arange(s)
    scale = hd ** -0.5

    def block(i):
        start = i * Q_BLOCK
        qb = lax.dynamic_slice_in_dim(q, start, Q_BLOCK, axis=3)
        sc = jnp.einsum('bhcqd,bhckd->bhcqk', qb, k,
                        preferred_element_type=jnp.float32) * scale
        q_pos = start + jnp.arange(Q_BLOCK)
        dist = (q_pos[:, None] - key_pos[None, :]).astype(jnp.float32)
        alibi = -slopes[:, None, None] * jnp.abs(dist)[None]
        sc = jnp.where((dist >= 0)[None, None, None], sc + alibi[None, :, None], -jnp.inf)
        p = jax.nn.softmax(sc, axis=-1)
        a = p[:, :, 0] - lam * p[:, :, 1]
        return jnp.einsum('bhqk,bhkd->bhqd', a.astype(v.dtype), v)

    out = lax.map(block, jnp.arange(nb))
    return out.transpose(1, 2, 0, 3, 4).reshape(bsz, nh, s, v.shape[-1])

def hierarchical_moe(h, w_rg, b_rg, w_re, b_re, w1, w3, w2):
    bsz, s, d = h.shape
    t = h.reshape(-1, d)
    n_tok = t.shape[0]
    g_prob = jax.nn.softmax((t @ w_rg + b_rg).astype(jnp.float32), axis=-1)
    g_gate, g_idx = lax.top_k(g_prob, 1)
    e_logits = (t @ w_re + b_re).astype(jnp.float32).reshape(n_tok, N_GROUPS, EXPERTS_PER_GROUP)
    e_logits = jnp.take_along_axis(e_logits, g_idx[:, :, None], axis=1)[:, 0]
    e_w, e_idx = lax.top_k(jax.nn.softmax(e_logits, axis=-1), TOP_K)
    e_w = e_w / jnp.sum(e_w, axis=-1, keepdims=True)
    weight = g_gate * e_w
    expert_id = g_idx * EXPERTS_PER_GROUP + e_idx
    combine = jnp.sum(jax.nn.one_hot(expert_id, N_EXPERTS, dtype=jnp.float32)
                      * weight[..., None], axis=1)

    def expert_block(args):
        tk, c = args
        hid = jax.nn.silu(jnp.einsum('td,edf->tef', tk, w1)) * jnp.einsum('td,edf->tef', tk, w3)
        hid = hid * c[:, :, None].astype(hid.dtype)
        return jnp.einsum('tef,efd->td', hid, w2)

    y = lax.map(expert_block, (t.reshape(-1, MOE_BLOCK, d),
                               combine.reshape(-1, MOE_BLOCK, N_EXPERTS)))
    return y.reshape(bsz, s, d)

def first_inputs(seed: int = 0) -> dict:
    key = jax.random.key(seed)
    ks = jax.random.split(key, 32)
    f32 = jnp.float32
    L, D = DEPTH, D_MODEL

    def nrm(k, shape, scale):
        return jax.random.normal(k, shape, f32) * scale

    def gain(k, shape):
        return 1.0 + 0.02 * jax.random.normal(k, shape, f32)

    return {
        "x": jax.random.normal(ks[0], (BATCH, SEQ, D), f32),
        "norm1_g": gain(ks[1], (L, D)),
        "w_in": nrm(ks[2], (L, D, IN_COLS), D ** -0.5),
        "v_norm_g": gain(ks[3], (L, A_GROUPS, A_GROUP_DIM)),
        "w_s": nrm(ks[4], (L, A_GROUPS, CHUNK, CHUNK), CHUNK ** -0.5),
        "b_s": 1.0 + 0.02 * jax.random.normal(ks[5], (L, A_GROUPS, CHUNK), f32),
        "q_norm_g": gain(ks[6], (L, B_HEAD_DIM)),
        "k_norm_g": gain(ks[7], (L, B_HEAD_DIM)),
        "lambda_q1": nrm(ks[8], (L, B_HEAD_DIM), 0.1),
        "lambda_k1": nrm(ks[9], (L, B_HEAD_DIM), 0.1),
        "lambda_q2": nrm(ks[10], (L, B_HEAD_DIM), 0.1),
        "lambda_k2": nrm(ks[11], (L, B_HEAD_DIM), 0.1),
        "sub_norm_g": gain(ks[12], (L, B_V_DIM)),
        "w_up_a": nrm(ks[13], (L, A_WIDTH, D), A_WIDTH ** -0.5),
        "w_up_b": nrm(ks[14], (L, B_WIDTH, D), B_WIDTH ** -0.5),
        "w_gate": nrm(ks[15], (L, D, 2 * D), D ** -0.5),
        "b_gate": nrm(ks[16], (L, 2 * D), 0.02),
        "w_out": nrm(ks[17], (L, D, D), D ** -0.5),
        "norm2_g": gain(ks[18], (L, D)),
        "w_rg": nrm(ks[19], (L, D, N_GROUPS), D ** -0.5),
        "b_rg": nrm(ks[20], (L, N_GROUPS), 0.01),
        "w_re": nrm(ks[21], (L, D, N_EXPERTS), D ** -0.5),
        "b_re": nrm(ks[22], (L, N_EXPERTS), 0.01),
        "w1": nrm(ks[23], (L, N_EXPERTS, D, D_EXPERT), D ** -0.5),
        "w3": nrm(ks[24], (L, N_EXPERTS, D, D_EXPERT), D ** -0.5),
        "w2": nrm(ks[25], (L, N_EXPERTS, D_EXPERT, D), D_EXPERT ** -0.5),
    }

def first_block(x, norm1_g, w_in, v_norm_g, w_s, b_s, q_norm_g, k_norm_g,
              lambda_q1, lambda_k1, lambda_q2, lambda_k2, sub_norm_g,
              w_up_a, w_up_b, w_gate, b_gate, w_out, norm2_g,
              w_rg, b_rg, w_re, b_re, w1, w3, w2):
    bsz, s, d = x.shape
    slopes = jnp.exp2(-8.0 * (jnp.arange(B_HEADS) + 1) / B_HEADS)
    splits = [A_WIDTH, 2 * A_WIDTH, 2 * A_WIDTH + QK_WIDTH, 2 * A_WIDTH + 2 * QK_WIDTH]
    for l in range(DEPTH):
        lam_init = 0.8 - 0.6 * math.exp(-0.3 * l)
        h = rmsnorm(x, norm1_g[l])
        proj = h @ w_in[l]
        u, v_a, q, k, v_b = jnp.split(proj, splits, axis=-1)

        y_a = chunked_spatial_gating(u, v_a, v_norm_g[l], w_s[l], b_s[l])

        q = rmsnorm(q.reshape(bsz, s, B_HEADS, 2, B_HEAD_DIM), q_norm_g[l]).transpose(0, 2, 3, 1, 4)
        k = rmsnorm(k.reshape(bsz, s, B_HEADS, 2, B_HEAD_DIM), k_norm_g[l]).transpose(0, 2, 3, 1, 4)
        vb = v_b.reshape(bsz, s, B_HEADS, B_V_DIM).transpose(0, 2, 1, 3)
        lam = (jnp.exp(jnp.sum(lambda_q1[l].astype(jnp.float32) * lambda_k1[l].astype(jnp.float32)))
               - jnp.exp(jnp.sum(lambda_q2[l].astype(jnp.float32) * lambda_k2[l].astype(jnp.float32)))
               + lam_init)
        o = diff_attention(q, k, vb, lam, slopes)
        o = rmsnorm(o, sub_norm_g[l]) * (1.0 - lam_init)
        y_b = o.transpose(0, 2, 1, 3).reshape(bsz, s, B_WIDTH)

        gates = jax.nn.sigmoid(h @ w_gate[l] + b_gate[l])
        g_a, g_b = jnp.split(gates, 2, axis=-1)
        merged = g_a * (y_a @ w_up_a[l]) + g_b * (y_b @ w_up_b[l])
        x = x + merged @ w_out[l]

        h2 = rmsnorm(x, norm2_g[l])
        x = x + hierarchical_moe(h2, w_rg[l], b_rg[l], w_re[l], b_re[l], w1[l], w3[l], w2[l])
    return x


DEPTH_2 = 2

GRID_W = 64
CTX_LEN = 256
HEAD_DIM = 64
ATTN_W = D_MODEL // 2
N_Q_HEADS = ATTN_W // HEAD_DIM
N_KV_HEADS = N_Q_HEADS // 4
Q_PER_KV = N_Q_HEADS // N_KV_HEADS
KV_W = N_KV_HEADS * HEAD_DIM
POOL_W = D_MODEL // 4
POOL_WINDOWS = (2, 4, 8, 16)
N_POOL_GROUPS = len(POOL_WINDOWS)
POOL_GROUP_W = POOL_W // N_POOL_GROUPS
FFT_W = D_MODEL // 4
N_FFT_GROUPS = 4
FFT_GROUP_W = FFT_W // N_FFT_GROUPS
MIX_W = ATTN_W + POOL_W + FFT_W
IN_W = ATTN_W + 2 * KV_W + POOL_W + FFT_W
D_FF = ((8 * D_MODEL // 3 + 127) // 128) * 128
ROPE_THETA = 10000.0
N_MOD = 9
ATTN_SCALE = HEAD_DIM ** -0.5


def rms_norm(x):
    xf = x.astype(jnp.float32)
    return (xf * lax.rsqrt(jnp.mean(xf * xf, axis=-1, keepdims=True) + EPS)).astype(x.dtype)

def modulate(h, shift, scale):
    return h * (1 + scale[:, None, :]) + shift[:, None, :]

def swiglu(h, w_gu, w_down):
    g, u = jnp.split(h @ w_gu, 2, axis=-1)
    return (jax.nn.silu(g) * u) @ w_down

def axial_rope_tables(length):
    rows = length // GRID_W
    row = jnp.repeat(jnp.arange(rows), GRID_W).astype(jnp.float32)
    col = jnp.tile(jnp.arange(GRID_W), rows).astype(jnp.float32)
    n_freq = HEAD_DIM // 4
    inv_freq = ROPE_THETA ** (-jnp.arange(n_freq, dtype=jnp.float32) / n_freq)
    ang = jnp.concatenate([row[:, None] * inv_freq, col[:, None] * inv_freq], axis=-1)
    return jnp.cos(ang), jnp.sin(ang)

def apply_rope(x, cos, sin):
    shape = (1, cos.shape[0]) + (1,) * (x.ndim - 3) + (cos.shape[1],)
    cos = cos.reshape(shape).astype(x.dtype)
    sin = sin.reshape(shape).astype(x.dtype)
    half = HEAD_DIM // 2
    x1, x2 = x[..., :half], x[..., half:]
    return jnp.concatenate([x1 * cos - x2 * sin, x1 * sin + x2 * cos], axis=-1)

def split_in(z):
    b = [ATTN_W, ATTN_W + KV_W, ATTN_W + 2 * KV_W, ATTN_W + 2 * KV_W + POOL_W]
    return jnp.split(z, b, axis=-1)

def q_heads(q, gain):
    q = q.reshape(q.shape[:2] + (N_KV_HEADS, Q_PER_KV, HEAD_DIM))
    return rms_norm(q) * gain

def kv_heads(t):
    return t.reshape(t.shape[:2] + (N_KV_HEADS, HEAD_DIM))

def attend_latent(q, k, v, k_ctx, v_ctx):
    k_all = jnp.concatenate([k, k_ctx], axis=1)
    v_all = jnp.concatenate([v, v_ctx], axis=1)
    bsz, length = q.shape[:2]
    n_blk = length // Q_BLOCK
    qb = q.reshape((bsz, n_blk, Q_BLOCK) + q.shape[2:]).transpose(1, 0, 2, 3, 4, 5)

    def one_block(q_blk):
        s = jnp.einsum('bqkgd,bskd->bkgqs', q_blk, k_all).astype(jnp.float32) * ATTN_SCALE
        p = jax.nn.softmax(s, axis=-1).astype(v_all.dtype)
        return jnp.einsum('bkgqs,bskd->bqkgd', p, v_all)

    o = lax.map(one_block, qb)
    return o.transpose(1, 0, 2, 3, 4, 5).reshape(bsz, length, ATTN_W)

def attend_context(q, k, v):
    s = jnp.einsum('bqkgd,bskd->bkgqs', q, k).astype(jnp.float32) * ATTN_SCALE
    p = jax.nn.softmax(s, axis=-1).astype(v.dtype)
    o = jnp.einsum('bkgqs,bskd->bqkgd', p, v)
    return o.reshape(q.shape[0], q.shape[1], ATTN_W)

def pool_minus_self(u):
    bsz, length, _ = u.shape
    ug = u.reshape(bsz, length, N_POOL_GROUPS, POOL_GROUP_W).astype(jnp.float32)
    cs = jnp.cumsum(ug, axis=1)
    cs = jnp.concatenate([jnp.zeros_like(cs[:, :1]), cs], axis=1)
    t = jnp.arange(length)
    means = []
    for g, w in enumerate(POOL_WINDOWS):
        lo = jnp.clip(t - w // 2, 0, length)
        hi = jnp.clip(t + w - w // 2, 0, length)
        cs_g = cs[:, :, g]
        s = jnp.take(cs_g, hi, axis=1) - jnp.take(cs_g, lo, axis=1)
        cnt = (hi - lo).astype(jnp.float32)[None, :, None]
        means.append(s / cnt)
    mean = jnp.stack(means, axis=2)
    return (mean - ug).astype(u.dtype)

def fourier_2d(u):
    bsz, length, _ = u.shape
    ug = u.reshape(bsz, length, N_FFT_GROUPS, FFT_GROUP_W).astype(jnp.float32)
    f = jnp.fft.fft2(ug, axes=(1, 3), norm='ortho').real
    return f.reshape(bsz, length, FFT_W).astype(u.dtype)

def merge_mixers(attn_out, u_pool, u_fft, pool_w_l, pool_scale_l, fft_w_l, w_out_l):
    bsz, length, _ = u_pool.shape
    yp = jnp.einsum('blgc,gcd->blgd', pool_minus_self(u_pool), pool_w_l).reshape(bsz, length, POOL_W) * pool_scale_l
    yf = fourier_2d(u_fft) @ fft_w_l
    return jnp.concatenate([attn_out, yp, yf], axis=-1) @ w_out_l

def second_inputs(seed: int = 0) -> dict:
    key = jax.random.key(seed)
    ks = jax.random.split(key, 20)

    def nrm(k, shape, std):
        return jax.random.normal(k, shape, jnp.float32) * std

    return {
        'x': nrm(ks[0], (BATCH, SEQ, D_MODEL), 1.0),
        'c': nrm(ks[1], (BATCH, D_MODEL), 1.0),
        'ctx': nrm(ks[2], (BATCH, CTX_LEN, D_MODEL), 1.0),
        'c_ctx': nrm(ks[3], (D_MODEL,), 1.0),
        'ada_w': nrm(ks[4], (DEPTH_2, D_MODEL, N_MOD * D_MODEL), 0.5 * D_MODEL ** -0.5),
        'ada_b': nrm(ks[5], (DEPTH_2, N_MOD * D_MODEL), 0.01),
        'ffn1_w_gu': nrm(ks[6], (DEPTH_2, D_MODEL, 2 * D_FF), D_MODEL ** -0.5),
        'ffn1_w_down': nrm(ks[7], (DEPTH_2, D_FF, D_MODEL), D_FF ** -0.5),
        'w_in': nrm(ks[8], (DEPTH_2, D_MODEL, IN_W), D_MODEL ** -0.5),
        'q_gain': 1.0 + nrm(ks[9], (DEPTH_2, HEAD_DIM), 0.1),
        'k_gain': 1.0 + nrm(ks[10], (DEPTH_2, HEAD_DIM), 0.1),
        'pool_w': nrm(ks[11], (DEPTH_2, N_POOL_GROUPS, POOL_GROUP_W, POOL_GROUP_W), POOL_GROUP_W ** -0.5),
        'pool_scale': 1.0 + nrm(ks[12], (DEPTH_2, POOL_W), 0.1),
        'fft_w': nrm(ks[13], (DEPTH_2, FFT_W, FFT_W), FFT_W ** -0.5),
        'w_out': nrm(ks[14], (DEPTH_2, MIX_W, D_MODEL), MIX_W ** -0.5),
        'ffn2_w_gu': nrm(ks[15], (DEPTH_2, D_MODEL, 2 * D_FF), D_MODEL ** -0.5),
        'ffn2_w_down': nrm(ks[16], (DEPTH_2, D_FF, D_MODEL), D_FF ** -0.5),
        'final_gain': 1.0 + nrm(ks[17], (D_MODEL,), 0.1),
    }

def second_block(x, c, ctx, c_ctx, ada_w, ada_b, ffn1_w_gu, ffn1_w_down, w_in, q_gain, k_gain,
              pool_w, pool_scale, fft_w, w_out, ffn2_w_gu, ffn2_w_down, final_gain):
    cos, sin = axial_rope_tables(x.shape[1])
    for layer in range(DEPTH_2):
        last = layer == DEPTH_2 - 1
        mx = jnp.split(jax.nn.silu(c) @ ada_w[layer] + ada_b[layer], N_MOD, axis=-1)
        mc = jnp.split((jax.nn.silu(c_ctx) @ ada_w[layer] + ada_b[layer])[None, :], N_MOD, axis=-1)

        x = x + 0.5 * mx[2][:, None] * swiglu(modulate(rms_norm(x), mx[0], mx[1]), ffn1_w_gu[layer], ffn1_w_down[layer])
        ctx = ctx + 0.5 * mc[2][:, None] * swiglu(modulate(rms_norm(ctx), mc[0], mc[1]), ffn1_w_gu[layer], ffn1_w_down[layer])

        hx = modulate(rms_norm(x), mx[3], mx[4])
        hc = modulate(rms_norm(ctx), mc[3], mc[4])
        if last:
            kc, vc = jnp.split(hc @ w_in[layer, :, ATTN_W:ATTN_W + 2 * KV_W], 2, axis=-1)
        else:
            qc, kc, vc, upc, ufc = split_in(hc @ w_in[layer])
        kc = rms_norm(kv_heads(kc)) * k_gain[layer]
        vc = kv_heads(vc)

        qx, kx, vx, upx, ufx = split_in(hx @ w_in[layer])
        qx = apply_rope(q_heads(qx, q_gain[layer]), cos, sin)
        kx = apply_rope(rms_norm(kv_heads(kx)) * k_gain[layer], cos, sin)
        vx = kv_heads(vx)
        ax = attend_latent(qx, kx, vx, kc, vc)
        x = x + mx[5][:, None] * merge_mixers(ax, upx, ufx, pool_w[layer], pool_scale[layer], fft_w[layer], w_out[layer])

        x = x + 0.5 * mx[8][:, None] * swiglu(modulate(rms_norm(x), mx[6], mx[7]), ffn2_w_gu[layer], ffn2_w_down[layer])

        if not last:
            ac = attend_context(q_heads(qc, q_gain[layer]), kc, vc)
            ctx = ctx + mc[5][:, None] * merge_mixers(ac, upc, ufc, pool_w[layer], pool_scale[layer], fft_w[layer], w_out[layer])
            ctx = ctx + 0.5 * mc[8][:, None] * swiglu(modulate(rms_norm(ctx), mc[6], mc[7]), ffn2_w_gu[layer], ffn2_w_down[layer])

    return rms_norm(x) * final_gain


def setup_inputs(seed=0):
    out = dict(first_inputs(seed))
    for name, value in second_inputs(seed + 1).items():
        if name != "x":
            out[name + "_2"] = value
    return out


def reference(
    x, norm1_g, w_in, v_norm_g, w_s, b_s, q_norm_g, k_norm_g, lambda_q1, lambda_k1, lambda_q2,
    lambda_k2, sub_norm_g, w_up_a, w_up_b, w_gate, b_gate, w_out, norm2_g, w_rg, b_rg, w_re,
    b_re, w1, w3, w2, c_2, ctx_2, c_ctx_2, ada_w_2, ada_b_2, ffn1_w_gu_2, ffn1_w_down_2, w_in_2,
    q_gain_2, k_gain_2, pool_w_2, pool_scale_2, fft_w_2, w_out_2, ffn2_w_gu_2, ffn2_w_down_2,
    final_gain_2,
):
    x = first_block(
        x, norm1_g, w_in, v_norm_g, w_s, b_s, q_norm_g, k_norm_g, lambda_q1, lambda_k1,
        lambda_q2, lambda_k2, sub_norm_g, w_up_a, w_up_b, w_gate, b_gate, w_out, norm2_g, w_rg,
        b_rg, w_re, b_re, w1, w3, w2,
    )
    return second_block(
        x, c_2, ctx_2, c_ctx_2, ada_w_2, ada_b_2, ffn1_w_gu_2, ffn1_w_down_2, w_in_2, q_gain_2,
        k_gain_2, pool_w_2, pool_scale_2, fft_w_2, w_out_2, ffn2_w_gu_2, ffn2_w_down_2,
        final_gain_2,
    )


_drawn_inputs = setup_inputs


def setup_inputs(seed=0):
    import zlib

    import numpy as np

    out = dict(_drawn_inputs(seed))
    spreads = {}
    factors = {'v_norm_g': 14.325,
     'b_s': 8.96,
     'q_norm_g': 4.628,
     'k_norm_g': 3.259,
     'lambda_k1': 8.0,
     'lambda_q2': 8.0,
     'sub_norm_g': 12.29,
     'b_gate': 3.435,
     'b_rg': 31.397,
     'b_re': 17.588,
     'ctx_2': 4.879,
     'ada_b_2': 18.107,
     'q_gain_2': 40.918,
     'k_gain_2': 37.606,
     'pool_scale_2': 28.456,
     'norm2_g': 3.868,
     'c_ctx_2': 3.094,
     'ffn1_w_gu_2': 3.885,
     'ffn1_w_down_2': 3.96,
     'fft_w_2': 3.798,
     'ffn2_w_gu_2': 3.929,
     'ffn2_w_down_2': 3.912}
    for name, (base, spread) in spreads.items():
        noise = np.random.default_rng([zlib.crc32(name.encode()), seed]).standard_normal(out[name].shape)
        drawn = base * np.exp(spread * noise) if base else spread * noise
        out[name] = __import__('jax').numpy.asarray(drawn.astype(out[name].dtype))
    for name, factor in factors.items():
        out[name] = (out[name] * factor).astype(out[name].dtype)
    return out
```

```python
import math
from collections import Counter
from contextlib import ExitStack, contextmanager

from concourse import mybir

F32 = mybir.dt.float32
F32R = mybir.dt.float32r
ACT = mybir.ActivationFunctionType
ALU = mybir.AluOpType
AX = mybir.AxisListType.X

P = 128
D = 1024
KT = D // P
S = 256
TB = S // P
EPS = 1e-6
HEADS = 8
LAM_INIT = 0.8 - 0.6
N_GROUPS, PER_GROUP = 4, 8
N_EXPERTS = N_GROUPS * PER_GROUP
FE = D // 4
LAYERS = 2
D_FF = ((8 * D // 3 + 127) // 128) * 128
FT_HALF = D_FF // P // 2
N_MOD = 9
MODT = N_MOD * KT
HD = 64
BIG = 1e30

RAW_SLOTS = 4
HI_SLOTS = 2
CHUNK = 2048
SPLIT = CHUNK

N1, N2, BG, VG, CV, PS, FG, SN, QN, KN, QG2, KG2, N_COLS = 0, 8, 16, 32, 40, 56, 60, 68, 69, 70, 71, 73, 75
IDENT, MEAN_D, MEAN_P, MEAN_HD, ROT, DUP0, DUP1, DFT_C, DFT_S, N_MATS = range(10)

MOE_ORDER = [("w1", 0), ("w3", 0), ("w1", 1), ("w3", 1), ("w2", 0), ("w1", 2), ("w3", 2), ("w2", 1),
             ("w1", 3), ("w3", 3), ("w2", 2), ("w2", 3)]


START = {"gated": 1, "mod_read": 1, "silu_ready": 1}


class Tally:

    def __init__(self, eng):
        self.eng, self.n, self.turn, self.per = eng, Counter(START), None, {}
        self.pos = self.used = 0

    def at(self, key, back=0):
        v = self.n[key] - back
        if self.turn is not None and self.per.get(key):
            v = self.turn * self.per[key] + v
        return v

    def next(self, key, by=1):
        self.n[key] += by
        return self.at(key)

    @contextmanager
    def loop(self, turns, per):
        before = Counter(self.n)
        with self.eng.Fori(0, turns) as i:
            self.turn, self.per = i, per
            yield i
        self.turn = None
        grown = {k: v - before[k] for k, v in self.n.items() if v != before[k]}
        assert grown == {k: v for k, v in per.items() if v}, (grown, per)
        for k, v in grown.items():
            self.n[k] += v * (turns - 1)

    def take(self):
        s = self.pos % RAW_SLOTS
        self.pos += 1
        self.next(f"fill{s}")
        return s

    def use(self):
        s = self.used % RAW_SLOTS
        self.used += 1
        return s, self.next(f"used{s}")


def ring_counts(pos, chunks, *kinds):
    out = Counter()
    for i in range(chunks):
        for kind in kinds:
            out[f"{kind}{(pos + i) % RAW_SLOTS}"] += 1
    return out


def build(nc, a, out, comb_rows):
    ctx = ExitStack()
    with ctx:
        def sem(name):
            return ctx.enter_context(nc.semaphore(name))

        base = 16512
        cursor = [base]

        def sb(name, shape, dt=F32):
            n = 4
            for d in shape[1:]:
                n *= d
            h = nc.alloc_sbuf_tensor_at(name, shape, dt, offset=cursor[0])
            cursor[0] += (n + 31) // 32 * 32
            return h

        XC = sb("XC", [P, KT, 2 * S])
        hH, hL = (sb(n, [P, KT, 2 * S], F32R) for n in ("hH", "hL"))
        raw_at = cursor[0]
        RAW = [sb(f"RAW{i}", [P, CHUNK]) for i in range(RAW_SLOTS)]
        LO = [nc.alloc_sbuf_tensor_at(f"LO{i}", [P, CHUNK], F32R, offset=raw_at + 4 * CHUNK * i)
              for i in range(RAW_SLOTS)]
        HI = [sb(f"HI{i}", [P, CHUNK], F32R) for i in range(HI_SLOTS)]
        T = [sb(f"T{i}", [P, 512]) for i in range(6)]
        SQ = T[4:6]
        R = [sb(f"R{i}", [P, 512]) for i in range(2)]
        MATS = sb("MATS", [P, N_MATS, P])
        WR = sb("WR", [P, KT, N_GROUPS + N_EXPERTS])
        BR = sb("BR", [P, N_GROUPS + N_EXPERTS])
        PT = sb("PT", [P, N_COLS])
        ADB = sb("ADB", [P, LAYERS, MODT])
        MOD = sb("MOD", [P, LAYERS, MODT, 2])
        CS = sb("CS", [P, KT, 2])
        GQ = sb("GQ", [P, 2])
        ZERO = sb("ZERO", [P, 512])
        DESC = sb("DESC", [P, N_GROUPS + PER_GROUP])
        SM, SM2 = sb("SM", [P, 32]), sb("SM2", [P, 32])
        union = cursor[0]

        def at(kb, name, shape, dt=F32):
            return nc.alloc_sbuf_tensor_at(name, shape, dt, offset=union + 1024 * kb)

        QK = at(0, "QK", [P, 2 * HEADS, S])
        MH, ML = at(0, "MH", [P, KT, S], F32R), at(8, "ML", [P, KT, S], F32R)
        VB = at(16, "VB", [P, TB, D])
        ZB = at(24, "ZB", [P, KT, S])
        VA = at(32, "VA", [P, TB, D])
        WST = at(40, "WST", [P, KT, P])
        BSB = at(44, "BSB", [P, KT, P])
        YAH, YAL = at(48, "YAH", [P, KT, S], F32R), at(56, "YAL", [P, KT, S], F32R)
        YBH, YBL = at(64, "YBH", [P, KT, S], F32R), at(72, "YBL", [P, KT, S], F32R)
        XS = at(48, "XS", [P, 2, TB, D])
        WS = at(64, "WS", [P, KT, P])
        PA = at(68, "PA", [N_COLS, P])
        PB = at(69, "PB", [MODT, LAYERS, P])
        HF1 = at(72, "HF1", [P, KT, S])
        ND = at(80, "ND", [P, TB, S])
        LV = at(82, "LV", [P, 4, HD])
        CB = at(0, "CB", [P, N_EXPERTS, S])
        HIDH = [at(32 + 4 * i, f"HIDH{i}", [P, 2, S], F32R) for i in range(2)]
        HIDL = [at(34 + 4 * i, f"HIDL{i}", [P, 2, S], F32R) for i in range(2)]
        HF2 = at(40, "HF2", [P, KT, S])
        RT = at(48, "RT", [P, 12, 2 * 36])
        CT = at(52, "CT", [N_EXPERTS, S])
        aH, aL = at(0, "aH", [P, FT_HALF, 2 * S], F32R), at(22, "aL", [P, FT_HALF, 2 * S], F32R)
        HF = at(45, "HF", [P, KT, 2 * S])
        OUTB = at(0, "OUTB", [P, TB, D])
        XH, XL = at(0, "XH", [P, KT, 2 * S], F32R), at(16, "XL", [P, KT, 2 * S], F32R)
        QQ = at(32, "QQ", [P, 5, 2 * S])
        KD = at(42, "KD", [P, 2, 2 * S])
        VD = at(46, "VD", [P, 2 * TB, 2, 2, HD])
        AB = at(58, "AB", [P, 2 * S])
        PF = at(50, "PF", [P, 2 * TB, 2, S])
        POOL = at(61, "POOL", [P, 4, TB, S])
        DFT = at(69, "DFT", [P, 2, TB, S])
        TRIG = at(73, "TRIG", [P, 2, S])
        PWB = at(75, "PWB", [P, LAYERS, 2, P])
        FW = at(77, "FW", [P, LAYERS, 2, S])
        assert union + 1024 * 83 <= nc.sbuf_usable_end, (union + 1024 * 83 - nc.sbuf_usable_end)

        B = [ctx.enter_context(nc.psum_tensor(f"B{i}", [P, 512], F32)) for i in range(8)]

        raw_loaded = [sem(f"raw_loaded{i}") for i in range(RAW_SLOTS)]
        hi_done = [sem(f"hi_done{i}") for i in range(RAW_SLOTS)]
        lo_done = [sem(f"lo_done{i}") for i in range(RAW_SLOTS)]
        slot_used = [sem(f"slot_used{i}") for i in range(RAW_SLOTS)]
        names = (
            "x_loaded rows_loaded ws_loaded mats_loaded misc_loaded mix_consts_loaded comb_stored comb_loaded out_stored "
            "params_done x_done ws_done sq_used stats_done z_done scores_done probT_done pv_done "
            "logits_done combT_done gate_done acc_done rot_done dup_done pool_done "
            "pwb_done fftab_done fft_done yf_done fin_done "
            "vec_step params_ready zeros_ready mod_read var_ready h_ready qk_ready vb_ready va_ready zb_ready ya_ready yb_ready "
            "lam_sums sc_read max_ready prob_ready up_read merged_ready logits_read top_ready m2_ready comb_ready combT_ready "
            "gated hid_ready x_ready xn_ready qn_ready q_ready mix_ready hf_done "
            "cs_ready x_copied wst_ready sq_ready std_ready qk_copied vb_copied va_copied lam_exps exp_ready probT_ready "
            "o_ready gate_ready exp4_ready exp2_ready silu_ready hf_ready q_copied kd_ready v_ready pf_ready pm_ready "
            "ab_ready ft_ready mix_hi outb_ready "
            "ws_masked pwb_zero").split()
        E = {n: sem(n) for n in names}
        dma_total = Counter()

        def mat(i):
            return MATS[:, i, :]

        def bank2(b):
            return B[b][:].rearrange("p (a n) -> p a n", a=2)

        def pair(x, j):
            return x[:, 2 * j:2 * j + 2, :].rearrange("p a n -> p (a n)")

        def attention_units(l):
            units = [(h, P * i, 0, 2 * S) for h in range(8) for i in range(TB)]
            if l + 1 < LAYERS:
                units += [(h, S + P * i, S, S) for h in range(8) for i in range(TB)]
            return units

        def bc(x, dim, shape):
            return x.unsqueeze(dim).to_broadcast(shape)

        block = ctx.enter_context(nc.Block())

        @block.sync
        def _(sp):
            t = Tally(sp)

            def chunk(first, second, words):
                s = t.take()
                if t.n[f"fill{s}"] > 1:
                    sp.wait_ge(slot_used[s], t.at(f"fill{s}", 1))
                h0 = words[0]
                sp.dma_start(RAW[s][:, 0:h0].rearrange("p (k n) -> p k n", n=first.shape[-1]), first)\
                    .then_inc(raw_loaded[s], 16)
                sp.dma_start(RAW[s][:, h0:h0 + words[1]].rearrange("p (k n) -> p k n", n=second.shape[-1]), second)\
                    .then_inc(raw_loaded[s], 16)

            def columns(w, c0):
                v = w.rearrange("(k p) n -> p k n", p=P)
                chunk(v[:, 0:4, c0:c0 + 256], v[:, 4:8, c0:c0 + 256], (1024, 1024))

            def ada(l):
                v = a["ada_w_2"][l].rearrange("(k p) (i n) -> p k i n", p=P, n=256)
                peeled = 1 if l == 0 else 0
                for c in range(4 * peeled):
                    chunk(v[:, 0:4, c, :], v[:, 4:8, c, :], (1024, 1024))
                with t.loop(MODT // 8 - peeled, ring_counts(t.pos, 4, "fill")) as i:
                    for c in range(4):
                        at_ = (i + peeled) * 4 + c
                        chunk(v[:, 0:4, at_, :], v[:, 4:8, at_, :], (1024, 1024))

            def ffn(l, gu, down):
                g = a[gu][l].rearrange("(k p) (t h n) -> p k t h n", p=P, t=2, h=2)
                w = a[down][l].rearrange("(h k p) n -> p h k n", p=P, h=2)
                with t.loop(2, ring_counts(t.pos, FT_HALF + KT, "fill")) as half:
                    for j in range(FT_HALF):
                        chunk(g[:, :, 0, half, j * P:(j + 1) * P], g[:, :, 1, half, j * P:(j + 1) * P], (1024, 1024))
                    for m in range(KT):
                        chunk(w[:, half, 0:6, m * P:(m + 1) * P], w[:, half, 6:11, m * P:(m + 1) * P], (768, 640))
                    t.pos += 1

            x_v = a["x"][0].rearrange("(b p) d -> p b d", p=P)
            c_v = a["ctx_2"][0].rearrange("(b p) d -> p b d", p=P)
            sp.dma_start(XS[:, 0], x_v).then_inc(E["x_loaded"], 16)
            sp.dma_start(XS[:, 1], c_v).then_inc(E["x_loaded"], 16)
            sp.dma_start(WS[:], a["w_s"][0].rearrange("g t s -> t g s")).then_inc(E["ws_loaded"], 16)
            for l in range(LAYERS):
                ada(l)
            w_in = a["w_in"][0]
            for c in range(8):
                columns(w_in, 2 * D + 256 * c)
            for c in range(4):
                columns(w_in, 4 * D + 256 * c)
            for c in range(4):
                columns(w_in, D + 256 * c)
            for c in range(4):
                columns(w_in, 256 * c)
            for c in range(4):
                columns(a["w_gate"][0], 256 * c)
                columns(a["w_gate"][0], D + 256 * c)
                columns(a["w_up_a"][0], 256 * c)
                columns(a["w_up_b"][0], 256 * c)
            for c in range(4):
                columns(a["w_out"][0], 256 * c)
            w1 = a["w1"][0].rearrange("e (k p) n -> p e k n", p=P)
            w3 = a["w3"][0].rearrange("e (k p) n -> p e k n", p=P)
            w2 = a["w2"][0].rearrange("e (k p) n -> p e k n", p=P)
            with t.loop(N_EXPERTS // 4, ring_counts(t.pos, 12, "fill")) as i:
                for which, e in MOE_ORDER:
                    if which == "w2":
                        chunk(w2[:, i * 4 + e, 0:1, :], w2[:, i * 4 + e, 1:2, :], (1024, 1024))
                    else:
                        v = w1 if which == "w1" else w3
                        chunk(v[:, i * 4 + e, 0:4, :], v[:, i * 4 + e, 4:8, :], (1024, 1024))
            for l in range(LAYERS):
                ffn(l, "ffn1_w_gu_2", "ffn1_w_down_2")
                for c in range(5):
                    columns(a["w_in_2"][l], 256 * c)
                for c in range(4):
                    columns(a["w_out_2"][l], 256 * c)
                ffn(l, "ffn2_w_gu_2", "ffn2_w_down_2")
            sp.wait_ge(E["outb_ready"], 4)
            sp.dma_start(out[0].rearrange("(b p) d -> p b d", p=P), OUTB[:]).then_inc(E["out_stored"], 16)
            sp.wait_ge(E["out_stored"], 16)

        @block.gpsimd
        def _(pool):
            rows = [("norm1_g", N1, 8), ("norm2_g", N2, 8), ("b_gate", BG, 16), ("v_norm_g", VG, 8), ("c_2", CV, 8),
                    ("c_ctx_2", CV + 8, 8), ("pool_scale_2", PS, 4), ("final_gain_2", FG, 8), ("sub_norm_g", SN, 1)]
            n = 0

            def flat(x):
                while len(x.shape) > 1:
                    x = x.rearrange("a b c -> (a b) c") if len(x.shape) == 3 else x.rearrange("a b -> (a b)")
                return x

            pool.dma_start(MATS[:], a["mats"]).then_inc(E["mats_loaded"], 16)
            for name, c0, k in rows:
                pool.dma_start(PA[c0:c0 + k, :], flat(a[name]).rearrange("(r p) -> r p", p=P))\
                    .then_inc(E["rows_loaded"], 16)
                n += 1
            for name, l, c0 in (("q_norm_g", 0, QN), ("k_norm_g", 0, KN), ("q_gain_2", 0, QG2), ("q_gain_2", 1, QG2 + 1),
                                ("k_gain_2", 0, KG2), ("k_gain_2", 1, KG2 + 1)):
                for half in range(2):
                    pool.dma_start(PA[c0:c0 + 1, half * HD:(half + 1) * HD], a[name][l:l + 1, :])\
                        .then_inc(E["rows_loaded"], 16)
                    n += 1
            pool.dma_start(PB[:], a["ada_b_2"].rearrange("l (r p) -> r l p", p=P)).then_inc(E["rows_loaded"], 16)
            n += 1
            dma_total["rows"] = 16 * n
            for i, name in enumerate(("lambda_q1", "lambda_k1", "lambda_q2", "lambda_k2")):
                pool.dma_start(LV[:, i, :], a[name][0].partition_broadcast(P)).then_inc(E["misc_loaded"], 16)
            pool.dma_start(ND[:], a["neg_dist"]).then_inc(E["misc_loaded"], 16)
            pool.dma_start(BSB[:].rearrange("p g t -> p (g t)"), flat(a["b_s"]).partition_broadcast(P))\
                .then_inc(E["misc_loaded"], 16)
            pool.dma_start(BR[:, 0:N_GROUPS], a["b_rg"][0].partition_broadcast(P)).then_inc(E["misc_loaded"], 16)
            pool.dma_start(BR[:, N_GROUPS:], a["b_re"][0].partition_broadcast(P)).then_inc(E["misc_loaded"], 16)
            pool.dma_start(WR[:, :, 0:N_GROUPS], a["w_rg"][0].rearrange("(k p) n -> p k n", p=P))\
                .then_inc(E["misc_loaded"], 16)
            pool.dma_start(WR[:, :, N_GROUPS:], a["w_re"][0].rearrange("(k p) n -> p k n", p=P))\
                .then_inc(E["misc_loaded"], 16)
            pool.dma_start(DESC[:], a["descending"].partition_broadcast(P)).then_inc(E["misc_loaded"], 16)
            dma_total["misc"] = 16 * 11
            pool.wait_ge(E["ws_loaded"], 16)
            nc.gpsimd.affine_select(out=WS[:], in_=WS[:], compare_op=ALU.is_ge, fill=0.0, base=0,
                                    pattern=[[0, KT], [-1, P]], channel_multiplier=1).then_inc(E["ws_masked"], 1)
            pool.wait_ge(E["combT_ready"], 1)
            pool.dma_start(comb_rows, CT[:]).then_inc(E["comb_stored"], 16)
            pool.wait_ge(E["comb_stored"], 16)
            pool.dma_start(CB[:].rearrange("p e t -> p (e t)"),
                           comb_rows.rearrange("e t -> (e t)").partition_broadcast(P)).then_inc(E["comb_loaded"], 16)
            pool.dma_start(POOL[:], a["pool_mix"]).then_inc(E["mix_consts_loaded"], 16)
            pool.dma_start(DFT[:], a["dft"]).then_inc(E["mix_consts_loaded"], 16)
            pool.dma_start(TRIG[:], a["trig"]).then_inc(E["mix_consts_loaded"], 16)
            pool.dma_start(FW[:], a["fft_w_2"].rearrange("l (t p) n -> p l t n", p=P))\
                .then_inc(E["mix_consts_loaded"], 16)
            nc.gpsimd.memset(PWB[:], 0.0).then_inc(E["pwb_zero"], 1)
            pool.wait_ge(E["pwb_zero"], 1)
            for l in range(LAYERS):
                for g in range(4):
                    p0 = HD * (g % 2)
                    pool.dma_start(PWB[p0:p0 + HD, l, g // 2, p0:p0 + HD], a["pool_w_2"][l, g])\
                        .then_inc(E["mix_consts_loaded"], 16)
            dma_total["mix"] = 16 * (4 + 4 * LAYERS)

        @block.vector
        def _(ve):
            t = Tally(ve)
            V = nc.vector

            def link(ins):
                ins.then_inc(E["vec_step"], 1)
                ve.wait_ge(E["vec_step"], t.next("vec_step"))

            def got(name):
                ve.wait_ge(E[name], t.next(name))

            def products():
                s, n = t.use()
                ve.wait_ge(slot_used[s], n)

            def prep(words=CHUNK):
                s = t.take()
                ve.wait_ge(hi_done[s], t.next(f"split{s}"))
                V.tensor_tensor(LO[s][:, :words], RAW[s][:, :words], HI[s % HI_SLOTS][:, :words].bitcast(F32),
                                ALU.subtract).then_inc(lo_done[s], 1)

            def split(hi, lo, x, done):
                link(V.tensor_copy(hi, x))
                V.tensor_tensor(lo, x, hi.bitcast(F32), ALU.subtract).then_inc(E[done], 1)

            def rstd(mean, r):
                V.tensor_scalar(r, mean, EPS, None, ALU.add).then_inc(E["var_ready"], 1)
                got("std_ready")
                link(V.reciprocal(r, r))

            V.memset(ZERO[:, 0:256], 0.0).then_inc(E["gated"], START["gated"])
            V.memset(ZERO[:, 256:512], 0.0).then_inc(E["mod_read"], START["mod_read"])
            got("params_done")
            V.tensor_copy(PT[:], B[0][:, 0:N_COLS])
            for l in range(LAYERS):
                ins = V.tensor_copy(ADB[:, l, :], B[0][:, P + l * P:P + l * P + MODT])
            link(ins)
            V.tensor_scalar(GQ[:, 0:1], PT[:, QN:QN + 1], HD ** -0.5, None, ALU.mult)
            V.tensor_scalar(GQ[:, 1:2], PT[:, SN:SN + 1], 1.0 - LAM_INIT, None, ALU.mult).then_inc(E["params_ready"], 1)
            ve.wait_ge(E["misc_loaded"], dma_total["misc"])
            lv = LV[:].rearrange("p (a b) d -> p a b d", b=2)
            prod = T[1][:, 0:2 * HD].rearrange("p (a d) -> p a d", a=2)
            link(V.tensor_tensor(prod, lv[:, :, 0, :], lv[:, :, 1, :], ALU.mult))
            V.tensor_reduce(SM[:, 0:2], prod, AX, ALU.add).then_inc(E["lam_sums"], 1)
            got("lam_exps")
            link(V.tensor_tensor(SM[:, 4:5], SM[:, 3:4], SM[:, 2:3], ALU.subtract))
            link(V.tensor_scalar(SM[:, 5:6], SM[:, 4:5], -LAM_INIT, None, ALU.add))
            neg_lam = SM[:, 5:6]

            for l in range(LAYERS):
                mod = MOD[:, l].rearrange("p (i m) v -> p i m v", m=8)
                bias = ADB[:, l].rearrange("p (i m) -> p i m", m=8)
                with t.loop(MODT // 8, {**ring_counts(t.used, 4, "used"), "mod_read": 0}) as i:
                    for _ in range(3):
                        t.use()
                    products()
                    V.tensor_tensor(mod[:, i, :, :], B[3][:, 0:16].rearrange("p (m v) -> p m v", v=2),
                                    bc(bias[:, i, :], 2, [P, 8, 2]), ALU.add).then_inc(E["mod_read"], 1)
                ve.wait_ge(E["mod_read"], START["mod_read"] + MODT // 8 * (l + 1))
                for k in (1, 4, 7):
                    m = MOD[:, l, k * KT:(k + 1) * KT, :]
                    ins = V.tensor_scalar(m, m, 1.0, None, ALU.add)
                for k in (2, 8):
                    m = MOD[:, l, k * KT:(k + 1) * KT, :]
                    ins = V.tensor_scalar(m, m, 0.5, None, ALU.mult)
                link(ins)
            prep()

            def norm_first(hf, gain):
                got("stats_done")
                rstd(B[0][:, 0:S], R[0][:, :S])
                for k in range(KT):
                    link(V.scalar_tensor_tensor(hf[:, k, :], XC[:, k, 0:S], PT[:, gain + k:gain + k + 1], R[0][:, :S],
                                                ALU.mult, ALU.mult))
                    split(hH[:, k, 0:S], hL[:, k, 0:S], hf[:, k, :], "h_ready")

            norm_first(HF1, N1)

            for c in range(12):
                prep()
                products_c = t.use()
                if 1 <= c <= 8:
                    got("stats_done")
                    r = R[(c - 1) % 2][:]
                    rstd(B[2 + (c - 1) % 2][:], r)
                    gain = GQ[:, 0:1] if c - 1 < 4 else PT[:, KN:KN + 1]
                    V.scalar_tensor_tensor(pair(QK, c - 1), pair(QK, c - 1), gain, r, ALU.mult, ALU.mult)\
                        .then_inc(E["qk_ready"], 1)

            SC = [T[0][:, 0:2 * P].rearrange("p (c n) -> p c n", c=2), T[1][:].rearrange("p (c n) -> p c n", c=2)]
            ss = SM[:, 8:24].rearrange("p (b g) -> p b g", b=TB)
            for h in range(HEADS):
                for i in range(TB):
                    nk = P * (i + 1)
                    mx, nm = SM[:, 24 + 4 * i:26 + 4 * i], SM[:, 26 + 4 * i:28 + 4 * i]
                    got("scores_done")
                    for c in range(2):
                        V.scalar_tensor_tensor(SC[i][:, c, :], ND[:, i, 0:nk], 2.0 ** -(h + 1), B[6 * i + c][:, 0:nk],
                                               ALU.mult, ALU.add).then_inc(E["sc_read"], 1)
                        t.next("sc_read")
                    ve.wait_ge(E["sc_read"], t.at("sc_read"))
                    link(V.tensor_reduce(mx, SC[i], AX, ALU.max))
                    V.tensor_scalar(nm, mx, -1.0, None, ALU.mult).then_inc(E["max_ready"], 1)
                prep()
                for i in range(TB):
                    rs, ri = SM2[:, 4 * i:4 * i + 2], SM2[:, 4 * i + 2:4 * i + 4]
                    got("exp_ready")
                    link(V.reciprocal(ri, rs))
                    link(V.tensor_tensor(ri[:, 1:2], ri[:, 1:2], neg_lam, ALU.mult))
                    link(V.tensor_scalar(SC[i][:, 0, :], SC[i][:, 0, :], ri[:, 0:1], None, ALU.mult))
                    V.scalar_tensor_tensor(SC[i][:, 0, :], SC[i][:, 1, :], ri[:, 1:2], SC[i][:, 0, :],
                                           ALU.mult, ALU.add).then_inc(E["prob_ready"], 1)
                if h < 4:
                    t.use()
                    got("va_copied")
                    va = VA[:, :, 256 * h:256 * (h + 1)]
                    sq = T[2][:].rearrange("p (b n) -> p b n", b=TB)
                    link(V.tensor_tensor(sq, va, va, ALU.mult))
                    for b in range(TB):
                        ins = V.tensor_reduce(ss[:, b, 2 * h:2 * h + 2],
                                              sq[:, b, :].rearrange("p (g n) -> p g n", g=2), AX, ALU.add)
                    if h < 3:
                        link(ins)
                    else:
                        link(ins)
                        link(V.tensor_scalar(SM[:, 8:24], SM[:, 8:24], 1.0 / P, EPS, ALU.mult, ALU.add))
                        V.tensor_copy(R[0][:, 0:16], SM[:, 8:24]).then_inc(E["var_ready"], 1)
                        got("std_ready")
                        link(V.reciprocal(R[0][:, 0:16], R[0][:, 0:16]))
                        for b in range(TB):
                            v = VA[:, b, :].rearrange("p (g n) -> p g n", g=KT)
                            ins = V.tensor_tensor(v, v, bc(R[0][:, KT * b:KT * b + KT], 2, [P, KT, P]), ALU.mult)
                        ins.then_inc(E["va_ready"], 1)
                        for g in range(KT):
                            if g % 2 == 0:
                                got("z_done")
                            ins = V.scalar_tensor_tensor(
                                ZB[:, g, :].rearrange("p (b n) -> p b n", b=TB),
                                bank2(6 + g // 2 % 2)[:, g % 2, :].rearrange("p (b n) -> p b n", b=TB),
                                PT[:, VG + g:VG + g + 1], bc(BSB[:, g, :], 1, [P, TB, P]), ALU.mult, ALU.add)
                            if g % 2:
                                ins.then_inc(E["zb_ready"], 1)
                        ve.wait_ge(E["zb_ready"], KT // 2)
                else:
                    j = h - 4
                    products()
                    V.tensor_tensor(T[2][:], B[4 + h % 2][:], pair(ZB, j), ALU.mult).then_inc(E["ya_ready"], 1)
                    ve.wait_ge(E["ya_ready"], 2 * j + 1)
                    split(pair(YAH, j), pair(YAL, j), T[2][:], "ya_ready")

            for j in range(4):
                got("stats_done")
                rstd(B[4 + j][:], R[j % 2][:])
                link(V.scalar_tensor_tensor(T[2 + j % 2][:], pair(QK, j), GQ[:, 1:2], R[j % 2][:], ALU.mult, ALU.mult))
                split(pair(YBH, j), pair(YBL, j), T[2 + j % 2][:], "yb_ready")

            for j in range(4):
                b = 4 * (j % 2)
                for _ in range(2):
                    prep()
                    t.use()
                gates = [T[2 * (j % 2)], T[2 * (j % 2) + 1]]
                for n in range(2):
                    prep()
                    products()
                    got("gate_ready")
                    V.tensor_tensor(T[4 + n][:], B[b + 2 + n][:], gates[n][:], ALU.mult).then_inc(E["up_read"], 1)
                ve.wait_ge(E["up_read"], 2 * (j + 1))
                link(V.tensor_tensor(T[4][:], T[4][:], T[5][:], ALU.add))
                split(pair(MH, j), pair(ML, j), T[4][:], "merged_ready")

            for j in range(4):
                prep()
                products()
                x = XC[:, 2 * j:2 * j + 2, 0:S]
                V.tensor_tensor(x, x, bank2(j), ALU.add).then_inc(E["x_ready"], 1)

            norm_first(HF2, N2)
            got("logits_done")
            NR = N_GROUPS + N_EXPERTS

            def rt(i, *dims):
                n = 1
                for d in dims:
                    n *= d
                x = RT[:, i, 0:TB * n].rearrange("p (b n) -> p b n", b=TB)
                return x.rearrange("p b (g j) -> p b g j", g=dims[0]) if len(dims) == 2 else x

            def last(x, n):
                return x.to_broadcast([P, TB, n])

            logits = rt(0, NR)
            V.tensor_tensor(logits, B[1][:, 0:TB * NR].rearrange("p (b n) -> p b n", b=TB), bc(BR[:], 1, [P, TB, NR]),
                            ALU.add).then_inc(E["logits_read"], 1)
            ve.wait_ge(E["logits_read"], 1)
            gl = logits[:, :, 0:N_GROUPS]
            el = logits[:, :, N_GROUPS:].rearrange("p b (g j) -> p b g j", g=N_GROUPS)
            m, s4, gate, kmax = (SM2[:, 8 + 2 * i:10 + 2 * i].unsqueeze(2) for i in range(4))

            def first_max(x, is_max, n, desc, key):
                link(V.tensor_tensor(key, is_max, bc(desc, 1, [P, TB, n]), ALU.mult))
                link(V.tensor_reduce(kmax, key, AX, ALU.max))
                link(V.tensor_tensor(x, key, last(kmax, n), ALU.is_equal))

            d4, e4, oh4, key4 = rt(1, 4), rt(2, 4), rt(3, 4), rt(4, 4)
            link(V.tensor_reduce(m, gl, AX, ALU.max))
            V.tensor_tensor(d4, gl, last(m, 4), ALU.subtract).then_inc(E["top_ready"], 1)
            ve.wait_ge(E["top_ready"], 1)
            link(V.tensor_scalar(key4, d4, 0.0, None, ALU.is_ge))
            first_max(oh4, key4, 4, DESC[:, 0:N_GROUPS], key4)
            got("exp4_ready")
            link(V.tensor_reduce(s4, e4, AX, ALU.add))
            link(V.reciprocal(gate, s4))
            sel, e8 = rt(5, 4, 8), rt(6, 8)
            link(V.tensor_tensor(sel, el, oh4.unsqueeze(3).to_broadcast([P, TB, 4, 8]), ALU.mult))
            link(V.tensor_reduce(e8, sel.rearrange("p b g j -> p b j g"), AX, ALU.add))
            d8, key8, oh1, oh2, rest = rt(7, 8), rt(8, 8), rt(9, 8), rt(10, 8), rt(11, 8)
            link(V.tensor_reduce(m, e8, AX, ALU.max))
            link(V.tensor_tensor(d8, e8, last(m, 8), ALU.subtract))
            link(V.tensor_scalar(key8, d8, 0.0, None, ALU.is_ge))
            first_max(oh1, key8, 8, DESC[:, N_GROUPS:], key8)
            link(V.scalar_tensor_tensor(rest, oh1, -BIG, d8, ALU.mult, ALU.add))
            V.tensor_reduce(m, rest, AX, ALU.max).then_inc(E["m2_ready"], 1)
            ve.wait_ge(E["m2_ready"], 1)
            link(V.tensor_tensor(key8, rest, last(m, 8), ALU.is_equal))
            first_max(oh2, key8, 8, DESC[:, N_GROUPS:], key8)
            e2, w1_, w2_ = (SM2[:, 16 + 2 * i:18 + 2 * i].unsqueeze(2) for i in range(3))
            got("exp2_ready")
            link(V.tensor_scalar(s4, e2, 1.0, None, ALU.add))
            link(V.reciprocal(s4, s4))
            link(V.tensor_tensor(w1_, s4, gate, ALU.mult))
            link(V.tensor_tensor(w2_, w1_, e2, ALU.mult))
            link(V.tensor_tensor(oh1, oh1, last(w1_, 8), ALU.mult))
            link(V.tensor_tensor(oh2, oh2, last(w2_, 8), ALU.mult))
            link(V.tensor_tensor(oh1, oh1, oh2, ALU.add))
            for b in range(TB):
                ins = V.tensor_tensor(sel[:, b], bc(oh1[:, b, :], 1, [P, 4, 8]), bc(oh4[:, b, :], 2, [P, 4, 8]), ALU.mult)
            ins.then_inc(E["comb_ready"], 1)
            got("combT_done")
            V.tensor_copy(CT[:], B[2][0:N_EXPERTS, 0:S]).then_inc(E["combT_ready"], 1)

            ve.wait_ge(E["comb_loaded"], 16)
            cb = CB[:].rearrange("p (i e) n -> p i e n", e=4)
            with t.loop(N_EXPERTS // 4, {**ring_counts(t.used, 12, "used", "fill", "split"), "silu_ready": 4, "gated": 4,
                                         "vec_step": 8}) as i:
                for which, e in MOE_ORDER:
                    prep()
                    if which != "w3":
                        t.use()
                        continue
                    products()
                    got("silu_ready")
                    V.tensor_tensor(T[2 + e % 2][:], B[2 * (e % 2) + 1][:], T[e % 2][:], ALU.mult).then_inc(E["gated"], 1)
                    got("gated")
                    x = T[2 + e % 2][:].rearrange("p (f n) -> p f n", f=2)
                    for f in range(2):
                        ins = V.tensor_tensor(x[:, f, :], x[:, f, :], cb[:, i, e, :], ALU.mult)
                    link(ins)
                    split(HIDH[e % 2][:], HIDL[e % 2][:], x, "hid_ready")
            got("acc_done")
            for j in range(4):
                x = XC[:, 2 * j:2 * j + 2, 0:S]
                V.tensor_tensor(x, x, bank2(4 + j), ALU.add).then_inc(E["x_ready"], 1)

            def norm(n):
                got("stats_done")
                rstd(B[0][:, 0:n], R[0][:, :n])
                for k in range(KT + 1):
                    if k < KT:
                        V.tensor_tensor(HF[:, k, :n], XC[:, k, :n], R[0][:, :n], ALU.mult).then_inc(E["xn_ready"], 1)
                    if k >= 1:
                        got("hf_ready")
                        split(hH[:, k - 1, :n], hL[:, k - 1, :n], HF[:, k - 1, :n], "h_ready")

            def residual(l, gate, m, b, n):
                for v in range(n // S):
                    x = XC[:, m, v * S:(v + 1) * S]
                    ins = V.scalar_tensor_tensor(x, B[b][:, v * S:(v + 1) * S], MOD[:, l, gate * KT + m, v:v + 1], x,
                                                 ALU.mult, ALU.add)
                ins.then_inc(E["x_ready"], 1)

            def ffn(l, gate, n, lead):
                counts = {**ring_counts(t.used, FT_HALF + KT, "used", "fill", "split"), "silu_ready": FT_HALF,
                          "gated": FT_HALF, "vec_step": FT_HALF}
                with t.loop(2, counts):
                    if not lead:
                        prep()
                    for j in range(FT_HALF):
                        prep(CHUNK if j + 1 < FT_HALF else FT_HALF * P)
                        products()
                        got("silu_ready")
                        V.tensor_tensor(T[2 + j % 2][:, :n], B[2 * (j % 2) + 1][:, :n], T[j % 2][:, :n], ALU.mult)\
                            .then_inc(E["gated"], 1)
                        got("gated")
                        split(aH[:, j, :n], aL[:, j, :n], T[2 + j % 2][:, :n], "hid_ready")
                    for m in range(KT):
                        if m + 1 < KT:
                            prep(FT_HALF * P)
                        else:
                            t.pos += 1
                            if lead:
                                prep()
                        products()
                        residual(l, gate, m, 4 + m % 4, n)
                    t.used += 1

            def mix_split(x, m, p0, np_, c0, n):
                got("mix_hi")
                V.tensor_tensor(XL[p0:p0 + np_, m, c0:c0 + n], x, XH[p0:p0 + np_, m, c0:c0 + n].bitcast(F32),
                                ALU.subtract).then_inc(E["mix_ready"], 1)

            def mixers(l):
                n = 2 * S if l + 1 < LAYERS else S
                for c in range(5):
                    prep()
                    t.use()
                if l == 0:
                    ve.wait_ge(E["mix_consts_loaded"], dma_total["mix"])
                for i in range(6):
                    if i < 5:
                        got("stats_done")
                        w = n if i < 4 else 2 * S
                        rstd(B[2 + i % 2][:, :w], R[i % 2][:, :w])
                        gain = PT[:, QG2 + l:QG2 + l + 1] if i < 4 else PT[:, KG2 + l:KG2 + l + 1]
                        V.scalar_tensor_tensor(QQ[:, i, :w], QQ[:, i, :w], gain, R[i % 2][:, :w], ALU.mult, ALU.mult)\
                            .then_inc(E["qn_ready"], 1)
                        t.next("qn_ready")
                    if i >= 1:
                        x = QQ[:, i - 1, 0:S]
                        got("rot_done")
                        c, s = T[2 * (i % 2)][:, :S], T[2 * (i % 2) + 1][:, :S]
                        V.tensor_tensor(c, x, TRIG[:, 0, :], ALU.mult)
                        link(V.tensor_tensor(s, B[4 + (i - 1) % 2][:, :S], TRIG[:, 1, :], ALU.mult))
                        V.tensor_tensor(x, c, s, ALU.add).then_inc(E["q_ready"], 1)
                for p in range(2):
                    got("mix_hi")
                    V.scalar_tensor_tensor(XL[:, 4 + p, :n], B[7][:, :n], PT[:, PS + 2 * l + p:PS + 2 * l + p + 1],
                                           XH[:, 4 + p, :n].bitcast(F32), ALU.mult, ALU.subtract)\
                        .then_inc(E["mix_ready"], 1)
                for d in range(2):
                    mix_split(B[6 + d][:, :n], 6 + d, 0, P, 0, n)
                units = attention_units(l)
                for u in range(len(units) + 2):
                    if u < len(units):
                        h, q0, k0, nk = units[u]
                        got("scores_done")
                        mx, nm = SM[:, 8 + u % 2:9 + u % 2], SM[:, 10 + u % 2:11 + u % 2]
                        link(V.tensor_reduce(mx, B[u % 2][:, :nk], AX, ALU.max))
                        V.tensor_scalar(nm, mx, -(HD ** -0.5), None, ALU.mult).then_inc(E["max_ready"], 1)
                    if 1 <= u <= len(units):
                        h, q0, k0, nk = units[u - 1]
                        rs, ri = SM2[:, (u - 1) % 2:(u - 1) % 2 + 1], SM2[:, 2 + (u - 1) % 2:3 + (u - 1) % 2]
                        got("exp_ready")
                        link(V.reciprocal(ri, rs))
                        e = T[(u - 1) % 2][:, :nk]
                        V.tensor_scalar(e, e, ri, None, ALU.mult).then_inc(E["prob_ready"], 1)
                    if u >= 2:
                        h, q0, k0, nk = units[u - 2]
                        p0 = HD * (h % 2)
                        mix_split(B[4 + (u - 2) % 2][p0:p0 + HD, 0:P], h // 2, p0, HD, q0, P)
                for j in range(4):
                    if j < 3 or l + 1 < LAYERS:
                        prep()
                    products()
                    for m in (2 * j, 2 * j + 1):
                        residual(l, 5, m, m, n)

            for l in range(LAYERS):
                n = 2 * S if l + 1 < LAYERS else S
                norm(2 * S)
                ffn(l, 2, 2 * S, True)
                norm(2 * S)
                mixers(l)
                norm(n)
                ffn(l, 8, n, l + 1 < LAYERS)

            got("stats_done")
            rstd(B[0][:, 0:S], R[0][:, :S])
            for k in range(KT):
                ins = V.scalar_tensor_tensor(HF[:, k, :S], XC[:, k, :S], PT[:, FG + k:FG + k + 1], R[0][:, :S],
                                             ALU.mult, ALU.mult)
                ins.then_inc(E["hf_done"], 1)

        @block.scalar
        def _(act):
            t = Tally(act)
            A = nc.scalar

            def got(name):
                act.wait_ge(E[name], t.next(name))

            def products():
                s, n = t.use()
                act.wait_ge(slot_used[s], n)

            def prep(words=CHUNK):
                s = t.take()
                before = (s + HI_SLOTS) % RAW_SLOTS
                act.wait_ge(raw_loaded[s], t.at(f"fill{s}") * 32)
                if t.n[f"fill{before}"]:
                    act.wait_ge(slot_used[before], t.at(f"fill{before}"))
                A.activation(HI[s % HI_SLOTS][:, :words], RAW[s][:, :words], ACT.Copy).then_inc(hi_done[s], 1)

            def root(r):
                got("var_ready")
                A.activation(r, r, ACT.Sqrt).then_inc(E["std_ready"], 1)

            def squares(n, fresh):
                for k in range(KT):
                    fresh(k)
                    if k >= 2:
                        got("sq_used")
                    A.activation(SQ[k % 2][:, :n], XC[:, k, :n], ACT.Square).then_inc(E["sq_ready"], 1)
                root(R[0][:, :n])

            for j in range(8):
                got("x_done")
                v, c = j // 4, j % 4
                A.activation(XC[:, 2 * c:2 * c + 2, v * S:(v + 1) * S], bank2((j + 1) % 8), ACT.Copy)\
                    .then_inc(E["x_copied"], 1)
            got("params_ready")
            for v, done in enumerate(("silu_ready", "cs_ready")):
                A.activation(CS[:, :, v], PT[:, CV + v * KT:CV + (v + 1) * KT], ACT.Silu).then_inc(E[done], 1)
            for i in range(2):
                got("ws_done")
                A.activation(WST[:, 4 * i:4 * i + 4, :].rearrange("p g t -> p (g t)"), B[1 + i][:], ACT.Copy)\
                    .then_inc(E["wst_ready"], 1)
            got("lam_sums")
            A.activation(SM[:, 2:4], SM[:, 0:2], ACT.Exp).then_inc(E["lam_exps"], 1)

            for s in range(RAW_SLOTS):
                for kind in ("fill", "used"):
                    t.n[f"{kind}{s}"] += LAYERS * MODT // 2 // RAW_SLOTS
            prep()

            def from_start(k):
                act.wait_ge(E["x_copied"], 8)
            squares(S, from_start)
            for c in range(12):
                prep()
                products()
                if c < 8:
                    A.activation(pair(QK, c), B[4 + c % 2][:], ACT.Copy)
                    A.activation(SQ[c % 2][:], B[4 + c % 2][:], ACT.Square).then_inc(E["sq_ready"], 1)
                else:
                    A.activation(VB[:, :, 256 * (c - 8):256 * (c - 7)], bank2(4 + c % 2), ACT.Copy).then_inc(E["vb_ready"], 1)
                if 1 <= c <= 8:
                    root(R[(c - 1) % 2][:])

            SC = [T[0][:, 0:2 * P].rearrange("p (c n) -> p c n", c=2), T[1][:].rearrange("p (c n) -> p c n", c=2)]

            def head_out(h):
                got("pv_done")
                A.activation(QK[:, h, :], B[3][:, 0:S], ACT.Copy).then_inc(E["o_ready"], 1)

            for h in range(HEADS):
                if h >= 1:
                    head_out(h - 1)
                for i in range(TB):
                    got("max_ready")
                    for c in range(2):
                        ins = A.activation(SC[i][:, c, :], SC[i][:, c, :], ACT.Exp, bias=SM[:, 26 + 4 * i + c:27 + 4 * i + c],
                                           accum_out=SM2[:, 4 * i + c:4 * i + c + 1])
                    ins.then_inc(E["exp_ready"], 1)
                prep()
                if h < 4:
                    products()
                    A.activation(VA[:, :, 256 * h:256 * (h + 1)], bank2(4 + h % 2), ACT.Copy).then_inc(E["va_copied"], 1)
                    if h == 3:
                        root(R[0][:, 0:16])
                else:
                    t.use()
                got("probT_done")
                A.activation(T[3][:, 0:3 * P], B[2][:, 0:3 * P], ACT.Copy).then_inc(E["probT_ready"], 1)
            head_out(HEADS - 1)
            act.wait_ge(E["o_ready"], HEADS)
            for j in range(4):
                A.activation(SQ[j % 2][:], pair(QK, j), ACT.Square).then_inc(E["sq_ready"], 1)
                if j >= 1:
                    root(R[(j - 1) % 2][:])
            root(R[1][:])

            for j in range(4):
                if j == 1:
                    act.wait_ge(E["yb_ready"], 4)
                if j >= 2:
                    act.wait_ge(E["up_read"], 2 * (j - 1))
                for n in range(2):
                    prep()
                    products()
                    for m in range(2):
                        col = BG + KT * n + 2 * j + m
                        ins = A.activation(T[2 * (j % 2) + n][:, m * S:(m + 1) * S], bank2(4 * (j % 2) + n)[:, m, :],
                                           ACT.Sigmoid, bias=PT[:, col:col + 1])
                    ins.then_inc(E["gate_ready"], 1)
                for n in range(2):
                    prep()
                    t.use()
            for j in range(4):
                prep()
                t.use()

            def by_pair(k):
                if k % 2 == 0:
                    got("x_ready")

            def by_tile(k):
                got("x_ready")
            squares(S, by_pair)

            def rt(i, n):
                return RT[:, i, 0:TB * n]
            got("top_ready")
            A.activation(rt(2, 4), rt(1, 4), ACT.Exp).then_inc(E["exp4_ready"], 1)
            got("m2_ready")
            A.activation(SM2[:, 16:18], SM2[:, 8:10], ACT.Exp).then_inc(E["exp2_ready"], 1)

            with t.loop(N_EXPERTS // 4, {**ring_counts(t.used, 12, "used", "fill"), "silu_ready": 0, "gated": 4}) as i:
                for which, e in MOE_ORDER:
                    prep()
                    if which != "w1":
                        t.use()
                        if which == "w3":
                            t.next("gated")
                        continue
                    products()
                    if e >= 2:
                        act.wait_ge(E["gated"], t.at("gated", 1))
                    else:
                        act.wait_ge(E["gated"], t.at("gated", e))
                    A.activation(T[e % 2][:], B[2 * (e % 2)][:], ACT.Silu).then_inc(E["silu_ready"], 1)

            def norm(l, shift, scale, n, fresh):
                squares(n, fresh)
                for k in range(KT):
                    got("xn_ready")
                    for v in range(n // S):
                        h = HF[:, k, v * S:(v + 1) * S]
                        ins = A.activation(h, h, ACT.Identity, bias=MOD[:, l, shift * KT + k, v:v + 1],
                                           scale=MOD[:, l, scale * KT + k, v:v + 1])
                    ins.then_inc(E["hf_ready"], 1)

            def ffn(n, lead):
                counts = {**ring_counts(t.used, FT_HALF + KT, "used", "fill"), "gated": FT_HALF, "gate_done": FT_HALF}
                with t.loop(2, counts):
                    if not lead:
                        prep()
                    for j in range(FT_HALF):
                        prep(CHUNK if j + 1 < FT_HALF else FT_HALF * P)
                        got("gate_done")
                        act.wait_ge(E["gated"], t.at("gated", min(j, 1)))
                        A.activation(T[j % 2][:, :n], B[2 * (j % 2)][:, :n], ACT.Silu).then_inc(E["silu_ready"], 1)
                        t.next("gated")
                        t.use()
                    for m in range(KT):
                        if m + 1 < KT:
                            prep(FT_HALF * P)
                        else:
                            t.pos += 1
                            if lead:
                                prep()
                        t.use()
                    t.used += 1
                t.n["x_ready"] += KT

            def mix_high(x, m, p0, np_, c0, n, **scale):
                A.activation(XH[p0:p0 + np_, m, c0:c0 + n], x, ACT.Copy, **scale).then_inc(E["mix_hi"], 1)

            def mixers(l):
                n = 2 * S if l + 1 < LAYERS else S
                sets = n // S
                for c in range(5):
                    prep()
                    products()
                    if c < 2:
                        for i in (2 * c, 2 * c + 1):
                            A.activation(QQ[:, i, :n], B[i][:, :n], ACT.Copy).then_inc(E["q_copied"], 1)
                    elif c == 2:
                        A.activation(QQ[:, 4, :], B[4][:], ACT.Copy).then_inc(E["q_copied"], 1)
                        for kv in range(2):
                            src = B[5][:].rearrange("p (b n) -> p b n", b=4)[:, :, kv * HD:(kv + 1) * HD]
                            ins = A.activation(VD[:, :, kv], bc(src, 2, [P, 4, 2, HD]), ACT.Copy)
                        ins.then_inc(E["v_ready"], 1)
                    else:
                        for s in range(sets):
                            ins = A.activation(PF[:, 2 * s:2 * s + 2, c - 3, :], bank2([6, 0][c - 3] + s), ACT.Copy)
                            ins.then_inc(E["pf_ready"], 1)
                act.wait_ge(E["q_copied"], 5 * (l + 1))
                for i in range(6):
                    if i < 5:
                        w = n if i < 4 else 2 * S
                        A.activation(SQ[i % 2][:, :w], QQ[:, i, :w], ACT.Square).then_inc(E["sq_ready"], 1)
                    if i >= 1:
                        w = n if i < 5 else 2 * S
                        root(R[(i - 1) % 2][:, :w])
                for kv in range(2):
                    got("dup_done")
                    A.activation(KD[:, kv, :], B[6 + kv][:], ACT.Copy).then_inc(E["kd_ready"], 1)
                for p in range(2):
                    for s in range(sets):
                        got("pool_done")
                        for g in range(2):
                            rows = slice(HD * g, HD * (g + 1))
                            ins = A.activation(T[4][rows, s * S:(s + 1) * S], bank2(6)[rows, g, :], ACT.Copy)
                        ins.then_inc(E["pm_ready"], 1)
                    got("pwb_done")
                    col = PS + 2 * l + p
                    mix_high(B[7][:, :n], 4 + p, 0, P, 0, n, scale=PT[:, col:col + 1])
                for p in range(2):
                    for s in range(sets):
                        got("fftab_done")
                        A.activation(AB[:], B[6][:], ACT.Copy).then_inc(E["ab_ready"], 1)
                        got("fft_done")
                        A.activation(T[2 + p][:, s * S:(s + 1) * S], B[7][:, :S], ACT.Copy).then_inc(E["ft_ready"], 1)
                for d in range(2):
                    got("yf_done")
                    mix_high(B[6 + d][:, :n], 6 + d, 0, P, 0, n)
                units = attention_units(l)
                for u in range(len(units) + 2):
                    if u < len(units):
                        h, q0, k0, nk = units[u]
                        got("max_ready")
                        A.activation(T[u % 2][:, :nk], B[u % 2][:, :nk], ACT.Exp, bias=SM[:, 10 + u % 2:11 + u % 2],
                                     scale=HD ** -0.5, accum_out=SM2[:, u % 2:u % 2 + 1]).then_inc(E["exp_ready"], 1)
                    if 1 <= u <= len(units):
                        h, q0, k0, nk = units[u - 1]
                        got("probT_done")
                        A.activation(T[2 + (u - 1) % 2][:, :nk], B[2 + (u - 1) % 2][:, :nk], ACT.Copy)\
                            .then_inc(E["probT_ready"], 1)
                    if u >= 2:
                        h, q0, k0, nk = units[u - 2]
                        p0 = HD * (h % 2)
                        got("pv_done")
                        mix_high(B[4 + (u - 2) % 2][p0:p0 + HD, 0:P], h // 2, p0, HD, q0, P)
                for j in range(4):
                    if j < 3 or l + 1 < LAYERS:
                        prep()
                    t.use()

            for l in range(LAYERS):
                n = 2 * S if l + 1 < LAYERS else S
                norm(l, 0, 1, 2 * S, by_pair if l == 0 else by_tile)
                ffn(2 * S, True)
                norm(l, 3, 4, 2 * S, by_tile)
                mixers(l)
                norm(l, 6, 7, n, by_tile)
                ffn(n, l + 1 < LAYERS)
            squares(S, by_tile)

            for j in range(4):
                got("fin_done")
                b, half = j // 2, j % 2
                A.activation(OUTB[:, b, 512 * half:512 * (half + 1)], B[1 + j][:], ACT.Copy).then_inc(E["outb_ready"], 1)

        @block.tensor
        def _(pe):
            t = Tally(pe)
            mm = nc.tensor.matmul
            release = {}
            turn_start = {}

            def got(name):
                pe.wait_ge(E[name], t.next(name))

            def claim(b, reader):
                if b in release:
                    name, n = release[b]
                    pe.wait_ge(E[name], n)
                elif t.turn is not None:
                    pe.wait_ge(E[reader], turn_start[reader])
                release[b] = (reader, t.next(reader))

            @contextmanager
            def turns(n, counts, events):
                for name, v in release.values():
                    pe.wait_ge(E[name], v)
                release.clear()
                with t.loop(n, counts) as i:
                    for e in events:
                        turn_start[e] = t.at(e)
                    yield i
                for b, (name, _) in release.items():
                    release[b] = (name, t.n[name])

            def chunk():
                s = t.take()
                pe.wait_ge(lo_done[s], t.next(f"split{s}"))
                return s

            def used(ins, s):
                ins.then_inc(slot_used[s], 1)

            def exact(o, wh, wl, xh, xl, first=True, last=True, **more):
                mm(o, wh, xh, start=first, stop=False, **more)
                mm(o, wh, xl, start=False, stop=False, **more)
                return mm(o, wl, xh, start=False, stop=last, **more)

            def slot(s, **dims):
                v = "p (k n) -> p k n"
                return HI[s % HI_SLOTS][:].rearrange(v, **dims), LO[s][:].rearrange(v, **dims)

            def features(s, col, o, xh, xl, n, wait=None):
                wh, wl = slot(s, k=KT)
                for k in range(KT):
                    if wait:
                        wait(k)
                    ins = exact(o, wh[:, k, col:col + P], wl[:, k, col:col + P], xh[:, k, :n], xl[:, k, :n],
                                k == 0, k == KT - 1)
                return ins

            def tokens(s, block, o, col=0, w=256):
                wh, wl = slot(s, k=KT)
                rows = slice(P * block, P * (block + 1))
                for k in range(KT):
                    ins = exact(o, hH[:, k, rows], hL[:, k, rows], wh[:, k, col:col + w], wl[:, k, col:col + w],
                                k == 0, k == KT - 1)
                return ins

            def mean_of_squares(n, b=0):
                claim(b, "var_ready")
                for k in range(KT):
                    got("sq_ready")
                    ins = mm(B[b][:, :n], mat(MEAN_D), SQ[k % 2][:, :n], start=(k == 0), stop=(k == KT - 1))
                    if k < KT - 2:
                        ins.then_inc(E["sq_used"], 1)
                ins.then_inc(E["stats_done"], 1)

            def stats(m, i, b, n=512):
                claim(b, "var_ready")
                got("sq_ready")
                mm(B[b][:, :n], mat(m), SQ[i % 2][:, :n], start=True, stop=True).then_inc(E["stats_done"], 1)

            def wait_h(k):
                got("h_ready")

            pe.wait_ge(E["mats_loaded"], 16)
            pe.wait_ge(E["rows_loaded"], dma_total["rows"])
            claim(0, "params_ready")
            nc.tensor.transpose(B[0][:, 0:N_COLS], PA[:], mat(IDENT)[0:N_COLS, 0:N_COLS])
            for l in range(LAYERS):
                ins = nc.tensor.transpose(B[0][:, P + l * P:P + l * P + MODT], PB[:, l, :], mat(IDENT)[0:MODT, 0:MODT])
            ins.then_inc(E["params_done"], 1)
            pe.wait_ge(E["x_loaded"], 32)
            for j in range(8):
                v, c = j // 4, j % 4
                b = (j + 1) % 8
                claim(b, "x_copied")
                for m in range(2):
                    for blk in range(TB):
                        ins = nc.tensor.transpose(bank2(b)[:, m, blk * P:(blk + 1) * P],
                                                  XS[:, v, blk, (2 * c + m) * P:(2 * c + m + 1) * P], mat(IDENT))
                ins.then_inc(E["x_done"], 1)
            pe.wait_ge(E["ws_masked"], 1)
            for i in range(2):
                claim(1 + i, "wst_ready")
                for g in range(4):
                    ins = nc.tensor.transpose(B[1 + i][:, g * P:(g + 1) * P], WS[:, 4 * i + g, :], mat(IDENT))
                ins.then_inc(E["ws_done"], 1)

            pe.wait_ge(E["silu_ready"], 1)
            pe.wait_ge(E["cs_ready"], 1)
            for l in range(LAYERS):
                with turns(MODT // 8, {**ring_counts(t.pos, 4, "fill"), "mod_read": 1}, ["mod_read"]):
                    claim(3, "mod_read")
                    for c in range(4):
                        s = t.take()
                        pe.wait_ge(raw_loaded[s], t.at(f"fill{s}") * 32)
                        w = RAW[s][:].rearrange("p (k n) -> p k n", k=KT)
                        for m in range(2):
                            o = B[3][:, 4 * c + 2 * m:4 * c + 2 * m + 2]
                            for k in range(KT):
                                ins = mm(o, w[:, k, m * P:(m + 1) * P], CS[:, k, :], start=(k == 0), stop=(k == KT - 1))
                        used(ins, s)

            mean_of_squares(S)
            for c in range(12):
                s = chunk()
                b = 4 + c % 2
                claim(b, "sq_ready" if c < 8 else "vb_ready")
                if c < 8:
                    t.n["sq_ready"] -= 1
                    release[b] = ("sq_ready", KT + c + 1)
                    for m in range(2):
                        ins = features(s, m * P, bank2(b)[:, m, :], hH, hL, S, wait_h if c == 0 and m == 0 else None)
                else:
                    for blk in range(TB):
                        ins = tokens(s, blk, bank2(b)[:, blk, :])
                used(ins, s)
                if 1 <= c <= 8:
                    stats(MEAN_HD, c - 1, 2 + (c - 1) % 2)

            pe.wait_ge(E["qk_ready"], 8)
            pe.wait_ge(E["vb_ready"], 4)
            SC = [T[0][:, 0:2 * P].rearrange("p (c n) -> p c n", c=2), T[1][:].rearrange("p (c n) -> p c n", c=2)]

            def head_out(h):
                claim(3, "o_ready")
                got("probT_ready")
                v = VB[:, :, h * P:(h + 1) * P]
                pT = T[3]
                mm(B[3][:, 0:P], v[:, 0, :], pT[:, 0:P], start=True, stop=True)
                mm(B[3][:, P:S], v[:, 0, :], pT[:, P:2 * P], start=True, stop=False)
                mm(B[3][:, P:S], v[:, 1, :], pT[:, 2 * P:3 * P], start=False, stop=True).then_inc(E["pv_done"], 1)

            for h in range(HEADS):
                for i in range(TB):
                    nk = P * (i + 1)
                    for c in range(2):
                        rows = slice(HD * c, HD * (c + 1))
                        claim(6 * i + c, "sc_read")
                        ins = mm(B[6 * i + c][:, 0:nk], QK[rows, h, i * P:(i + 1) * P], QK[rows, HEADS + h, 0:nk],
                                 start=True, stop=True)
                    ins.then_inc(E["scores_done"], 1)
                if h >= 1:
                    head_out(h - 1)
                s = chunk()
                b = 4 + h % 2
                if h < 4:
                    claim(b, "va_copied")
                    for blk in range(TB):
                        ins = tokens(s, blk, bank2(b)[:, blk, :])
                else:
                    claim(b, "ya_ready")
                    release[b] = ("ya_ready", t.next("ya_ready") - 1)
                    for m in range(2):
                        ins = features(s, m * P, bank2(b)[:, m, :], hH, hL, S)
                used(ins, s)
                claim(2, "probT_ready")
                t.n["probT_ready"] -= 1
                release[2] = ("probT_ready", h + 1)
                got("prob_ready")
                nc.tensor.transpose(B[2][:, 0:P], SC[0][:, 0, :], mat(IDENT))
                got("prob_ready")
                nc.tensor.transpose(B[2][:, P:2 * P], SC[1][:, 0, 0:P], mat(IDENT))
                nc.tensor.transpose(B[2][:, 2 * P:3 * P], SC[1][:, 0, P:S], mat(IDENT)).then_inc(E["probT_done"], 1)
                if h == 3:
                    got("va_ready")
                    t.next("var_ready")
                    pe.wait_ge(E["wst_ready"], 2)
                    for g in range(KT):
                        if g % 2 == 0:
                            claim(6 + g // 2 % 2, "zb_ready")
                        for blk in range(TB):
                            ins = mm(bank2(6 + g // 2 % 2)[:, g % 2, blk * P:(blk + 1) * P], VA[:, blk, g * P:(g + 1) * P],
                                     WST[:, g, :], start=True, stop=True)
                        if g % 2:
                            ins.then_inc(E["z_done"], 1)
            head_out(HEADS - 1)
            for j in range(4):
                stats(MEAN_P, j, 4 + j)

            for j in range(4):
                b = 4 * (j % 2)
                for n in range(4):
                    s = chunk()
                    claim(b + n, "gate_ready" if n < 2 else "up_read")
                    if j == 0 and n == 2:
                        pe.wait_ge(E["ya_ready"], 8)
                    if j == 0 and n == 3:
                        pe.wait_ge(E["yb_ready"], 4)
                    xh, xl = ((hH, hL), (hH, hL), (YAH, YAL), (YBH, YBL))[n]
                    for m in range(2):
                        ins = features(s, m * P, bank2(b + n)[:, m, :], xh, xl, S)
                    used(ins, s)
            pe.wait_ge(E["merged_ready"], 4)
            for j in range(4):
                s = chunk()
                claim(j, "x_ready")
                for m in range(2):
                    ins = features(s, m * P, bank2(j)[:, m, :], MH, ML, S)
                used(ins, s)

            mean_of_squares(S)
            for k in range(KT):
                got("h_ready")
            claim(1, "logits_read")
            NR = N_GROUPS + N_EXPERTS
            for blk in range(TB):
                for k in range(KT):
                    ins = mm(B[1][:, blk * NR:(blk + 1) * NR], HF2[:, k, blk * P:(blk + 1) * P], WR[:, k, :],
                             start=(k == 0), stop=(k == KT - 1))
            ins.then_inc(E["logits_done"], 1)
            got("comb_ready")
            claim(2, "combT_ready")
            comb = RT[:, 5, 0:TB * N_EXPERTS].rearrange("p (b e) -> p b e", b=TB)
            for blk in range(TB):
                ins = nc.tensor.transpose(B[2][0:N_EXPERTS, blk * P:(blk + 1) * P], comb[:, blk, :], mat(IDENT))
            ins.then_inc(E["combT_done"], 1)

            zeros = ZERO[:]
            pe.wait_ge(E["mod_read"], 1)
            for b in range(4, 8):
                claim(b, "x_ready")
                mm(B[b][:], zeros[:, 0:P], zeros[:], start=True, stop=False, skip_group_check=True)
            acc_release = {b: release.pop(b) for b in range(4, 8)}
            counts = {**ring_counts(t.pos, 12, "fill", "split"), "silu_ready": 4, "gated": 4, "hid_ready": 4}
            with turns(N_EXPERTS // 4, counts, ["silu_ready", "gated"]):
                for which, e in MOE_ORDER:
                    s = chunk()
                    if which == "w2":
                        got("hid_ready")
                        wh, wl = slot(s, k=2)
                        for m in range(KT):
                            for f in range(2):
                                ins = exact(bank2(4 + m // 2)[:, m % 2, :], wh[:, f, m * P:(m + 1) * P],
                                            wl[:, f, m * P:(m + 1) * P], HIDH[e % 2][:, f, :], HIDL[e % 2][:, f, :],
                                            False, False, skip_group_check=True)
                    else:
                        b = 2 * (e % 2) + (which == "w3")
                        claim(b, "gated" if which == "w3" else "silu_ready")
                        for f in range(2):
                            ins = features(s, f * P, bank2(b)[:, f, :], hH, hL, S)
                    used(ins, s)
            for b in range(4, 8):
                ins = mm(B[b][:, 0:2], zeros[:, 0:P], zeros[:, 0:2], start=False, stop=True, skip_group_check=True)
            ins.then_inc(E["acc_done"], 1)
            release.update(acc_release)

            def ffn(n):
                counts = {**ring_counts(t.pos, FT_HALF + KT, "fill", "split"), "silu_ready": FT_HALF, "gated": FT_HALF,
                          "hid_ready": FT_HALF, "x_ready": KT}
                with turns(2, counts, ["silu_ready", "gated", "x_ready"]):
                    for j in range(FT_HALF):
                        s = chunk()
                        wh, wl = slot(s, k=2 * KT)
                        for which in range(2):
                            b = 2 * (j % 2) + which
                            claim(b, ("silu_ready", "gated")[which])
                            for k in range(KT):
                                ins = exact(B[b][:, :n], wh[:, which * KT + k, :], wl[:, which * KT + k, :], hH[:, k, :n],
                                            hL[:, k, :n], k == 0, k == KT - 1)
                            if which == 0:
                                ins.then_inc(E["gate_done"], 1)
                        used(ins, s)
                    for m in range(KT):
                        s = chunk()
                        b = 4 + m % 4
                        claim(b, "x_ready")
                        wh = HI[s % HI_SLOTS][:, :FT_HALF * P].rearrange("p (k n) -> p k n", n=P)
                        wl = LO[s][:, :FT_HALF * P].rearrange("p (k n) -> p k n", n=P)
                        for k in range(FT_HALF):
                            if m == 0:
                                got("hid_ready")
                            ins = exact(B[b][:, :n], wh[:, k, :], wl[:, k, :], aH[:, k, :n], aL[:, k, :n], k == 0,
                                        k == FT_HALF - 1)
                        used(ins, s)
                    t.pos += 1

            def mixers(l):
                n = 2 * S if l + 1 < LAYERS else S
                sets = n // S
                for c in range(5):
                    s = chunk()
                    if c < 2:
                        for m in range(2):
                            claim(2 * c + m, "q_copied")
                            ins = features(s, m * P, B[2 * c + m][:, :n], hH, hL, n)
                    elif c == 2:
                        claim(4, "q_copied")
                        features(s, 0, B[4][:], hH, hL, 2 * S)
                        claim(5, "v_ready")
                        for blk in range(2 * TB):
                            ins = tokens(s, blk, B[5][:, blk * P:(blk + 1) * P], P, P)
                    else:
                        for blk in range(sets * TB):
                            b = [6, 0][c - 3] + blk // TB
                            if blk % TB == 0:
                                claim(b, "pf_ready")
                            ins = tokens(s, blk, bank2(b)[:, blk % TB, :])
                    used(ins, s)
                for i in range(6):
                    if i < 5:
                        stats(MEAN_HD, i, 2 + i % 2, n if i < 4 else 2 * S)
                    if i >= 1:
                        got("qn_ready")
                        claim(4 + (i - 1) % 2, "q_ready")
                        mm(B[4 + (i - 1) % 2][:, :S], mat(ROT), QQ[:, i - 1, 0:S], start=True, stop=True)\
                            .then_inc(E["rot_done"], 1)
                pe.wait_ge(E["q_ready"], 5 * (l + 1))
                for kv in range(2):
                    claim(6 + kv, "kd_ready")
                    mm(B[6 + kv][:], mat(DUP0 + kv), QQ[:, 4, :], start=True, stop=True).then_inc(E["dup_done"], 1)
                pe.wait_ge(E["pf_ready"], t.n["pf_ready"])
                if l == 0:
                    pe.wait_ge(E["mix_consts_loaded"], dma_total["mix"])
                for p in range(2):
                    for s in range(sets):
                        claim(6, "pm_ready")
                        for g in range(2):
                            for blk in range(TB):
                                ins = mm(bank2(6)[:, g, :], PF[:, 2 * s + blk, 0, p * P:(p + 1) * P], POOL[:, 2 * p + g, blk, :],
                                         start=(blk == 0), stop=(blk == TB - 1))
                        ins.then_inc(E["pool_done"], 1)
                    pe.wait_ge(E["pm_ready"], t.n["pm_ready"])
                    claim(7, "mix_ready")
                    mm(B[7][:, :n], PWB[:, l, p, :], T[4][:, :n], start=True, stop=True).then_inc(E["pwb_done"], 1)
                for p in range(2):
                    for s in range(sets):
                        claim(6, "ab_ready")
                        for f in range(2):
                            for blk in range(TB):
                                ins = mm(bank2(6)[:, f, :], PF[:, 2 * s + blk, 1, p * P:(p + 1) * P], DFT[:, f, blk, :],
                                         start=(blk == 0), stop=(blk == TB - 1))
                        ins.then_inc(E["fftab_done"], 1)
                        pe.wait_ge(E["ab_ready"], t.n["ab_ready"])
                        claim(7, "ft_ready")
                        mm(B[7][:, :S], mat(DFT_C), AB[:, 0:S], start=True, stop=False)
                        mm(B[7][:, :S], mat(DFT_S), AB[:, S:2 * S], start=False, stop=True).then_inc(E["fft_done"], 1)
                pe.wait_ge(E["ft_ready"], t.n["ft_ready"])
                for d in range(2):
                    claim(6 + d, "mix_ready")
                    for p in range(2):
                        ins = mm(B[6 + d][:, :n], FW[:, l, p, d * P:(d + 1) * P], T[2 + p][:, :n], start=(p == 0), stop=(p == 1))
                    ins.then_inc(E["yf_done"], 1)
                pe.wait_ge(E["kd_ready"], t.n["kd_ready"])
                pe.wait_ge(E["v_ready"], l + 1)
                if l == 0:
                    t.n["exp_ready"] += HEADS * TB
                units = attention_units(l)
                for u in range(len(units) + 2):
                    if u < len(units):
                        h, q0, k0, nk = units[u]
                        rows = slice(HD * (h % 2), HD * (h % 2) + HD)
                        claim(u % 2, "exp_ready")
                        mm(B[u % 2][:, :nk], QQ[rows, h // 2, q0:q0 + P], KD[rows, h // 4, k0:k0 + nk], start=True, stop=True)\
                            .then_inc(E["scores_done"], 1)
                    if 1 <= u <= len(units):
                        h, q0, k0, nk = units[u - 1]
                        b = 2 + (u - 1) % 2
                        claim(b, "probT_ready")
                        t.n["probT_ready"] -= 1
                        release[b] = ("probT_ready", t.n["probT_ready"] + (2 if u >= 2 else 1))
                        got("prob_ready")
                        for kb in range(nk // P):
                            ins = nc.tensor.transpose(B[b][:, kb * P:(kb + 1) * P], T[(u - 1) % 2][:, kb * P:(kb + 1) * P],
                                                      mat(IDENT))
                        ins.then_inc(E["probT_done"], 1)
                    if u >= 2:
                        h, q0, k0, nk = units[u - 2]
                        b = 4 + (u - 2) % 2
                        got("probT_ready")
                        claim(b, "mix_ready")
                        for kb in range(nk // P):
                            ins = mm(B[b][:, 0:P], VD[:, k0 // P + kb, h // 4, :, :].rearrange("p a d -> p (a d)"),
                                     T[2 + (u - 2) % 2][:, kb * P:(kb + 1) * P], start=(kb == 0), stop=(kb == nk // P - 1))
                        ins.then_inc(E["pv_done"], 1)
                pe.wait_ge(E["mix_ready"], t.n["mix_ready"])
                for j in range(4):
                    s = chunk()
                    for m in (2 * j, 2 * j + 1):
                        claim(m, "x_ready")
                        ins = features(s, (m % 2) * P, B[m][:, :n], XH, XL, n)
                    used(ins, s)

            def norm(n):
                mean_of_squares(n)
                for k in range(KT):
                    got("h_ready")

            for l in range(LAYERS):
                n = 2 * S if l + 1 < LAYERS else S
                norm(2 * S)
                ffn(2 * S)
                norm(2 * S)
                mixers(l)
                norm(n)
                ffn(n)

            mean_of_squares(S)
            pe.wait_ge(E["hf_done"], KT)
            for j in range(4):
                blk, half = j // 2, j % 2
                claim(1 + j, "outb_ready")
                for k in range(4):
                    ins = nc.tensor.transpose(B[1 + j][:, k * P:(k + 1) * P], HF[:, 4 * half + k, blk * P:(blk + 1) * P],
                                              mat(IDENT))
                ins.then_inc(E["fin_done"], 1)


INPUTS = ("x norm1_g w_in v_norm_g w_s b_s q_norm_g k_norm_g lambda_q1 lambda_k1 lambda_q2 lambda_k2 sub_norm_g w_up_a "
          "w_up_b w_gate b_gate w_out norm2_g w_rg b_rg w_re b_re w1 w3 w2 c_2 ctx_2 c_ctx_2 ada_w_2 ada_b_2 ffn1_w_gu_2 "
          "ffn1_w_down_2 w_in_2 q_gain_2 k_gain_2 pool_w_2 pool_scale_2 fft_w_2 w_out_2 ffn2_w_gu_2 ffn2_w_down_2 "
          "final_gain_2").split()


def constants():
    import numpy as np

    i = np.arange(P)
    mats = np.zeros((P, N_MATS, P))
    mats[:, IDENT] = np.eye(P)
    mats[:, MEAN_D] = 1.0 / D
    mats[:, MEAN_P] = 1.0 / P
    half = i // HD
    mats[:, MEAN_HD] = (half[:, None] == half[None, :]) / HD
    q = HD // 2
    for d in range(P):
        if d % HD < q:
            mats[d + q, ROT, d] = -1.0
        else:
            mats[d - q, ROT, d] = 1.0
    for kv in range(2):
        for d in range(P):
            mats[HD * kv + d % HD, DUP0 + kv, d] = 1.0
    group = (half[:, None] == half[None, :])
    angle = 2 * np.pi * np.outer(i % HD, i % HD) / HD
    norm = 1.0 / math.sqrt(S * HD)
    mats[:, DFT_C] = group * np.cos(angle) * norm
    mats[:, DFT_S] = group * -np.sin(angle) * norm
    s = np.arange(S)
    tok = 2 * np.pi * (np.outer(s, s) % S) / S
    dft = np.stack([np.cos(tok), np.sin(tok)]).reshape(2, TB, P, S).transpose(2, 0, 1, 3)
    pool = np.zeros((4, S, S))
    for g, w in enumerate((2, 4, 8, 16)):
        for to in range(S):
            lo, hi = max(to - w // 2, 0), min(to + w - w // 2, S)
            pool[g, lo:hi, to] = 1.0 / (hi - lo)
        pool[g] -= np.eye(S)
    pool = pool.reshape(4, TB, P, S).transpose(2, 0, 1, 3)
    n_freq = HD // 4
    inv = 10000.0 ** (-np.arange(n_freq) / n_freq)
    ang = np.concatenate([(s // 64)[:, None] * inv, (s % 64)[:, None] * inv], axis=1)
    trig = np.stack([np.cos(ang), np.sin(ang)])[:, :, i % q].transpose(2, 0, 1)
    dist = s[:, None] - s[None, :]
    neg = np.where(dist >= 0, -dist, -BIG).reshape(TB, P, S).transpose(1, 0, 2)
    falling = np.concatenate([np.arange(n, 0, -1) for n in (N_GROUPS, PER_GROUP)])
    tables = {"mats": mats, "dft": dft, "pool_mix": pool, "trig": trig, "neg_dist": neg, "descending": falling}
    return {k: np.ascontiguousarray(v, dtype=np.float32) for k, v in tables.items()}


def kernel(**inputs):
    import numpy as np
    import concourse.bacc as bacc
    from concourse.bass_utils import run_bass_kernel_spmd

    nc = bacc.Bacc("TRN2", target_bir_lowering=False, num_devices=1)
    given = {f"in_{n}": np.ascontiguousarray(inputs[n]) for n in INPUTS}
    given.update({f"in_{n}": v for n, v in constants().items()})
    handles = {n[3:]: nc.dram_tensor(n, v.shape, F32, kind="ExternalInput").ap() for n, v in given.items()}
    out = nc.dram_tensor("out", (1, S, D), F32, kind="ExternalOutput").ap()
    comb_rows = nc.dram_tensor("comb_rows", (N_EXPERTS, S), F32, kind="Internal").ap()
    build(nc, handles, out, comb_rows)
    got = run_bass_kernel_spmd(nc, [given], core_ids=[0])
    return got.results[0]["out"]
```

```python
import math
from collections import Counter
from contextlib import ExitStack, contextmanager

from concourse import mybir

F32 = mybir.dt.float32
F32R = mybir.dt.float32r
ACT = mybir.ActivationFunctionType
ALU = mybir.AluOpType
AX = mybir.AxisListType.X

P = 128
D = 1024
KT = D // P
S = 256
TB = S // P
EPS = 1e-6
HEADS = 8
LAM_INIT = 0.8 - 0.6
N_GROUPS, PER_GROUP = 4, 8
N_EXPERTS = N_GROUPS * PER_GROUP
FE = D // 4
LAYERS = 2
D_FF = ((8 * D // 3 + 127) // 128) * 128
FT_HALF = D_FF // P // 2
N_MOD = 9
MODT = N_MOD * KT
ADA_W = 512
ADA_STEPS = N_MOD * D // ADA_W
CT_W = 32
COL_TILES = P // CT_W
HD = 64
BIG = 1e30

RAW_SLOTS = 4
HI_SLOTS = 2
CHUNK = 2048
SPLIT = CHUNK

N1, N2, BG, VG, CV, PS, FG, SN, QN, KN, QG2, KG2, N_COLS = 0, 8, 16, 32, 40, 56, 60, 68, 69, 70, 71, 73, 75
IDENT, MEAN_D, MEAN_P, MEAN_HD, ROT, DUP0, DUP1, DFT_C, DFT_S, N_MATS = range(10)

MOE_ORDER = [("w1", 0), ("w3", 0), ("w1", 1), ("w3", 1), ("w2", 0), ("w1", 2), ("w3", 2), ("w2", 1),
             ("w1", 3), ("w3", 3), ("w2", 2), ("w2", 3)]


START = {"gated": 1, "silu_ready": 1}


class Tally:

    def __init__(self, eng):
        self.eng, self.n, self.turn, self.per = eng, Counter(START), None, {}
        self.pos = self.used = 0

    def at(self, key, back=0):
        v = self.n[key] - back
        if self.turn is not None and self.per.get(key):
            v = self.turn * self.per[key] + v
        return v

    def next(self, key, by=1):
        self.n[key] += by
        return self.at(key)

    @contextmanager
    def loop(self, turns, per):
        before = Counter(self.n)
        with self.eng.Fori(0, turns) as i:
            self.turn, self.per = i, per
            yield i
        self.turn = None
        grown = {k: v - before[k] for k, v in self.n.items() if v != before[k]}
        assert grown == {k: v for k, v in per.items() if v}, (grown, per)
        for k, v in grown.items():
            self.n[k] += v * (turns - 1)

    def take(self):
        s = self.pos % RAW_SLOTS
        self.pos += 1
        self.next(f"fill{s}")
        return s

    def use(self):
        s = self.used % RAW_SLOTS
        self.used += 1
        return s, self.next(f"used{s}")


def ring_counts(pos, chunks, *kinds):
    out = Counter()
    for i in range(chunks):
        for kind in kinds:
            out[f"{kind}{(pos + i) % RAW_SLOTS}"] += 1
    return out


def build(nc, a, out, comb_rows):
    ctx = ExitStack()
    with ctx:
        def sem(name):
            return ctx.enter_context(nc.semaphore(name))

        base = 16512
        cursor = [base]

        def sb(name, shape, dt=F32):
            n = 4
            for d in shape[1:]:
                n *= d
            h = nc.alloc_sbuf_tensor_at(name, shape, dt, offset=cursor[0])
            cursor[0] += (n + 31) // 32 * 32
            return h

        XC = sb("XC", [P, KT, 2 * S])
        hH, hL = (sb(n, [P, KT, 2 * S], F32R) for n in ("hH", "hL"))
        raw_at = cursor[0]
        RAW = [sb(f"RAW{i}", [P, CHUNK]) for i in range(RAW_SLOTS)]
        LO = [nc.alloc_sbuf_tensor_at(f"LO{i}", [P, CHUNK], F32R, offset=raw_at + 4 * CHUNK * i)
              for i in range(RAW_SLOTS)]
        HI = [sb(f"HI{i}", [P, CHUNK], F32R) for i in range(HI_SLOTS)]
        T = [sb(f"T{i}", [P, 512]) for i in range(6)]
        SQ = T[4:6]
        ACC = T[4]
        R = [sb(f"R{i}", [P, 512]) for i in range(2)]
        MATS = sb("MATS", [P, N_MATS, P])
        WR = sb("WR", [P, KT, N_GROUPS + N_EXPERTS])
        BR = sb("BR", [P, N_GROUPS + N_EXPERTS])
        PT = sb("PT", [P, N_COLS])
        ADB = sb("ADB", [P, LAYERS, MODT])
        MOD = sb("MOD", [P, LAYERS, MODT, 2])
        CS = sb("CS", [P, KT, CT_W])
        ASEL = sb("ASEL", [P, 2])
        GQ = sb("GQ", [P, 2])
        ZERO = sb("ZERO", [P, 512])
        DESC = sb("DESC", [P, N_GROUPS + PER_GROUP])
        EPSC = sb("EPSC", [P, 1])
        SM, SM2 = sb("SM", [P, 32]), sb("SM2", [P, 32])
        SM3 = sb("SM3", [P, 16])
        union = cursor[0]

        def at(kb, name, shape, dt=F32):
            return nc.alloc_sbuf_tensor_at(name, shape, dt, offset=union + 1024 * kb)

        QK = at(0, "QK", [P, 2 * HEADS, S])
        MH, ML = at(0, "MH", [P, KT, S], F32R), at(8, "ML", [P, KT, S], F32R)
        VB = at(16, "VB", [P, TB, D])
        ZB = at(24, "ZB", [P, KT, S])
        VA = at(32, "VA", [P, TB, D])
        WST = at(40, "WST", [P, KT, P])
        BSB = at(44, "BSB", [P, KT, P])
        YAH, YAL = at(48, "YAH", [P, KT, S], F32R), at(56, "YAL", [P, KT, S], F32R)
        YBH, YBL = at(64, "YBH", [P, KT, S], F32R), at(72, "YBL", [P, KT, S], F32R)
        XS = at(48, "XS", [P, 2, TB, D])
        WS = at(64, "WS", [P, KT, P])
        PA = at(68, "PA", [N_COLS, P])
        PB = at(69, "PB", [MODT, LAYERS, P])
        HF1 = at(72, "HF1", [P, KT, S])
        ND = at(80, "ND", [P, TB, S])
        LV = at(82, "LV", [P, 4, HD])
        CB = at(0, "CB", [P, N_EXPERTS, S])
        HIDH = [at(32 + 4 * i, f"HIDH{i}", [P, 2, S], F32R) for i in range(2)]
        HIDL = [at(34 + 4 * i, f"HIDL{i}", [P, 2, S], F32R) for i in range(2)]
        HF2 = at(40, "HF2", [P, KT, S])
        RT = at(48, "RT", [P, 12, 2 * 36])
        CT = at(52, "CT", [N_EXPERTS, S])
        aH, aL = at(0, "aH", [P, FT_HALF, 2 * S], F32R), at(22, "aL", [P, FT_HALF, 2 * S], F32R)
        HF = at(45, "HF", [P, KT, 2 * S])
        OUTB = at(0, "OUTB", [P, TB, D])
        XH, XL = at(0, "XH", [P, KT, 2 * S], F32R), at(16, "XL", [P, KT, 2 * S], F32R)
        QQ = at(32, "QQ", [P, 5, 2 * S])
        KD = at(42, "KD", [P, 2, 2 * S])
        VD = at(46, "VD", [P, 2 * TB, 2, 2, HD])
        AB = at(58, "AB", [P, 2 * S])
        PF = at(50, "PF", [P, 2 * TB, 2, S])
        POOL = at(61, "POOL", [P, 4, TB, S])
        DFT = at(69, "DFT", [P, 2, TB, S])
        TRIG = at(73, "TRIG", [P, 2, S])
        PWB = at(75, "PWB", [P, LAYERS, 2, P])
        FW = at(77, "FW", [P, LAYERS, 2, S])
        assert union + 1024 * 83 <= nc.sbuf_usable_end, (union + 1024 * 83 - nc.sbuf_usable_end)

        h_at = [base + 4 * KT * 2 * S * i for i in (1, 2)]
        HF32 = [nc.alloc_sbuf_tensor_at(f"HF32_{i}", [P, KT, 2 * S], F32, offset=h_at[i]) for i in range(2)]
        ADW = [[h[:, :, S:].rearrange("p (k b) n -> p k b n", b=2) for h in HF32],
               [h[:, k:k + 4, :].rearrange("p k (b n) -> p k b n", b=2) for h in HF32 for k in (0, 4)]]
        ADW[0] += [at(64 + 8 * i, f"ADW{i}", [P, 4, 2, S])[:] for i in range(2)]
        ADT = [T[5], at(81, "ADT1", [P, ADA_W])]
        SC = [[T[0][:, 2 * P * i:2 * P * (i + 1)].rearrange("p (c n) -> p c n", c=2),
               T[(1, 4)[i]][:].rearrange("p (c n) -> p c n", c=2)] for i in range(2)]

        B = [ctx.enter_context(nc.psum_tensor(f"B{i}", [P, 512], F32)) for i in range(8)]

        raw_loaded = [sem(f"raw_loaded{i}") for i in range(RAW_SLOTS)]
        hi_done = [sem(f"hi_done{i}") for i in range(RAW_SLOTS)]
        lo_done = [sem(f"lo_done{i}") for i in range(RAW_SLOTS)]
        slot_used = [sem(f"slot_used{i}") for i in range(RAW_SLOTS)]
        ada_loaded = [sem(f"ada_loaded{i}") for i in range(4)]
        ada_used = [sem(f"ada_used{i}") for i in range(4)]
        names = (
            "x_loaded rows_loaded ws_loaded mats_loaded misc_loaded mix_consts_loaded comb_stored comb_loaded out_stored "
            "params_done x_done ws_done sq_used stats_done z_done scores_done probT_done pv_done "
            "logits_done combT_done gate_done acc_done rot_done dup_done pool_done "
            "pwb_done fftab_done fft_done yf_done fin_done ada_done "
            "vec_step params_ready mod_read var_ready r_ready h_ready qk_ready vb_ready va_ready zb_ready ya_ready yb_ready "
            "lam_sums sc_read max_ready prob_ready up_read merged_ready logits_read top_ready m2_ready comb_ready combT_ready "
            "gated hid_ready x_ready xn_ready qn_ready q_ready mix_ready hf_done "
            "ada_copied cs_ready x_copied wst_ready sq_ready std_ready qk_copied vb_copied va_copied lam_exps exp_ready probT_ready "
            "o_ready gate_ready exp4_ready exp2_ready silu_ready hf_ready q_copied kd_ready v_ready pf_ready pm_ready "
            "ab_ready ft_ready mix_hi outb_ready "
            "pool_step ws_masked pwb_zero acc_ready xp_ready").split()
        E = {n: sem(n) for n in names}
        dma_total = Counter()

        def mat(i):
            return MATS[:, i, :]

        def bank2(b):
            return B[b][:].rearrange("p (a n) -> p a n", a=2)

        def pair(x, j):
            return x[:, 2 * j:2 * j + 2, :].rearrange("p a n -> p (a n)")

        def attention_units(l):
            units = [(h, P * i, 0, 2 * S) for h in range(8) for i in range(TB)]
            if l + 1 < LAYERS:
                units += [(h, S + P * i, S, S) for h in range(8) for i in range(TB)]
            return units

        SCORE_BANKS, PROBS = (0, 1, 5), (T[0], T[1], T[4])
        ADA_CHUNKS = (9, 10, 11)
        ada_at = [min(len(ADA_CHUNKS) + 2 * h, ADA_STEPS) for h in range(HEADS + 1)]
        MIX_STEPS = 2 * 2 * 2

        def ada_beside(l, u):
            if l + 1 < LAYERS:
                last, left = len(attention_units(l)) + 2, ADA_STEPS - MIX_STEPS
                return {k * last // (left - 1): (l + 1) * ADA_STEPS + MIX_STEPS + k for k in range(left)}.get(u)

        def bc(x, dim, shape):
            return x.unsqueeze(dim).to_broadcast(shape)

        block = ctx.enter_context(nc.Block())

        @block.sync
        def _(sp):
            t = Tally(sp)

            def chunk(first, second, words):
                s = t.take()
                if t.n[f"fill{s}"] > 1:
                    sp.wait_ge(slot_used[s], t.at(f"fill{s}", 1))
                h0 = words[0]
                sp.dma_start(RAW[s][:, 0:h0].rearrange("p (k n) -> p k n", n=first.shape[-1]), first)\
                    .then_inc(raw_loaded[s], 16)
                sp.dma_start(RAW[s][:, h0:h0 + words[1]].rearrange("p (k n) -> p k n", n=second.shape[-1]), second)\
                    .then_inc(raw_loaded[s], 16)

            def columns(w, c0):
                v = w.rearrange("(k p) n -> p k n", p=P)
                chunk(v[:, 0:4, c0:c0 + 256], v[:, 4:8, c0:c0 + 256], (1024, 1024))

            def ffn(l, gu, down):
                g = a[gu][l].rearrange("(k p) (t h n) -> p k t h n", p=P, t=2, h=2)
                w = a[down][l].rearrange("(h k p) n -> p h k n", p=P, h=2)
                with t.loop(2, ring_counts(t.pos, FT_HALF + KT, "fill")) as half:
                    for j in range(FT_HALF):
                        chunk(g[:, :, 0, half, j * P:(j + 1) * P], g[:, :, 1, half, j * P:(j + 1) * P], (1024, 1024))
                    for m in range(KT):
                        chunk(w[:, half, 0:6, m * P:(m + 1) * P], w[:, half, 6:11, m * P:(m + 1) * P], (768, 640))
                    t.pos += 1

            x_v = a["x"][0].rearrange("(b p) d -> p b d", p=P)
            c_v = a["ctx_2"][0].rearrange("(b p) d -> p b d", p=P)
            sp.dma_start(XS[:, 0], x_v).then_inc(E["x_loaded"], 16)
            sp.dma_start(XS[:, 1], c_v).then_inc(E["x_loaded"], 16)
            sp.dma_start(WS[:], a["w_s"][0].rearrange("g t s -> t g s")).then_inc(E["ws_loaded"], 16)
            w_in = a["w_in"][0]
            for c in range(8):
                columns(w_in, 2 * D + 256 * c)
            for c in range(4):
                columns(w_in, 4 * D + 256 * c)
            for c in range(4):
                columns(w_in, D + 256 * c)
            for c in range(4):
                columns(w_in, 256 * c)
            for c in range(4):
                columns(a["w_gate"][0], 256 * c)
                columns(a["w_gate"][0], D + 256 * c)
                columns(a["w_up_a"][0], 256 * c)
                columns(a["w_up_b"][0], 256 * c)
            for c in range(4):
                columns(a["w_out"][0], 256 * c)
            w1 = a["w1"][0].rearrange("e (k p) n -> p e k n", p=P)
            w3 = a["w3"][0].rearrange("e (k p) n -> p e k n", p=P)
            w2 = a["w2"][0].rearrange("e (k p) n -> p e k n", p=P)
            with t.loop(N_EXPERTS // 4, ring_counts(t.pos, 12, "fill")) as i:
                for which, e in MOE_ORDER:
                    if which == "w2":
                        chunk(w2[:, i * 4 + e, 0:1, :], w2[:, i * 4 + e, 1:2, :], (1024, 1024))
                    else:
                        v = w1 if which == "w1" else w3
                        chunk(v[:, i * 4 + e, 0:4, :], v[:, i * 4 + e, 4:8, :], (1024, 1024))
            for l in range(LAYERS):
                ffn(l, "ffn1_w_gu_2", "ffn1_w_down_2")
                for c in range(5):
                    columns(a["w_in_2"][l], 256 * c)
                for c in range(4):
                    columns(a["w_out_2"][l], 256 * c)
                ffn(l, "ffn2_w_gu_2", "ffn2_w_down_2")
            sp.wait_ge(E["outb_ready"], 4)
            sp.dma_start(out[0].rearrange("(b p) d -> p b d", p=P), OUTB[:]).then_inc(E["out_stored"], 16)
            sp.wait_ge(E["out_stored"], 16)

        @block.gpsimd
        def _(pool):
            t = Tally(pool)

            def link(ins):
                ins.then_inc(E["pool_step"], 1)
                pool.wait_ge(E["pool_step"], t.next("pool_step"))

            def squares(tiles, n, fresh, c0=0):
                for k in range(tiles):
                    fresh(k)
                    x = XC[:, k, c0:c0 + n]
                    acc, sq = ACC[:, c0:c0 + n], R[1][:, c0:c0 + n]
                    ins = nc.gpsimd.tensor_tensor(acc if k == 0 else sq, x, x, ALU.mult)
                    if k > 0:
                        link(ins)
                        ins = nc.gpsimd.tensor_tensor(acc, acc, sq, ALU.add)
                    if k < tiles - 1:
                        link(ins)
                ins.then_inc(E["acc_ready"], 1)

            def by_pair(k):
                if k % 2 == 0:
                    pool.wait_ge(E["x_ready"], t.next("x_ready"))

            def by_tile(k):
                pool.wait_ge(E["x_ready"], t.next("x_ready"))

            def normed(n):
                pool.wait_ge(E["r_ready"], t.next("r_ready"))
                for k in range(1, KT, 2):
                    nc.gpsimd.tensor_tensor(HF[:, k, :n], XC[:, k, :n], R[0][:, :n], ALU.mult).then_inc(E["xp_ready"], 1)

            def norm(n):
                squares(KT - 1, n, by_tile)
                t.next("x_ready")
                normed(n)

            def ada_weights(l):
                v = a["ada_w_2"][l].rearrange("(h k p) (i b n) -> p h k i b n", p=P, h=2, b=2, n=S)

                def two_steps(i, first):
                    for k in range(2):
                        if first and k:
                            pool.wait_ge(E["ws_done"], 2)
                            pool.wait_ge(E["h_ready"], KT)
                        for half in range(2):
                            place = 2 * k + half
                            if not first:
                                pool.wait_ge(ada_used[place], t.next(f"ada_used{place}"))
                            for b in range(2):
                                pool.dma_start(ADW[l][place][:, :, b, :], v[:, half, :, i * 2 + k, b, :])\
                                    .then_inc(ada_loaded[place], 16)

                peeled = 1 if l == 0 else 0
                if peeled:
                    two_steps(0, True)
                with t.loop(ADA_STEPS // 2 - peeled, {f"ada_used{place}": 1 for place in range(4)}) as i:
                    two_steps(i + peeled, False)

            rows = [("norm1_g", N1, 8), ("norm2_g", N2, 8), ("b_gate", BG, 16), ("v_norm_g", VG, 8), ("c_2", CV, 8),
                    ("c_ctx_2", CV + 8, 8), ("pool_scale_2", PS, 4), ("final_gain_2", FG, 8), ("sub_norm_g", SN, 1)]
            n = 0

            def flat(x):
                while len(x.shape) > 1:
                    x = x.rearrange("a b c -> (a b) c") if len(x.shape) == 3 else x.rearrange("a b -> (a b)")
                return x

            pool.dma_start(MATS[:], a["mats"]).then_inc(E["mats_loaded"], 16)
            for name, c0, k in rows:
                pool.dma_start(PA[c0:c0 + k, :], flat(a[name]).rearrange("(r p) -> r p", p=P))\
                    .then_inc(E["rows_loaded"], 16)
                n += 1
            for name, l, c0 in (("q_norm_g", 0, QN), ("k_norm_g", 0, KN), ("q_gain_2", 0, QG2), ("q_gain_2", 1, QG2 + 1),
                                ("k_gain_2", 0, KG2), ("k_gain_2", 1, KG2 + 1)):
                for half in range(2):
                    pool.dma_start(PA[c0:c0 + 1, half * HD:(half + 1) * HD], a[name][l:l + 1, :])\
                        .then_inc(E["rows_loaded"], 16)
                    n += 1
            pool.dma_start(PB[:], a["ada_b_2"].rearrange("l (r p) -> r l p", p=P)).then_inc(E["rows_loaded"], 16)
            n += 1
            dma_total["rows"] = 16 * n
            for i, name in enumerate(("lambda_q1", "lambda_k1", "lambda_q2", "lambda_k2")):
                pool.dma_start(LV[:, i, :], a[name][0].partition_broadcast(P)).then_inc(E["misc_loaded"], 16)
            pool.dma_start(ND[:], a["neg_dist"]).then_inc(E["misc_loaded"], 16)
            pool.dma_start(BSB[:].rearrange("p g t -> p (g t)"), flat(a["b_s"]).partition_broadcast(P))\
                .then_inc(E["misc_loaded"], 16)
            pool.dma_start(BR[:, 0:N_GROUPS], a["b_rg"][0].partition_broadcast(P)).then_inc(E["misc_loaded"], 16)
            pool.dma_start(BR[:, N_GROUPS:], a["b_re"][0].partition_broadcast(P)).then_inc(E["misc_loaded"], 16)
            pool.dma_start(WR[:, :, 0:N_GROUPS], a["w_rg"][0].rearrange("(k p) n -> p k n", p=P))\
                .then_inc(E["misc_loaded"], 16)
            pool.dma_start(WR[:, :, N_GROUPS:], a["w_re"][0].rearrange("(k p) n -> p k n", p=P))\
                .then_inc(E["misc_loaded"], 16)
            pool.dma_start(DESC[:], a["descending"].partition_broadcast(P)).then_inc(E["misc_loaded"], 16)
            pool.dma_start(ASEL[:], a["ada_select"]).then_inc(E["misc_loaded"], 16)
            dma_total["misc"] = 16 * 12
            pool.wait_ge(E["ws_loaded"], 16)
            nc.gpsimd.affine_select(out=WS[:], in_=WS[:], compare_op=ALU.is_ge, fill=0.0, base=0,
                                    pattern=[[0, KT], [-1, P]], channel_multiplier=1).then_inc(E["ws_masked"], 1)
            ada_weights(0)
            squares(KT - 1, S, by_pair)
            pool.wait_ge(E["combT_ready"], 1)
            pool.dma_start(comb_rows, CT[:]).then_inc(E["comb_stored"], 16)
            pool.wait_ge(E["comb_stored"], 16)
            pool.dma_start(CB[:].rearrange("p e t -> p (e t)"),
                           comb_rows.rearrange("e t -> (e t)").partition_broadcast(P)).then_inc(E["comb_loaded"], 16)
            squares(KT, S, lambda k: None, S)
            pool.dma_start(POOL[:], a["pool_mix"]).then_inc(E["mix_consts_loaded"], 16)
            pool.dma_start(DFT[:], a["dft"]).then_inc(E["mix_consts_loaded"], 16)
            pool.dma_start(TRIG[:], a["trig"]).then_inc(E["mix_consts_loaded"], 16)
            pool.dma_start(FW[:], a["fft_w_2"].rearrange("l (t p) n -> p l t n", p=P))\
                .then_inc(E["mix_consts_loaded"], 16)
            nc.gpsimd.memset(PWB[:], 0.0).then_inc(E["pwb_zero"], 1)
            pool.wait_ge(E["pwb_zero"], 1)
            for l in range(LAYERS):
                for g in range(4):
                    p0 = HD * (g % 2)
                    pool.dma_start(PWB[p0:p0 + HD, l, g // 2, p0:p0 + HD], a["pool_w_2"][l, g])\
                        .then_inc(E["mix_consts_loaded"], 16)
            dma_total["mix"] = 16 * (4 + 4 * LAYERS)
            t.n["x_ready"] += KT // 2
            normed(2 * S)
            for l in range(LAYERS):
                n = 2 * S if l + 1 < LAYERS else S
                t.n["x_ready"] += KT
                norm(2 * S)
                if l + 1 < LAYERS:
                    pool.wait_ge(E["pf_ready"], 4 * (l + 1))
                    ada_weights(l + 1)
                norm(n)
                t.n["x_ready"] += KT
                if l + 1 < LAYERS:
                    norm(n)
            squares(KT - 1, S, by_tile)

        @block.vector
        def _(ve):
            t = Tally(ve)
            V = nc.vector

            def link(ins):
                ins.then_inc(E["vec_step"], 1)
                ve.wait_ge(E["vec_step"], t.next("vec_step"))

            def got(name):
                ve.wait_ge(E[name], t.next(name))

            def products():
                s, n = t.use()
                ve.wait_ge(slot_used[s], n)

            def prep(words=CHUNK):
                s = t.take()
                ve.wait_ge(hi_done[s], t.next(f"split{s}"))
                V.tensor_tensor(LO[s][:, :words], RAW[s][:, :words], HI[s % HI_SLOTS][:, :words].bitcast(F32),
                                ALU.subtract).then_inc(lo_done[s], 1)

            def split(hi, lo, x, done):
                link(V.tensor_copy(hi, x))
                V.tensor_tensor(lo, x, hi.bitcast(F32), ALU.subtract).then_inc(E[done], 1)

            def rstd(r):
                got("std_ready")
                link(V.reciprocal(r, r))

            V.memset(EPSC[:], EPS)
            V.memset(CS[:], 0.0).then_inc(E["silu_ready"], START["silu_ready"])
            V.memset(ZERO[:], 0.0).then_inc(E["gated"], START["gated"])
            got("params_done")
            V.tensor_copy(PT[:], B[0][:, 0:N_COLS])
            for l in range(LAYERS):
                ins = V.tensor_copy(ADB[:, l, :], B[0][:, P + l * P:P + l * P + MODT])
            link(ins)
            V.tensor_scalar(GQ[:, 0:1], PT[:, QN:QN + 1], HD ** -0.5, None, ALU.mult)
            V.tensor_scalar(GQ[:, 1:2], PT[:, SN:SN + 1], 1.0 - LAM_INIT, None, ALU.mult).then_inc(E["params_ready"], 1)
            ve.wait_ge(E["misc_loaded"], dma_total["misc"])
            lv = LV[:].rearrange("p (a b) d -> p a b d", b=2)
            prod = T[1][:, 0:2 * HD].rearrange("p (a d) -> p a d", a=2)
            link(V.tensor_tensor(prod, lv[:, :, 0, :], lv[:, :, 1, :], ALU.mult))
            V.tensor_reduce(SM[:, 0:2], prod, AX, ALU.add).then_inc(E["lam_sums"], 1)
            got("lam_exps")
            link(V.tensor_tensor(SM[:, 4:5], SM[:, 3:4], SM[:, 2:3], ALU.subtract))
            link(V.tensor_scalar(SM[:, 5:6], SM[:, 4:5], -LAM_INIT, None, ALU.add))
            neg_lam = SM[:, 5:6]

            def ada_read(n):
                l, tiles = n // ADA_STEPS, ADA_W // P
                m0 = n % ADA_STEPS * tiles
                got("ada_done")
                V.tensor_tensor(MOD[:, l, m0:m0 + tiles, :], B[7][:, 0:2 * tiles].rearrange("p (m v) -> p m v", v=2),
                                bc(ADB[:, l, m0:m0 + tiles], 2, [P, tiles, 2]), ALU.add).then_inc(E["mod_read"], 1)

            def ada_end(l):
                ada_read((l + 1) * ADA_STEPS - 1)
                ve.wait_ge(E["mod_read"], ADA_STEPS * (l + 1))
                for k in (1, 4, 7):
                    m = MOD[:, l, k * KT:(k + 1) * KT, :]
                    ins = V.tensor_scalar(m, m, 1.0, None, ALU.add)
                for k in (2, 8):
                    m = MOD[:, l, k * KT:(k + 1) * KT, :]
                    ins = V.tensor_scalar(m, m, 0.5, None, ALU.mult)
                link(ins)

            prep()

            def norm_first(hf, gain):
                rstd(R[0][:, :S])
                for k in range(KT):
                    link(V.scalar_tensor_tensor(hf[:, k, :], XC[:, k, 0:S], PT[:, gain + k:gain + k + 1], R[0][:, :S],
                                                ALU.mult, ALU.mult))
                    split(hH[:, k, 0:S], hL[:, k, 0:S], hf[:, k, :], "h_ready")

            norm_first(HF1, N1)

            for c in range(12):
                prep()
                t.use()
                if 1 <= c <= 8:
                    r = R[(c - 1) % 2][:]
                    rstd(r)
                    gain = GQ[:, 0:1] if c - 1 < 4 else PT[:, KN:KN + 1]
                    V.scalar_tensor_tensor(pair(QK, c - 1), pair(QK, c - 1), gain, r, ALU.mult, ALU.mult)\
                        .then_inc(E["qk_ready"], 1)
                if c in ADA_CHUNKS[1:]:
                    ada_read(c - ADA_CHUNKS[1])

            ss = SM[:, 8:24].rearrange("p (b g) -> p b g", b=TB)
            for h in range(HEADS):
                sc = SC[h % 2]
                got("scores_done")
                for i in range(TB):
                    nk = P * (i + 1)
                    col = 8 * (h % 2) + 4 * i
                    mx, nm = SM3[:, col:col + 2], SM3[:, col + 2:col + 4]
                    for c in range(2):
                        V.scalar_tensor_tensor(sc[i][:, c, :], ND[:, i, 0:nk], 2.0 ** -(h + 1), B[c][:, P * i:P * i + nk],
                                               ALU.mult, ALU.add).then_inc(E["sc_read"], 1)
                        t.next("sc_read")
                    ve.wait_ge(E["sc_read"], t.at("sc_read"))
                    link(V.tensor_reduce(mx, sc[i], AX, ALU.max))
                    V.tensor_scalar(nm, mx, -1.0, None, ALU.mult).then_inc(E["max_ready"], 1)
                prep()
                ada_read(ada_at[h] - 1)
                for i in range(TB):
                    col = 8 * (h % 2) + 4 * i
                    rs, ri = SM2[:, col:col + 2], SM2[:, col + 2:col + 4]
                    got("exp_ready")
                    link(V.reciprocal(ri, rs))
                    link(V.tensor_tensor(ri[:, 1:2], ri[:, 1:2], neg_lam, ALU.mult))
                    link(V.tensor_scalar(sc[i][:, 0, :], sc[i][:, 0, :], ri[:, 0:1], None, ALU.mult))
                    V.scalar_tensor_tensor(sc[i][:, 0, :], sc[i][:, 1, :], ri[:, 1:2], sc[i][:, 0, :],
                                           ALU.mult, ALU.add).then_inc(E["prob_ready"], 1)
                for n in range(ada_at[h], ada_at[h + 1] - 1):
                    ada_read(n)
                if h < 4:
                    t.use()
                    got("va_copied")
                    va = VA[:, :, 256 * h:256 * (h + 1)]
                    sq = T[2][:].rearrange("p (b n) -> p b n", b=TB)
                    link(V.tensor_tensor(sq, va, va, ALU.mult))
                    for b in range(TB):
                        ins = V.tensor_reduce(ss[:, b, 2 * h:2 * h + 2],
                                              sq[:, b, :].rearrange("p (g n) -> p g n", g=2), AX, ALU.add)
                    if h < 3:
                        link(ins)
                    else:
                        link(ins)
                        link(V.tensor_scalar(SM[:, 8:24], SM[:, 8:24], 1.0 / P, EPS, ALU.mult, ALU.add))
                        V.tensor_copy(R[0][:, 0:16], SM[:, 8:24]).then_inc(E["var_ready"], 1)
                        got("std_ready")
                        link(V.reciprocal(R[0][:, 0:16], R[0][:, 0:16]))
                        for b in range(TB):
                            v = VA[:, b, :].rearrange("p (g n) -> p g n", g=KT)
                            ins = V.tensor_tensor(v, v, bc(R[0][:, KT * b:KT * b + KT], 2, [P, KT, P]), ALU.mult)
                        ins.then_inc(E["va_ready"], 1)
                        for g in range(KT):
                            if g % 2 == 0:
                                got("z_done")
                            ins = V.scalar_tensor_tensor(
                                ZB[:, g, :].rearrange("p (b n) -> p b n", b=TB),
                                bank2(6 + g // 2 % 2)[:, g % 2, :].rearrange("p (b n) -> p b n", b=TB),
                                PT[:, VG + g:VG + g + 1], bc(BSB[:, g, :], 1, [P, TB, P]), ALU.mult, ALU.add)
                            if g % 2:
                                ins.then_inc(E["zb_ready"], 1)
                        ve.wait_ge(E["zb_ready"], KT // 2)
                else:
                    j = h - 4
                    products()
                    V.tensor_tensor(T[2][:], B[4 + h % 2][:], pair(ZB, j), ALU.mult).then_inc(E["ya_ready"], 1)
                    ve.wait_ge(E["ya_ready"], 2 * j + 1)
                    split(pair(YAH, j), pair(YAL, j), T[2][:], "ya_ready")

            ada_end(0)
            for j in range(4):
                rstd(R[j % 2][:])
                link(V.scalar_tensor_tensor(T[2 + j % 2][:], pair(QK, j), GQ[:, 1:2], R[j % 2][:], ALU.mult, ALU.mult))
                split(pair(YBH, j), pair(YBL, j), T[2 + j % 2][:], "yb_ready")
                if j in (0, 2):
                    prep()

            for j in range(4):
                b = 4 * (j % 2)
                for _ in range(2):
                    if j > 0:
                        prep()
                    t.use()
                gates = [T[2 * (j % 2)], T[2 * (j % 2) + 1]]
                for n in range(2):
                    prep()
                    products()
                    got("gate_ready")
                    V.tensor_tensor(T[4 + n][:], B[b + 2 + n][:], gates[n][:], ALU.mult).then_inc(E["up_read"], 1)
                ve.wait_ge(E["up_read"], 2 * (j + 1))
                link(V.tensor_tensor(T[4][:], T[4][:], T[5][:], ALU.add))
                split(pair(MH, j), pair(ML, j), T[4][:], "merged_ready")

            for j in range(4):
                prep()
                products()
                x = XC[:, 2 * j:2 * j + 2, 0:S]
                V.tensor_tensor(x, x, bank2(j), ALU.add).then_inc(E["x_ready"], 1)

            norm_first(HF2, N2)
            got("logits_done")
            NR = N_GROUPS + N_EXPERTS

            def rt(i, *dims):
                n = 1
                for d in dims:
                    n *= d
                x = RT[:, i, 0:TB * n].rearrange("p (b n) -> p b n", b=TB)
                return x.rearrange("p b (g j) -> p b g j", g=dims[0]) if len(dims) == 2 else x

            def last(x, n):
                return x.to_broadcast([P, TB, n])

            logits = rt(0, NR)
            V.tensor_tensor(logits, B[1][:, 0:TB * NR].rearrange("p (b n) -> p b n", b=TB), bc(BR[:], 1, [P, TB, NR]),
                            ALU.add).then_inc(E["logits_read"], 1)
            ve.wait_ge(E["logits_read"], 1)
            gl = logits[:, :, 0:N_GROUPS]
            el = logits[:, :, N_GROUPS:].rearrange("p b (g j) -> p b g j", g=N_GROUPS)
            m, s4, gate, kmax = (SM2[:, 8 + 2 * i:10 + 2 * i].unsqueeze(2) for i in range(4))

            def first_max(x, is_max, n, desc, key):
                link(V.tensor_tensor(key, is_max, bc(desc, 1, [P, TB, n]), ALU.mult))
                link(V.tensor_reduce(kmax, key, AX, ALU.max))
                link(V.tensor_tensor(x, key, last(kmax, n), ALU.is_equal))

            d4, e4, oh4, key4 = rt(1, 4), rt(2, 4), rt(3, 4), rt(4, 4)
            link(V.tensor_reduce(m, gl, AX, ALU.max))
            V.tensor_tensor(d4, gl, last(m, 4), ALU.subtract).then_inc(E["top_ready"], 1)
            ve.wait_ge(E["top_ready"], 1)
            link(V.tensor_scalar(key4, d4, 0.0, None, ALU.is_ge))
            first_max(oh4, key4, 4, DESC[:, 0:N_GROUPS], key4)
            got("exp4_ready")
            link(V.tensor_reduce(s4, e4, AX, ALU.add))
            link(V.reciprocal(gate, s4))
            sel, e8 = rt(5, 4, 8), rt(6, 8)
            link(V.tensor_tensor(sel, el, oh4.unsqueeze(3).to_broadcast([P, TB, 4, 8]), ALU.mult))
            link(V.tensor_reduce(e8, sel.rearrange("p b g j -> p b j g"), AX, ALU.add))
            d8, key8, oh1, oh2, rest = rt(7, 8), rt(8, 8), rt(9, 8), rt(10, 8), rt(11, 8)
            link(V.tensor_reduce(m, e8, AX, ALU.max))
            link(V.tensor_tensor(d8, e8, last(m, 8), ALU.subtract))
            link(V.tensor_scalar(key8, d8, 0.0, None, ALU.is_ge))
            first_max(oh1, key8, 8, DESC[:, N_GROUPS:], key8)
            link(V.scalar_tensor_tensor(rest, oh1, -BIG, d8, ALU.mult, ALU.add))
            V.tensor_reduce(m, rest, AX, ALU.max).then_inc(E["m2_ready"], 1)
            ve.wait_ge(E["m2_ready"], 1)
            link(V.tensor_tensor(key8, rest, last(m, 8), ALU.is_equal))
            first_max(oh2, key8, 8, DESC[:, N_GROUPS:], key8)
            e2, w1_, w2_ = (SM2[:, 16 + 2 * i:18 + 2 * i].unsqueeze(2) for i in range(3))
            got("exp2_ready")
            link(V.tensor_scalar(s4, e2, 1.0, None, ALU.add))
            link(V.reciprocal(s4, s4))
            link(V.tensor_tensor(w1_, s4, gate, ALU.mult))
            link(V.tensor_tensor(w2_, w1_, e2, ALU.mult))
            link(V.tensor_tensor(oh1, oh1, last(w1_, 8), ALU.mult))
            link(V.tensor_tensor(oh2, oh2, last(w2_, 8), ALU.mult))
            link(V.tensor_tensor(oh1, oh1, oh2, ALU.add))
            for b in range(TB):
                ins = V.tensor_tensor(sel[:, b], bc(oh1[:, b, :], 1, [P, 4, 8]), bc(oh4[:, b, :], 2, [P, 4, 8]), ALU.mult)
            ins.then_inc(E["comb_ready"], 1)
            got("combT_done")
            V.tensor_copy(CT[:], B[2][0:N_EXPERTS, 0:S]).then_inc(E["combT_ready"], 1)

            cb = CB[:].rearrange("p (i e) n -> p i e n", e=4)
            with t.loop(N_EXPERTS // 4, {**ring_counts(t.used, 12, "used", "fill", "split"), "silu_ready": 4, "gated": 4,
                                         "vec_step": 8}) as i:
                for which, e in MOE_ORDER:
                    prep()
                    if which != "w3":
                        t.use()
                        continue
                    products()
                    got("silu_ready")
                    V.tensor_tensor(T[2 + e % 2][:], B[2 * (e % 2) + 1][:], T[e % 2][:], ALU.mult).then_inc(E["gated"], 1)
                    got("gated")
                    x = T[2 + e % 2][:].rearrange("p (f n) -> p f n", f=2)
                    ve.wait_ge(E["comb_loaded"], 16)
                    for f in range(2):
                        ins = V.tensor_tensor(x[:, f, :], x[:, f, :], cb[:, i, e, :], ALU.mult)
                    link(ins)
                    split(HIDH[e % 2][:], HIDL[e % 2][:], x, "hid_ready")
            got("acc_done")
            for j in range(4):
                x = XC[:, 2 * j:2 * j + 2, 0:S]
                V.tensor_tensor(x, x, bank2(4 + j), ALU.add).then_inc(E["x_ready"], 1)

            def norm(n):
                got("std_ready")
                V.reciprocal(R[0][:, :n], R[0][:, :n]).then_inc(E["r_ready"], 1)
                got("r_ready")
                for k in range(KT):
                    if k == 0:
                        for m in (0, 2):
                            V.tensor_tensor(HF[:, m, :n], XC[:, m, :n], R[0][:, :n], ALU.mult).then_inc(E["xn_ready"], 1)
                    elif k % 2 == 0 and k + 2 < KT:
                        V.tensor_tensor(HF[:, k + 2, :n], XC[:, k + 2, :n], R[0][:, :n], ALU.mult)\
                            .then_inc(E["xn_ready"], 1)
                    got("hf_ready")
                    split(hH[:, k, :n], hL[:, k, :n], HF[:, k, :n], "h_ready")

            def residual(l, gate, m, b, n):
                for v in range(n // S):
                    x = XC[:, m, v * S:(v + 1) * S]
                    ins = V.scalar_tensor_tensor(x, B[b][:, v * S:(v + 1) * S], MOD[:, l, gate * KT + m, v:v + 1], x,
                                                 ALU.mult, ALU.add)
                ins.then_inc(E["x_ready"], 1)

            def ffn(l, gate, n, lead):
                counts = {**ring_counts(t.used, FT_HALF + KT, "used", "fill", "split"), "silu_ready": FT_HALF,
                          "gated": FT_HALF, "vec_step": FT_HALF}
                with t.loop(2, counts):
                    if not lead:
                        prep()
                    for j in range(FT_HALF):
                        prep(CHUNK if j + 1 < FT_HALF else FT_HALF * P)
                        products()
                        got("silu_ready")
                        V.tensor_tensor(T[2 + j % 2][:, :n], B[2 * (j % 2) + 1][:, :n], T[j % 2][:, :n], ALU.mult)\
                            .then_inc(E["gated"], 1)
                        got("gated")
                        split(aH[:, j, :n], aL[:, j, :n], T[2 + j % 2][:, :n], "hid_ready")
                    for m in range(KT):
                        if m + 1 < KT:
                            prep(FT_HALF * P)
                        else:
                            t.pos += 1
                            if lead:
                                prep()
                        products()
                        residual(l, gate, m, 4 + m % 4, n)
                    t.used += 1

            def mix_split(x, m, p0, np_, c0, n):
                got("mix_hi")
                V.tensor_tensor(XL[p0:p0 + np_, m, c0:c0 + n], x, XH[p0:p0 + np_, m, c0:c0 + n].bitcast(F32),
                                ALU.subtract).then_inc(E["mix_ready"], 1)

            def mixers(l):
                n = 2 * S if l + 1 < LAYERS else S
                for c in range(5):
                    prep()
                    t.use()
                if l == 0:
                    ve.wait_ge(E["mix_consts_loaded"], dma_total["mix"])
                step = ADA_STEPS * (l + 1) - 1
                for i in range(6):
                    if l + 1 < LAYERS and 1 <= i <= 4:
                        for _ in range(2):
                            if step >= ADA_STEPS * (l + 1):
                                ada_read(step)
                            step += 1
                    if 1 <= i <= 2:
                        p = i - 1
                        got("mix_hi")
                        V.scalar_tensor_tensor(XL[:, 4 + p, :n], B[1][:, :n], PT[:, PS + 2 * l + p:PS + 2 * l + p + 1],
                                               XH[:, 4 + p, :n].bitcast(F32), ALU.mult, ALU.subtract)\
                            .then_inc(E["mix_ready"], 1)
                    elif i == 5:
                        for d in range(2):
                            mix_split(B[2 + d][:, :n], 6 + d, 0, P, 0, n)
                    if i < 5:
                        w = n if i < 4 else 2 * S
                        rstd(R[i % 2][:, :w])
                        gain = PT[:, QG2 + l:QG2 + l + 1] if i < 4 else PT[:, KG2 + l:KG2 + l + 1]
                        V.scalar_tensor_tensor(QQ[:, i, :w], QQ[:, i, :w], gain, R[i % 2][:, :w], ALU.mult, ALU.mult)\
                            .then_inc(E["qn_ready"], 1)
                        t.next("qn_ready")
                    if i >= 1:
                        x = QQ[:, i - 1, 0:S]
                        got("rot_done")
                        c, s = T[i % 2][:, 0:S], T[i % 2][:, S:2 * S]
                        V.tensor_tensor(c, x, TRIG[:, 0, :], ALU.mult)
                        link(V.tensor_tensor(s, B[4 + (i - 1) % 2][:, :S], TRIG[:, 1, :], ALU.mult))
                        V.tensor_tensor(x, c, s, ALU.add).then_inc(E["q_ready"], 1)
                units = attention_units(l)
                for u in range(len(units) + 3):
                    if u < len(units):
                        h, q0, k0, nk = units[u]
                        i = u % 3
                        got("scores_done")
                        mx, nm = SM[:, 8 + i:9 + i], SM[:, 11 + i:12 + i]
                        link(V.tensor_reduce(mx, B[SCORE_BANKS[i]][:, :nk], AX, ALU.max))
                        V.tensor_scalar(nm, mx, -(HD ** -0.5), None, ALU.mult).then_inc(E["max_ready"], 1)
                    if 1 <= u <= len(units):
                        h, q0, k0, nk = units[u - 1]
                        i = (u - 1) % 3
                        rs, ri = SM2[:, i:i + 1], SM2[:, 3 + i:4 + i]
                        got("exp_ready")
                        link(V.reciprocal(ri, rs))
                        e = PROBS[i][:, :nk]
                        V.tensor_scalar(e, e, ri, None, ALU.mult).then_inc(E["prob_ready"], 1)
                    if u >= 3:
                        h, q0, k0, nk = units[u - 3]
                        p0 = HD * (h % 2)
                        mix_split(B[4][p0:p0 + HD, 0:P], h // 2, p0, HD, q0, P)
                    if ada_beside(l, u) is not None:
                        ada_read(ada_beside(l, u) - 1)
                if l + 1 < LAYERS:
                    ada_end(l + 1)
                for j in range(4):
                    if j < 3 or l + 1 < LAYERS:
                        prep()
                    products()
                    for m in (2 * j, 2 * j + 1):
                        residual(l, 5, m, m, n)

            for l in range(LAYERS):
                n = 2 * S if l + 1 < LAYERS else S
                norm(2 * S)
                ffn(l, 2, 2 * S, True)
                norm(2 * S)
                mixers(l)
                norm(n)
                ffn(l, 8, n, l + 1 < LAYERS)

            rstd(R[0][:, :S])
            for k in range(KT):
                ins = V.scalar_tensor_tensor(HF[:, k, :S], XC[:, k, :S], PT[:, FG + k:FG + k + 1], R[0][:, :S],
                                             ALU.mult, ALU.mult)
                ins.then_inc(E["hf_done"], 1)

        @block.scalar
        def _(act):
            t = Tally(act)
            A = nc.scalar

            def got(name):
                act.wait_ge(E[name], t.next(name))

            def products():
                s, n = t.use()
                act.wait_ge(slot_used[s], n)

            def prep(words=CHUNK):
                s = t.take()
                before = (s + HI_SLOTS) % RAW_SLOTS
                act.wait_ge(raw_loaded[s], t.at(f"fill{s}") * 32)
                if t.n[f"fill{before}"]:
                    act.wait_ge(slot_used[before], t.at(f"fill{before}"))
                A.activation(HI[s % HI_SLOTS][:, :words], RAW[s][:, :words], ACT.Copy).then_inc(hi_done[s], 1)

            def root(mean, r):
                got("stats_done")
                A.activation(r, mean, ACT.Sqrt, bias=EPSC[:]).then_inc(E["std_ready"], 1)

            def squares(fresh):
                for k in range(KT):
                    fresh(k)
                    if k >= 2:
                        got("sq_used")
                    A.activation(SQ[k % 2][:, :S], XC[:, k, :S], ACT.Square).then_inc(E["sq_ready"], 1)

            def last_square(n, residuals):
                t.n["x_ready"] += residuals
                act.wait_ge(E["x_ready"], t.n["x_ready"])
                A.activation(SQ[1][:, :n], XC[:, KT - 1, :n], ACT.Square).then_inc(E["sq_ready"], 1)
                root(B[0][:, :n], R[0][:, :n])

            for j in range(8):
                got("x_done")
                v, c = j // 4, j % 4
                A.activation(XC[:, 2 * c:2 * c + 2, v * S:(v + 1) * S], bank2((j + 1) % 8), ACT.Copy)\
                    .then_inc(E["x_copied"], 1)
            got("params_ready")
            for v in range(2):
                A.activation(CS[:, :, v], PT[:, CV + v * KT:CV + (v + 1) * KT], ACT.Silu).then_inc(E["cs_ready"], 1)
            for i in range(2):
                got("ws_done")
                A.activation(WST[:, 4 * i:4 * i + 4, :].rearrange("p g t -> p (g t)"), B[1 + i][:], ACT.Copy)\
                    .then_inc(E["wst_ready"], 1)
            got("lam_sums")
            A.activation(SM[:, 2:4], SM[:, 0:2], ACT.Exp).then_inc(E["lam_exps"], 1)

            prep()

            def ada_copy(n):
                act.wait_ge(ada_used[2 * (n % 2) + 1], n // 2 + 1)
                A.activation(ADT[n // ADA_STEPS][:], B[6][:], ACT.Copy).then_inc(E["ada_copied"], 1)

            def from_start(k):
                act.wait_ge(E["x_copied"], 8)
            squares(from_start)
            root(B[0][:, :S], R[0][:, :S])
            for c in range(12):
                prep()
                products()
                if c < 8:
                    A.activation(pair(QK, c), B[4 + c % 2][:], ACT.Copy)
                    A.activation(SQ[c % 2][:], B[4 + c % 2][:], ACT.Square).then_inc(E["sq_ready"], 1)
                else:
                    A.activation(VB[:, :, 256 * (c - 8):256 * (c - 7)], bank2(4 + c % 2), ACT.Copy).then_inc(E["vb_ready"], 1)
                if c in ADA_CHUNKS:
                    ada_copy(c - ADA_CHUNKS[0])
                if 1 <= c <= 8:
                    if c >= 3:
                        act.wait_ge(E["qk_ready"], c - 2)
                    root(B[2 + (c - 1) % 2][:], R[(c - 1) % 2][:])

            def head_probs(h):
                got("probT_done")
                A.activation(T[3][:, 0:3 * P], B[2][:, 0:3 * P], ACT.Copy).then_inc(E["probT_ready"], 1)

            def head_out(h):
                got("pv_done")
                A.activation(QK[:, h, :], B[3][:, 0:S], ACT.Copy).then_inc(E["o_ready"], 1)

            for h in range(HEADS):
                if h >= 1:
                    head_probs(h - 1)
                for i in range(TB):
                    got("max_ready")
                    for c in range(2):
                        col = 8 * (h % 2) + 4 * i + c
                        ins = A.activation(SC[h % 2][i][:, c, :], SC[h % 2][i][:, c, :], ACT.Exp,
                                           bias=SM3[:, col + 2:col + 3], accum_out=SM2[:, col:col + 1])
                    ins.then_inc(E["exp_ready"], 1)
                steps = list(range(ada_at[h], ada_at[h + 1]))
                ada_copy(steps[0])
                if h >= 1:
                    head_out(h - 1)
                prep()
                if h < 4:
                    products()
                    A.activation(VA[:, :, 256 * h:256 * (h + 1)], bank2(4 + h % 2), ACT.Copy).then_inc(E["va_copied"], 1)
                else:
                    t.use()
                for n in steps[1:]:
                    ada_copy(n)
                if h == 3:
                    got("var_ready")
                    A.activation(R[0][:, 0:16], R[0][:, 0:16], ACT.Sqrt).then_inc(E["std_ready"], 1)
            head_probs(HEADS - 1)
            head_out(HEADS - 1)
            act.wait_ge(E["mod_read"], ADA_STEPS)
            act.wait_ge(E["o_ready"], HEADS)
            for j in range(4):
                A.activation(SQ[j % 2][:], pair(QK, j), ACT.Square).then_inc(E["sq_ready"], 1)
                if j >= 1:
                    if j >= 3:
                        act.wait_ge(E["yb_ready"], j - 2)
                    root(B[4 + j - 1][:], R[(j - 1) % 2][:])
                if j in (1, 3):
                    prep()
            act.wait_ge(E["yb_ready"], 2)
            root(B[7][:], R[1][:])

            for j in range(4):
                if j == 1:
                    act.wait_ge(E["yb_ready"], 4)
                if j >= 2:
                    act.wait_ge(E["up_read"], 2 * (j - 1))
                for n in range(2):
                    if j > 0:
                        prep()
                    products()
                    for m in range(2):
                        col = BG + KT * n + 2 * j + m
                        ins = A.activation(T[2 * (j % 2) + n][:, m * S:(m + 1) * S], bank2(4 * (j % 2) + n)[:, m, :],
                                           ACT.Sigmoid, bias=PT[:, col:col + 1])
                    ins.then_inc(E["gate_ready"], 1)
                for n in range(2):
                    prep()
                    t.use()
            for j in range(4):
                prep()
                t.use()

            def by_pair(k):
                if k % 2 == 0:
                    got("x_ready")

            last_square(S, KT // 2)

            def rt(i, n):
                return RT[:, i, 0:TB * n]
            got("top_ready")
            A.activation(rt(2, 4), rt(1, 4), ACT.Exp).then_inc(E["exp4_ready"], 1)
            got("m2_ready")
            A.activation(SM2[:, 16:18], SM2[:, 8:10], ACT.Exp).then_inc(E["exp2_ready"], 1)

            with t.loop(N_EXPERTS // 4, {**ring_counts(t.used, 12, "used", "fill"), "silu_ready": 0, "gated": 4}) as i:
                for which, e in MOE_ORDER:
                    prep()
                    if which != "w1":
                        t.use()
                        if which == "w3":
                            t.next("gated")
                        continue
                    products()
                    if e >= 2:
                        act.wait_ge(E["gated"], t.at("gated", 1))
                    else:
                        act.wait_ge(E["gated"], t.at("gated", e))
                    A.activation(T[e % 2][:], B[2 * (e % 2)][:], ACT.Silu).then_inc(E["silu_ready"], 1)

            def norm(l, shift, scale, n):
                for k in range(KT):
                    got("xp_ready" if k % 2 else "xn_ready")
                    for v in range(n // S):
                        h = HF[:, k, v * S:(v + 1) * S]
                        ins = A.activation(h, h, ACT.Identity, bias=MOD[:, l, shift * KT + k, v:v + 1],
                                           scale=MOD[:, l, scale * KT + k, v:v + 1])
                    ins.then_inc(E["hf_ready"], 1)

            def ffn(n, lead):
                counts = {**ring_counts(t.used, FT_HALF + KT, "used", "fill"), "gated": FT_HALF, "gate_done": FT_HALF}
                with t.loop(2, counts):
                    if not lead:
                        prep()
                    for j in range(FT_HALF):
                        prep(CHUNK if j + 1 < FT_HALF else FT_HALF * P)
                        got("gate_done")
                        act.wait_ge(E["gated"], t.at("gated", min(j, 1)))
                        A.activation(T[j % 2][:, :n], B[2 * (j % 2)][:, :n], ACT.Silu).then_inc(E["silu_ready"], 1)
                        t.next("gated")
                        t.use()
                    for m in range(KT):
                        if m + 1 < KT:
                            prep(FT_HALF * P)
                        else:
                            t.pos += 1
                            if lead:
                                prep()
                        t.use()
                    t.used += 1
                t.n["x_ready"] += KT

            def mix_high(x, m, p0, np_, c0, n, **scale):
                A.activation(XH[p0:p0 + np_, m, c0:c0 + n], x, ACT.Copy, **scale).then_inc(E["mix_hi"], 1)

            def mixers(l):
                n = 2 * S if l + 1 < LAYERS else S
                sets = n // S
                for c in range(5):
                    prep()
                    products()
                    if c < 2:
                        for i in (2 * c, 2 * c + 1):
                            A.activation(QQ[:, i, :n], B[i][:, :n], ACT.Copy).then_inc(E["q_copied"], 1)
                    elif c == 2:
                        A.activation(QQ[:, 4, :], B[4][:], ACT.Copy).then_inc(E["q_copied"], 1)
                        for kv in range(2):
                            src = B[5][:].rearrange("p (b n) -> p b n", b=4)[:, :, kv * HD:(kv + 1) * HD]
                            ins = A.activation(VD[:, :, kv], bc(src, 2, [P, 4, 2, HD]), ACT.Copy)
                        ins.then_inc(E["v_ready"], 1)
                    else:
                        for s in range(sets):
                            ins = A.activation(PF[:, 2 * s:2 * s + 2, c - 3, :], bank2([6, 0][c - 3] + s), ACT.Copy)
                            ins.then_inc(E["pf_ready"], 1)
                act.wait_ge(E["q_copied"], 5 * (l + 1))
                step = ADA_STEPS * (l + 1)
                for i in range(6):
                    if i < 5:
                        w = n if i < 4 else 2 * S
                        A.activation(SQ[i % 2][:, :w], QQ[:, i, :w], ACT.Square).then_inc(E["sq_ready"], 1)
                    if i >= 1:
                        w = n if i < 5 else 2 * S
                        if i >= 3:
                            act.wait_ge(E["qn_ready"], 5 * l + i - 2)
                        root(B[2 + (i - 1) % 2][:, :w], R[(i - 1) % 2][:, :w])
                    if 1 <= i <= 2:
                        p = i - 1
                        for s in range(sets):
                            got("pool_done")
                            for g in range(2):
                                rows = slice(HD * g, HD * (g + 1))
                                ins = A.activation(T[2 + p][rows, s * S:(s + 1) * S], bank2(0)[rows, g, :], ACT.Copy)
                            ins.then_inc(E["pm_ready"], 1)
                            if l + 1 < LAYERS:
                                ada_copy(step)
                                step += 1
                        got("pwb_done")
                        col = PS + 2 * l + p
                        mix_high(B[1][:, :n], 4 + p, 0, P, 0, n, scale=PT[:, col:col + 1])
                    elif 3 <= i <= 4:
                        p = i - 3
                        for s in range(sets):
                            got("fftab_done")
                            A.activation(AB[:], B[0][:], ACT.Copy).then_inc(E["ab_ready"], 1)
                            if l + 1 < LAYERS:
                                ada_copy(step)
                                step += 1
                            got("fft_done")
                            A.activation(T[2 + p][:, s * S:(s + 1) * S], B[1][:, :S], ACT.Copy).then_inc(E["ft_ready"], 1)
                    elif i == 5:
                        for d in range(2):
                            got("yf_done")
                            mix_high(B[2 + d][:, :n], 6 + d, 0, P, 0, n)
                for kv in range(2):
                    got("dup_done")
                    A.activation(KD[:, kv, :], B[4 + kv][:], ACT.Copy).then_inc(E["kd_ready"], 1)
                units = attention_units(l)
                for u in range(len(units) + 3):
                    if u < len(units):
                        h, q0, k0, nk = units[u]
                        i = u % 3
                        got("max_ready")
                        A.activation(PROBS[i][:, :nk], B[SCORE_BANKS[i]][:, :nk], ACT.Exp, bias=SM[:, 11 + i:12 + i],
                                     scale=HD ** -0.5, accum_out=SM2[:, i:i + 1]).then_inc(E["exp_ready"], 1)
                    if 2 <= u < len(units) + 2:
                        h, q0, k0, nk = units[u - 2]
                        got("probT_done")
                        A.activation(T[2 + u % 2][:, :nk], B[2 + u % 2][:, :nk], ACT.Copy).then_inc(E["probT_ready"], 1)
                    if u >= 3:
                        h, q0, k0, nk = units[u - 3]
                        p0 = HD * (h % 2)
                        got("pv_done")
                        mix_high(B[4][p0:p0 + HD, 0:P], h // 2, p0, HD, q0, P)
                    if ada_beside(l, u) is not None:
                        ada_copy(ada_beside(l, u))
                for j in range(4):
                    if j < 3 or l + 1 < LAYERS:
                        prep()
                    t.use()

            for l in range(LAYERS):
                n = 2 * S if l + 1 < LAYERS else S
                if l == 0:
                    squares(by_pair)
                    root(B[0][:], R[0][:])
                else:
                    last_square(2 * S, KT)
                norm(l, 0, 1, 2 * S)
                ffn(2 * S, True)
                last_square(2 * S, KT)
                norm(l, 3, 4, 2 * S)
                mixers(l)
                last_square(n, KT)
                norm(l, 6, 7, n)
                ffn(n, l + 1 < LAYERS)
            last_square(S, KT)

            for j in range(4):
                got("fin_done")
                b, half = j // 2, j % 2
                A.activation(OUTB[:, b, 512 * half:512 * (half + 1)], B[1 + j][:], ACT.Copy).then_inc(E["outb_ready"], 1)

        @block.tensor
        def _(pe):
            t = Tally(pe)
            mm = nc.tensor.matmul
            release = {}
            turn_start = {}

            def got(name):
                pe.wait_ge(E[name], t.next(name))

            def claim(b, reader, count=None):
                if b in release:
                    name, n = release[b]
                    pe.wait_ge(E[name], n)
                elif t.turn is not None:
                    pe.wait_ge(E[reader], turn_start[reader])
                release[b] = (reader, count or t.next(reader))

            @contextmanager
            def turns(n, counts, events):
                for name, v in release.values():
                    pe.wait_ge(E[name], v)
                release.clear()
                with t.loop(n, counts) as i:
                    for e in events:
                        turn_start[e] = t.at(e)
                    yield i
                for b, (name, _) in release.items():
                    release[b] = (name, t.n[name])

            def chunk():
                s = t.take()
                pe.wait_ge(lo_done[s], t.next(f"split{s}"))
                return s

            def used(ins, s):
                ins.then_inc(slot_used[s], 1)

            def exact(o, wh, wl, xh, xl, first=True, last=True, **more):
                mm(o, wh, xh, start=first, stop=False, **more)
                mm(o, wh, xl, start=False, stop=False, **more)
                return mm(o, wl, xh, start=False, stop=last, **more)

            def slot(s, **dims):
                v = "p (k n) -> p k n"
                return HI[s % HI_SLOTS][:].rearrange(v, **dims), LO[s][:].rearrange(v, **dims)

            def features(s, col, o, xh, xl, n, wait=None):
                wh, wl = slot(s, k=KT)
                for k in range(KT):
                    if wait:
                        wait(k)
                    ins = exact(o, wh[:, k, col:col + P], wl[:, k, col:col + P], xh[:, k, :n], xl[:, k, :n],
                                k == 0, k == KT - 1)
                return ins

            def tokens(s, block, o, col=0, w=256):
                wh, wl = slot(s, k=KT)
                rows = slice(P * block, P * (block + 1))
                for k in range(KT):
                    ins = exact(o, hH[:, k, rows], hL[:, k, rows], wh[:, k, col:col + w], wl[:, k, col:col + w],
                                k == 0, k == KT - 1)
                return ins

            def mean_of_squares():
                claim(0, "std_ready")
                for k in range(KT):
                    got("sq_ready")
                    ins = mm(B[0][:, :S], mat(MEAN_D), SQ[k % 2][:, :S], start=(k == 0), stop=(k == KT - 1))
                    if k < KT - 2:
                        ins.then_inc(E["sq_used"], 1)
                return ins

            def mean_of_sums(n):
                claim(0, "std_ready")
                got("acc_ready")
                mm(B[0][:, :n], mat(MEAN_D), ACC[:, :n], start=True, stop=False)
                got("sq_ready")
                mm(B[0][:, :n], mat(MEAN_D), SQ[1][:, :n], start=False, stop=True).then_inc(E["stats_done"], 1)

            def stats(m, i, b, n=512):
                claim(b, "std_ready")
                got("sq_ready")
                mm(B[b][:, :n], mat(m), SQ[i % 2][:, :n], start=True, stop=True).then_inc(E["stats_done"], 1)

            def wait_h(k):
                got("h_ready")

            pe.wait_ge(E["mats_loaded"], 16)
            pe.wait_ge(E["rows_loaded"], dma_total["rows"])
            claim(0, "params_ready")
            nc.tensor.transpose(B[0][:, 0:N_COLS], PA[:], mat(IDENT)[0:N_COLS, 0:N_COLS])
            for l in range(LAYERS):
                ins = nc.tensor.transpose(B[0][:, P + l * P:P + l * P + MODT], PB[:, l, :], mat(IDENT)[0:MODT, 0:MODT])
            ins.then_inc(E["params_done"], 1)
            pe.wait_ge(E["x_loaded"], 32)
            for j in range(8):
                v, c = j // 4, j % 4
                b = (j + 1) % 8
                claim(b, "x_copied")
                for m in range(2):
                    for blk in range(TB):
                        ins = nc.tensor.transpose(bank2(b)[:, m, blk * P:(blk + 1) * P],
                                                  XS[:, v, blk, (2 * c + m) * P:(2 * c + m + 1) * P], mat(IDENT))
                ins.then_inc(E["x_done"], 1)
            pe.wait_ge(E["ws_masked"], 1)
            for i in range(2):
                claim(1 + i, "wst_ready")
                for g in range(4):
                    ins = nc.tensor.transpose(B[1 + i][:, g * P:(g + 1) * P], WS[:, 4 * i + g, :], mat(IDENT))
                ins.then_inc(E["ws_done"], 1)

            def ada_finish(n):
                got("ada_copied")
                claim(7, "mod_read")
                for m in range(ADA_W // P):
                    ins = mm(B[7][:, 2 * m:2 * m + 2], ADT[n // ADA_STEPS][:, m * P:(m + 1) * P], ASEL[:],
                             start=True, stop=True)
                ins.then_inc(E["ada_done"], 1)

            def ada(n):
                if n % ADA_STEPS:
                    ada_finish(n - 1)
                claim(6, "ada_copied", n + 1)
                for half in range(2):
                    place = 2 * (n % 2) + half
                    pe.wait_ge(ada_loaded[place], 32 * (n // 2 + 1))
                    for j in range(COL_TILES):
                        ins = mm(bank2(6)[CT_W * j:CT_W * (j + 1)], CS[:, COL_TILES * half + j, :], ADW[n // ADA_STEPS][place][:, j],
                                 start=(half == 0), stop=(half == 1))
                    ins.then_inc(ada_used[place], 1)

            mean_of_squares().then_inc(E["stats_done"], 1)
            for c in range(12):
                s = chunk()
                b = 4 + c % 2
                if c < 8:
                    claim(b, "sq_ready", KT + c + 1)
                    for m in range(2):
                        ins = features(s, m * P, bank2(b)[:, m, :], hH, hL, S, wait_h if c == 0 and m == 0 else None)
                else:
                    claim(b, "vb_ready")
                    for blk in range(TB):
                        ins = tokens(s, blk, bank2(b)[:, blk, :])
                used(ins, s)
                if 1 <= c <= 8:
                    stats(MEAN_HD, c - 1, 2 + (c - 1) % 2)
                if c == ADA_CHUNKS[0]:
                    pe.wait_ge(E["cs_ready"], 2)
                    pe.wait_ge(E["misc_loaded"], dma_total["misc"])
                if c in ADA_CHUNKS:
                    ada(c - ADA_CHUNKS[0])

            pe.wait_ge(E["qk_ready"], 8)
            pe.wait_ge(E["vb_ready"], 4)
            def head_probs(h):
                claim(2, "probT_ready", h + 1)
                got("prob_ready")
                sc = SC[h % 2]
                nc.tensor.transpose(B[2][:, 0:P], sc[0][:, 0, :], mat(IDENT))
                got("prob_ready")
                nc.tensor.transpose(B[2][:, P:2 * P], sc[1][:, 0, 0:P], mat(IDENT))
                nc.tensor.transpose(B[2][:, 2 * P:3 * P], sc[1][:, 0, P:S], mat(IDENT)).then_inc(E["probT_done"], 1)

            def head_out(h):
                claim(3, "o_ready")
                got("probT_ready")
                v = VB[:, :, h * P:(h + 1) * P]
                pT = T[3]
                mm(B[3][:, 0:P], v[:, 0, :], pT[:, 0:P], start=True, stop=True)
                mm(B[3][:, P:S], v[:, 0, :], pT[:, P:2 * P], start=True, stop=False)
                mm(B[3][:, P:S], v[:, 1, :], pT[:, 2 * P:3 * P], start=False, stop=True).then_inc(E["pv_done"], 1)

            for h in range(HEADS):
                for i in range(TB):
                    nk = P * (i + 1)
                    for c in range(2):
                        rows = slice(HD * c, HD * (c + 1))
                        if i == 0:
                            claim(c, "sc_read", 2 * TB * (h + 1))
                        ins = mm(B[c][:, P * i:P * i + nk], QK[rows, h, i * P:(i + 1) * P], QK[rows, HEADS + h, 0:nk],
                                 start=True, stop=True)
                ins.then_inc(E["scores_done"], 1)
                if h >= 1:
                    head_probs(h - 1)
                steps = list(range(ada_at[h], ada_at[h + 1]))
                ada(steps[0])
                if h >= 1:
                    head_out(h - 1)
                s = chunk()
                b = 4 + h % 2
                if h < 4:
                    claim(b, "va_copied")
                    for blk in range(TB):
                        ins = tokens(s, blk, bank2(b)[:, blk, :])
                else:
                    claim(b, "ya_ready", 2 * (h - 4) + 1)
                    for m in range(2):
                        ins = features(s, m * P, bank2(b)[:, m, :], hH, hL, S)
                used(ins, s)
                for n in steps[1:]:
                    ada(n)
                if h == 3:
                    got("va_ready")
                    t.next("std_ready")
                    pe.wait_ge(E["wst_ready"], 2)
                    for g in range(KT):
                        if g % 2 == 0:
                            claim(6 + g // 2 % 2, "zb_ready")
                        for blk in range(TB):
                            ins = mm(bank2(6 + g // 2 % 2)[:, g % 2, blk * P:(blk + 1) * P], VA[:, blk, g * P:(g + 1) * P],
                                     WST[:, g, :], start=True, stop=True)
                        if g % 2:
                            ins.then_inc(E["z_done"], 1)
            head_probs(HEADS - 1)
            ada_finish(ADA_STEPS - 1)
            head_out(HEADS - 1)
            for j in range(4):
                stats(MEAN_P, j, 4 + j)

            for j in range(4):
                b = 4 * (j % 2)
                for n in range(4):
                    s = chunk()
                    claim(b + n, "gate_ready" if n < 2 else "up_read")
                    if j == 0 and n == 2:
                        pe.wait_ge(E["ya_ready"], 8)
                    if j == 0 and n == 3:
                        pe.wait_ge(E["yb_ready"], 4)
                    xh, xl = ((hH, hL), (hH, hL), (YAH, YAL), (YBH, YBL))[n]
                    for m in range(2):
                        ins = features(s, m * P, bank2(b + n)[:, m, :], xh, xl, S)
                    used(ins, s)
            pe.wait_ge(E["merged_ready"], 4)
            for j in range(4):
                s = chunk()
                claim(j, "x_ready")
                for m in range(2):
                    ins = features(s, m * P, bank2(j)[:, m, :], MH, ML, S)
                used(ins, s)

            mean_of_sums(S)
            for k in range(KT):
                got("h_ready")
            claim(1, "logits_read")
            NR = N_GROUPS + N_EXPERTS
            for blk in range(TB):
                for k in range(KT):
                    ins = mm(B[1][:, blk * NR:(blk + 1) * NR], HF2[:, k, blk * P:(blk + 1) * P], WR[:, k, :],
                             start=(k == 0), stop=(k == KT - 1))
            ins.then_inc(E["logits_done"], 1)
            got("comb_ready")
            claim(2, "combT_ready")
            comb = RT[:, 5, 0:TB * N_EXPERTS].rearrange("p (b e) -> p b e", b=TB)
            for blk in range(TB):
                ins = nc.tensor.transpose(B[2][0:N_EXPERTS, blk * P:(blk + 1) * P], comb[:, blk, :], mat(IDENT))
            ins.then_inc(E["combT_done"], 1)

            zeros = ZERO[:]
            pe.wait_ge(E["gated"], START["gated"])
            for b in range(4, 8):
                claim(b, "x_ready")
                mm(B[b][:], zeros[:, 0:P], zeros[:], start=True, stop=False, skip_group_check=True)
            acc_release = {b: release.pop(b) for b in range(4, 8)}
            counts = {**ring_counts(t.pos, 12, "fill", "split"), "silu_ready": 4, "gated": 4, "hid_ready": 4}
            with turns(N_EXPERTS // 4, counts, ["silu_ready", "gated"]):
                for which, e in MOE_ORDER:
                    s = chunk()
                    if which == "w2":
                        got("hid_ready")
                        wh, wl = slot(s, k=2)
                        for m in range(KT):
                            for f in range(2):
                                ins = exact(bank2(4 + m // 2)[:, m % 2, :], wh[:, f, m * P:(m + 1) * P],
                                            wl[:, f, m * P:(m + 1) * P], HIDH[e % 2][:, f, :], HIDL[e % 2][:, f, :],
                                            False, False, skip_group_check=True)
                    else:
                        b = 2 * (e % 2) + (which == "w3")
                        claim(b, "gated" if which == "w3" else "silu_ready")
                        for f in range(2):
                            ins = features(s, f * P, bank2(b)[:, f, :], hH, hL, S)
                    used(ins, s)
            for b in range(4, 8):
                ins = mm(B[b][:, 0:2], zeros[:, 0:P], zeros[:, 0:2], start=False, stop=True, skip_group_check=True)
            ins.then_inc(E["acc_done"], 1)
            release.update(acc_release)

            def ffn(n):
                counts = {**ring_counts(t.pos, FT_HALF + KT, "fill", "split"), "silu_ready": FT_HALF, "gated": FT_HALF,
                          "hid_ready": FT_HALF, "x_ready": KT}
                normed = t.n["h_ready"]
                t.n["h_ready"] += KT
                with turns(2, counts, ["silu_ready", "gated", "x_ready"]):
                    for j in range(FT_HALF):
                        s = chunk()
                        wh, wl = slot(s, k=2 * KT)
                        for which in range(2):
                            b = 2 * (j % 2) + which
                            claim(b, ("silu_ready", "gated")[which])
                            for k in range(KT):
                                if j == 0 and which == 0:
                                    pe.wait_ge(E["h_ready"], normed + k + 1)
                                ins = exact(B[b][:, :n], wh[:, which * KT + k, :], wl[:, which * KT + k, :], hH[:, k, :n],
                                            hL[:, k, :n], k == 0, k == KT - 1)
                            if which == 0:
                                ins.then_inc(E["gate_done"], 1)
                        used(ins, s)
                    for m in range(KT):
                        s = chunk()
                        b = 4 + m % 4
                        claim(b, "x_ready")
                        wh = HI[s % HI_SLOTS][:, :FT_HALF * P].rearrange("p (k n) -> p k n", n=P)
                        wl = LO[s][:, :FT_HALF * P].rearrange("p (k n) -> p k n", n=P)
                        for k in range(FT_HALF):
                            if m == 0:
                                got("hid_ready")
                            ins = exact(B[b][:, :n], wh[:, k, :], wl[:, k, :], aH[:, k, :n], aL[:, k, :n], k == 0,
                                        k == FT_HALF - 1)
                        used(ins, s)
                    t.pos += 1

            def mixers(l):
                n = 2 * S if l + 1 < LAYERS else S
                sets = n // S
                for c in range(5):
                    s = chunk()
                    if c < 2:
                        for m in range(2):
                            claim(2 * c + m, "q_copied")
                            ins = features(s, m * P, B[2 * c + m][:, :n], hH, hL, n, wait_h if c == 0 and m == 0 else None)
                    elif c == 2:
                        claim(4, "q_copied")
                        features(s, 0, B[4][:], hH, hL, 2 * S)
                        claim(5, "v_ready")
                        for blk in range(2 * TB):
                            ins = tokens(s, blk, B[5][:, blk * P:(blk + 1) * P], P, P)
                    else:
                        for blk in range(sets * TB):
                            b = [6, 0][c - 3] + blk // TB
                            if blk % TB == 0:
                                claim(b, "pf_ready")
                            ins = tokens(s, blk, bank2(b)[:, blk % TB, :])
                    used(ins, s)
                pe.wait_ge(E["pf_ready"], t.n["pf_ready"])
                if l == 0:
                    pe.wait_ge(E["mix_consts_loaded"], dma_total["mix"])
                step = ADA_STEPS * (l + 1)

                def pooled(p):
                    nonlocal step
                    for s in range(sets):
                        claim(0, "pm_ready")
                        for g in range(2):
                            for blk in range(TB):
                                ins = mm(bank2(0)[:, g, :], PF[:, 2 * s + blk, 0, p * P:(p + 1) * P], POOL[:, 2 * p + g, blk, :],
                                         start=(blk == 0), stop=(blk == TB - 1))
                        ins.then_inc(E["pool_done"], 1)
                        if l + 1 < LAYERS:
                            ada(step)
                            step += 1
                    pe.wait_ge(E["pm_ready"], t.n["pm_ready"])
                    claim(1, "mix_ready")
                    mm(B[1][:, :n], PWB[:, l, p, :], T[2 + p][:, :n], start=True, stop=True).then_inc(E["pwb_done"], 1)

                def fourier(p):
                    nonlocal step
                    for s in range(sets):
                        claim(0, "ab_ready")
                        for f in range(2):
                            for blk in range(TB):
                                ins = mm(bank2(0)[:, f, :], PF[:, 2 * s + blk, 1, p * P:(p + 1) * P], DFT[:, f, blk, :],
                                         start=(blk == 0), stop=(blk == TB - 1))
                        ins.then_inc(E["fftab_done"], 1)
                        if l + 1 < LAYERS:
                            ada(step)
                            step += 1
                        pe.wait_ge(E["ab_ready"], t.n["ab_ready"])
                        claim(1, "ft_ready")
                        mm(B[1][:, :S], mat(DFT_C), AB[:, 0:S], start=True, stop=False)
                        mm(B[1][:, :S], mat(DFT_S), AB[:, S:2 * S], start=False, stop=True).then_inc(E["fft_done"], 1)

                for i in range(6):
                    if i < 5:
                        stats(MEAN_HD, i, 2 + i % 2, n if i < 4 else 2 * S)
                    if 1 <= i <= 2:
                        pooled(i - 1)
                    elif 3 <= i <= 4:
                        fourier(i - 3)
                    elif i == 5:
                        pe.wait_ge(E["ft_ready"], t.n["ft_ready"])
                        for d in range(2):
                            claim(2 + d, "mix_ready")
                            for p in range(2):
                                ins = mm(B[2 + d][:, :n], FW[:, l, p, d * P:(d + 1) * P], T[2 + p][:, :n], start=(p == 0),
                                         stop=(p == 1))
                            ins.then_inc(E["yf_done"], 1)
                    if i >= 1:
                        got("qn_ready")
                        claim(4 + (i - 1) % 2, "q_ready")
                        mm(B[4 + (i - 1) % 2][:, :S], mat(ROT), QQ[:, i - 1, 0:S], start=True, stop=True)\
                            .then_inc(E["rot_done"], 1)
                pe.wait_ge(E["q_ready"], 5 * (l + 1))
                for kv in range(2):
                    claim(4 + kv, "kd_ready")
                    mm(B[4 + kv][:], mat(DUP0 + kv), QQ[:, 4, :], start=True, stop=True).then_inc(E["dup_done"], 1)
                pe.wait_ge(E["kd_ready"], t.n["kd_ready"])
                pe.wait_ge(E["v_ready"], l + 1)
                if l == 0:
                    t.n["exp_ready"] += HEADS * TB
                units = attention_units(l)
                before = t.n["probT_ready"]
                for u in range(len(units) + 3):
                    if u < len(units):
                        h, q0, k0, nk = units[u]
                        rows = slice(HD * (h % 2), HD * (h % 2) + HD)
                        b = SCORE_BANKS[u % 3]
                        claim(b, "exp_ready")
                        mm(B[b][:, :nk], QQ[rows, h // 2, q0:q0 + P], KD[rows, h // 4, k0:k0 + nk], start=True, stop=True)\
                            .then_inc(E["scores_done"], 1)
                    if 2 <= u < len(units) + 2:
                        h, q0, k0, nk = units[u - 2]
                        b = 2 + u % 2
                        claim(b, "probT_ready", before + u - 1)
                        got("prob_ready")
                        for kb in range(nk // P):
                            ins = nc.tensor.transpose(B[b][:, kb * P:(kb + 1) * P],
                                                      PROBS[(u - 2) % 3][:, kb * P:(kb + 1) * P], mat(IDENT))
                        ins.then_inc(E["probT_done"], 1)
                    if u >= 3:
                        h, q0, k0, nk = units[u - 3]
                        got("probT_ready")
                        claim(4, "mix_ready")
                        for kb in range(nk // P):
                            ins = mm(B[4][:, 0:P], VD[:, k0 // P + kb, h // 4, :, :].rearrange("p a d -> p (a d)"),
                                     T[2 + (u - 3) % 2][:, kb * P:(kb + 1) * P], start=(kb == 0), stop=(kb == nk // P - 1))
                        ins.then_inc(E["pv_done"], 1)
                    if ada_beside(l, u) is not None:
                        ada(ada_beside(l, u))
                if l + 1 < LAYERS:
                    ada_finish(ADA_STEPS * (l + 2) - 1)
                pe.wait_ge(E["mix_ready"], t.n["mix_ready"])
                for j in range(4):
                    s = chunk()
                    for m in (2 * j, 2 * j + 1):
                        claim(m, "x_ready")
                        ins = features(s, (m % 2) * P, B[m][:, :n], XH, XL, n)
                    used(ins, s)

            for l in range(LAYERS):
                n = 2 * S if l + 1 < LAYERS else S
                if l == 0:
                    mean_of_squares()
                    got("acc_ready")
                    mm(B[0][:, S:], mat(MEAN_D), ACC[:, S:], start=True, stop=True).then_inc(E["stats_done"], 1)
                else:
                    mean_of_sums(2 * S)
                ffn(2 * S)
                mean_of_sums(2 * S)
                mixers(l)
                mean_of_sums(n)
                ffn(n)

            mean_of_sums(S)
            pe.wait_ge(E["hf_done"], KT)
            for j in range(4):
                blk, half = j // 2, j % 2
                claim(1 + j, "outb_ready")
                for k in range(4):
                    ins = nc.tensor.transpose(B[1 + j][:, k * P:(k + 1) * P], HF[:, 4 * half + k, blk * P:(blk + 1) * P],
                                              mat(IDENT))
                ins.then_inc(E["fin_done"], 1)


INPUTS = ("x norm1_g w_in v_norm_g w_s b_s q_norm_g k_norm_g lambda_q1 lambda_k1 lambda_q2 lambda_k2 sub_norm_g w_up_a "
          "w_up_b w_gate b_gate w_out norm2_g w_rg b_rg w_re b_re w1 w3 w2 c_2 ctx_2 c_ctx_2 ada_w_2 ada_b_2 ffn1_w_gu_2 "
          "ffn1_w_down_2 w_in_2 q_gain_2 k_gain_2 pool_w_2 pool_scale_2 fft_w_2 w_out_2 ffn2_w_gu_2 ffn2_w_down_2 "
          "final_gain_2").split()


def constants():
    import numpy as np

    i = np.arange(P)
    mats = np.zeros((P, N_MATS, P))
    mats[:, IDENT] = np.eye(P)
    mats[:, MEAN_D] = 1.0 / D
    mats[:, MEAN_P] = 1.0 / P
    half = i // HD
    mats[:, MEAN_HD] = (half[:, None] == half[None, :]) / HD
    q = HD // 2
    for d in range(P):
        if d % HD < q:
            mats[d + q, ROT, d] = -1.0
        else:
            mats[d - q, ROT, d] = 1.0
    for kv in range(2):
        for d in range(P):
            mats[HD * kv + d % HD, DUP0 + kv, d] = 1.0
    group = (half[:, None] == half[None, :])
    angle = 2 * np.pi * np.outer(i % HD, i % HD) / HD
    norm = 1.0 / math.sqrt(S * HD)
    mats[:, DFT_C] = group * np.cos(angle) * norm
    mats[:, DFT_S] = group * -np.sin(angle) * norm
    s = np.arange(S)
    tok = 2 * np.pi * (np.outer(s, s) % S) / S
    dft = np.stack([np.cos(tok), np.sin(tok)]).reshape(2, TB, P, S).transpose(2, 0, 1, 3)
    pool = np.zeros((4, S, S))
    for g, w in enumerate((2, 4, 8, 16)):
        for to in range(S):
            lo, hi = max(to - w // 2, 0), min(to + w - w // 2, S)
            pool[g, lo:hi, to] = 1.0 / (hi - lo)
        pool[g] -= np.eye(S)
    pool = pool.reshape(4, TB, P, S).transpose(2, 0, 1, 3)
    n_freq = HD // 4
    inv = 10000.0 ** (-np.arange(n_freq) / n_freq)
    ang = np.concatenate([(s // 64)[:, None] * inv, (s % 64)[:, None] * inv], axis=1)
    trig = np.stack([np.cos(ang), np.sin(ang)])[:, :, i % q].transpose(2, 0, 1)
    dist = s[:, None] - s[None, :]
    neg = np.where(dist >= 0, -dist, -BIG).reshape(TB, P, S).transpose(1, 0, 2)
    falling = np.concatenate([np.arange(n, 0, -1) for n in (N_GROUPS, PER_GROUP)])
    select = np.zeros((P, 2))
    for v in range(2):
        select[v::CT_W, v] = 1.0
    tables = {"ada_select": select, "mats": mats, "dft": dft, "pool_mix": pool, "trig": trig, "neg_dist": neg, "descending": falling}
    return {k: np.ascontiguousarray(v, dtype=np.float32) for k, v in tables.items()}


def kernel(**inputs):
    import numpy as np
    import concourse.bacc as bacc
    from concourse.bass_utils import run_bass_kernel_spmd

    nc = bacc.Bacc("TRN2", target_bir_lowering=False, num_devices=1)
    given = {f"in_{n}": np.ascontiguousarray(inputs[n]) for n in INPUTS}
    given.update({f"in_{n}": v for n, v in constants().items()})
    handles = {n[3:]: nc.dram_tensor(n, v.shape, F32, kind="ExternalInput").ap() for n, v in given.items()}
    out = nc.dram_tensor("out", (1, S, D), F32, kind="ExternalOutput").ap()
    comb_rows = nc.dram_tensor("comb_rows", (N_EXPERTS, S), F32, kind="Internal").ap()
    build(nc, handles, out, comb_rows)
    got = run_bass_kernel_spmd(nc, [given], core_ids=[0])
    return got.results[0]["out"]
```

```python
import math
from collections import Counter
from contextlib import ExitStack, contextmanager

from concourse import mybir

F32 = mybir.dt.float32
F32R = mybir.dt.float32r
ACT = mybir.ActivationFunctionType
ALU = mybir.AluOpType
AX = mybir.AxisListType.X

P = 128
D = 1024
KT = D // P
S = 256
TB = S // P
EPS = 1e-6
HEADS = 8
LAM_INIT = 0.8 - 0.6
N_GROUPS, PER_GROUP = 4, 8
N_EXPERTS = N_GROUPS * PER_GROUP
LAYERS = 2
D_FF = ((8 * D // 3 + 127) // 128) * 128
FT_HALF = D_FF // P // 2
N_MOD = 9
MODT = N_MOD * KT
ADA_W = 512
ADA_STEPS = N_MOD * D // ADA_W
CT_W = 32
COL_TILES = P // CT_W
HD = 64
BIG = 1e30

RAW_SLOTS = 4
HI_SLOTS = 2
CHUNK = 2048

N1, N2, BG, VG, CV, PS, FG, SN, QN, KN, QG2, KG2, N_COLS = 0, 8, 16, 32, 40, 56, 60, 68, 69, 70, 71, 73, 75
IDENT, MEAN_D, MEAN_P, MEAN_HD, ROT, DUP0, DUP1, DFT_C, DFT_S, N_MATS = range(10)

MOE_ORDER = [("w1", 0), ("w3", 0), ("w1", 1), ("w3", 1), ("w2", 0), ("w1", 2), ("w3", 2), ("w2", 1),
             ("w1", 3), ("w3", 3), ("w2", 2), ("w2", 3)]

DOWN_CHUNKS = [(0, 0, 6), (0, 6, FT_HALF - 6)] + [(m, 0, FT_HALF) for m in range(1, KT)]
FFN_CHUNKS = [CHUNK] * FT_HALF + [ks * P for _, _, ks in DOWN_CHUNKS]
assert len(FFN_CHUNKS) % RAW_SLOTS == 0

START = {"gated": 1, "silu_ready": 1}


class Tally:

    def __init__(self, eng):
        self.eng, self.n, self.turn, self.per = eng, Counter(START), None, {}
        self.pos = self.used = 0

    def at(self, key, back=0):
        v = self.n[key] - back
        if self.turn is not None and self.per.get(key):
            v = self.turn * self.per[key] + v
        return v

    def next(self, key, by=1):
        self.n[key] += by
        return self.at(key)

    @contextmanager
    def loop(self, turns, per):
        before = Counter(self.n)
        with self.eng.Fori(0, turns) as i:
            self.turn, self.per = i, per
            yield i
        self.turn = None
        grown = {k: v - before[k] for k, v in self.n.items() if v != before[k]}
        assert grown == {k: v for k, v in per.items() if v}, (grown, per)
        for k, v in grown.items():
            self.n[k] += v * (turns - 1)

    def take(self):
        s = self.pos % RAW_SLOTS
        self.pos += 1
        self.next(f"fill{s}")
        return s

    def use(self):
        s = self.used % RAW_SLOTS
        self.used += 1
        return s, self.next(f"used{s}")


def ring_counts(pos, chunks, *kinds):
    out = Counter()
    for i in range(chunks):
        for kind in kinds:
            out[f"{kind}{(pos + i) % RAW_SLOTS}"] += 1
    return out


def build(nc, a, out, comb_rows):
    ctx = ExitStack()
    with ctx:
        def sem(name):
            return ctx.enter_context(nc.semaphore(name))

        base = 16512
        cursor = [base]

        def sb(name, shape, dt=F32):
            n = 4
            for d in shape[1:]:
                n *= d
            h = nc.alloc_sbuf_tensor_at(name, shape, dt, offset=cursor[0])
            cursor[0] += (n + 31) // 32 * 32
            return h

        XC = sb("XC", [P, KT, 2 * S])
        hH, hL = (sb(n, [P, KT, 2 * S], F32R) for n in ("hH", "hL"))
        raw_at = cursor[0]
        RAW = [sb(f"RAW{i}", [P, CHUNK]) for i in range(RAW_SLOTS)]
        LO = [nc.alloc_sbuf_tensor_at(f"LO{i}", [P, CHUNK], F32R, offset=raw_at + 4 * CHUNK * i)
              for i in range(RAW_SLOTS)]
        HI = [sb(f"HI{i}", [P, CHUNK], F32R) for i in range(HI_SLOTS)]
        T = [sb(f"T{i}", [P, 512]) for i in range(6)]
        SQ = T[4:6]
        ACC = T[4]
        R = [sb(f"R{i}", [P, 512]) for i in range(2)]
        MATS = sb("MATS", [P, N_MATS, P])
        WR = sb("WR", [P, KT, N_GROUPS + N_EXPERTS])
        BR = sb("BR", [P, N_GROUPS + N_EXPERTS])
        PT = sb("PT", [P, N_COLS])
        ADB = sb("ADB", [P, LAYERS, MODT])
        MOD = sb("MOD", [P, LAYERS, MODT, 2])
        CS = sb("CS", [P, KT, CT_W])
        ASEL = sb("ASEL", [P, 2])
        GQ = sb("GQ", [P, 2])
        ZERO = sb("ZERO", [P, 512])
        DESC = sb("DESC", [P, N_GROUPS + PER_GROUP])
        EPSC = sb("EPSC", [P, 1])
        SM, SM2 = sb("SM", [P, 32]), sb("SM2", [P, 32])
        SM3 = sb("SM3", [P, 16])
        union = cursor[0]

        def at(kb, name, shape, dt=F32):
            return nc.alloc_sbuf_tensor_at(name, shape, dt, offset=union + 1024 * kb)

        QK = at(0, "QK", [P, 2 * HEADS, S])
        MH, ML = at(0, "MH", [P, KT, S], F32R), at(8, "ML", [P, KT, S], F32R)
        VB = at(16, "VB", [P, TB, D])
        ZB = at(24, "ZB", [P, KT, S])
        VA = at(32, "VA", [P, TB, D])
        WST = at(40, "WST", [P, KT, P])
        BSB = at(44, "BSB", [P, KT, P])
        YAH, YAL = at(48, "YAH", [P, KT, S], F32R), at(56, "YAL", [P, KT, S], F32R)
        YBH, YBL = at(64, "YBH", [P, KT, S], F32R), at(72, "YBL", [P, KT, S], F32R)
        XS = at(48, "XS", [P, 2, TB, D])
        WS = at(64, "WS", [P, KT, P])
        PA = at(68, "PA", [N_COLS, P])
        PB = at(69, "PB", [MODT, LAYERS, P])
        HF1 = at(72, "HF1", [P, KT, S])
        ND = at(80, "ND", [P, TB, S])
        LV = at(82, "LV", [P, 4, HD])
        CB = at(0, "CB", [P, N_EXPERTS, S])
        HIDH = [at(32 + 4 * i, f"HIDH{i}", [P, 2, S], F32R) for i in range(2)]
        HIDL = [at(34 + 4 * i, f"HIDL{i}", [P, 2, S], F32R) for i in range(2)]
        HF2 = at(40, "HF2", [P, KT, S])
        RT = at(48, "RT", [P, 12, 2 * 36])
        CT = at(52, "CT", [N_EXPERTS, S])
        aH, aL = at(0, "aH", [P, FT_HALF, 2 * S], F32R), at(22, "aL", [P, FT_HALF, 2 * S], F32R)
        HF = at(45, "HF", [P, KT, 2 * S])
        OUTB = at(0, "OUTB", [P, TB, D])
        XH, XL = at(0, "XH", [P, KT, 2 * S], F32R), at(16, "XL", [P, KT, 2 * S], F32R)
        QQ = at(32, "QQ", [P, 5, 2 * S])
        KD = at(42, "KD", [P, 2, 2 * S])
        VD = at(46, "VD", [P, 2 * TB, 2, HD])
        AB = at(58, "AB", [P, 2 * S])
        PF = at(50, "PF", [P, 2 * TB, 2, S])
        POOL = at(61, "POOL", [P, 4, TB, S])
        DFT = at(69, "DFT", [P, 2, TB, S])
        TRIG = at(73, "TRIG", [P, 2, S])
        PWB = at(75, "PWB", [P, LAYERS, 2, P])
        FW = at(77, "FW", [P, LAYERS, 2, S])
        assert union + 1024 * 83 <= nc.sbuf_usable_end, (union + 1024 * 83 - nc.sbuf_usable_end)

        h_at = [base + 4 * KT * 2 * S * i for i in (1, 2)]
        HF32 = [nc.alloc_sbuf_tensor_at(f"HF32_{i}", [P, KT, 2 * S], F32, offset=h_at[i]) for i in range(2)]
        ADW = [[h[:, :, S:].rearrange("p (k b) n -> p k b n", b=2) for h in HF32],
               [h[:, k:k + 4, :].rearrange("p k (b n) -> p k b n", b=2) for h in HF32 for k in (0, 4)]]
        ADW[0] += [at(64 + 8 * i, f"ADW{i}", [P, 4, 2, S])[:] for i in range(2)]
        ADT1 = at(81, "ADT1", [P, ADA_W])

        def adt(n):
            return T[5] if len(ADA_CHUNKS) <= n < ADA_LATE else T[2] if n < ADA_STEPS else ADT1

        SC = [[T[0][:, 2 * P * i:2 * P * (i + 1)].rearrange("p (c n) -> p c n", c=2),
               T[(1, 4)[i]][:].rearrange("p (c n) -> p c n", c=2)] for i in range(2)]

        B = [ctx.enter_context(nc.psum_tensor(f"B{i}", [P, 512], F32)) for i in range(8)]

        raw_loaded = [sem(f"raw_loaded{i}") for i in range(RAW_SLOTS)]
        hi_done = [sem(f"hi_done{i}") for i in range(RAW_SLOTS)]
        lo_done = [sem(f"lo_done{i}") for i in range(RAW_SLOTS)]
        slot_used = [sem(f"slot_used{i}") for i in range(RAW_SLOTS)]
        ada_loaded = [sem(f"ada_loaded{i}") for i in range(4)]
        ada_used = [sem(f"ada_used{i}") for i in range(4)]
        names = (
            "x_loaded ctx_loaded rows_loaded ws_loaded mats_loaded misc_loaded mix_consts_loaded "
            "comb_stored comb_first comb_loaded out_stored "
            "params_done x_done ws_done sq_used stats_done z_done scores_done probT_done pv_done "
            "logits_done combT_done gate_done acc_done rot_done dup_done pool_done "
            "pwb_done fftab_done fft_done yf_done fin_done ada_done "
            "vec_step params_ready mod_read var_ready r_ready h_ready qk_ready vb_ready va_ready zb_ready ya_ready yb_ready "
            "lam_sums sc_read max_ready prob_ready up_read merged_ready logits_read top_ready m2_ready "
            "comb_ready combT_ready "
            "gated hid_ready x_ready xn_ready qn_ready q_ready mix_ready hf_done "
            "ada_copied cs_ready x_copied wst_ready sq_ready std_ready va_copied lam_exps exp_ready probT_ready "
            "o_ready gate_ready exp4_ready exp2_ready silu_ready hf_ready q_copied kd_ready v_ready pf_ready pm_ready "
            "ab_ready ft_ready mix_hi outb_ready "
            "pool_step ws_masked pwb_zero acc_ready xp_ready").split()
        E = {n: sem(n) for n in names}
        dma_total = Counter()

        def mat(i):
            return MATS[:, i, :]

        def bank2(b):
            return B[b][:].rearrange("p (a n) -> p a n", a=2)

        def pair(x, j):
            return x[:, 2 * j:2 * j + 2, :].rearrange("p a n -> p (a n)")

        def attention_pairs(l):
            pairs = [(h, P * i, 0, 2 * S) for h in range(0, 8, 2) for i in range(TB)]
            if l + 1 < LAYERS:
                pairs += [(h, S + P * i, S, S) for h in range(0, 8, 2) for i in range(TB)]
            return pairs

        MIX_BANKS = (0, 5)
        SCORE_BANKS, PROBS = (0, 1, 5), (T[0], T[1], T[4], T[5])
        ADA_CHUNKS = range(8, 12)
        ADA_LATE = len(ADA_CHUNKS) + HEADS
        assert ADA_LATE + 4 + 2 == ADA_STEPS
        MIX_STEPS = 4

        def ada_beside(l, u):
            if l + 1 < LAYERS:
                last, left = len(attention_pairs(l)) + 1, ADA_STEPS - MIX_STEPS
                return {k * last // (left - 1): (l + 1) * ADA_STEPS + MIX_STEPS + k for k in range(left)}.get(u)

        def flat(x):
            while len(x.shape) > 1:
                x = x.rearrange("a b c -> (a b) c") if len(x.shape) == 3 else x.rearrange("a b -> (a b)")
            return x

        vectors = [(flat(a[name]).rearrange("(r p) -> r p", p=P), PA[c0:c0 + k, :])
                   for name, c0, k in (("norm1_g", N1, 8), ("norm2_g", N2, 8), ("b_gate", BG, 16), ("v_norm_g", VG, 8),
                                       ("c_2", CV, 8), ("c_ctx_2", CV + 8, 8), ("pool_scale_2", PS, 4),
                                       ("final_gain_2", FG, 8), ("sub_norm_g", SN, 1))]
        vectors += [(a[name][:, :], PA[c0:c0 + a[name].shape[0], half * HD:(half + 1) * HD])
                    for name, c0 in (("q_norm_g", QN), ("k_norm_g", KN), ("q_gain_2", QG2), ("k_gain_2", KG2))
                    for half in range(2)]
        vectors.append((a["ada_b_2"].rearrange("l (r p) -> r l p", p=P), PB[:]))
        dma_total["rows"] = 16 * len(vectors)

        def bc(x, dim, shape):
            return x.unsqueeze(dim).to_broadcast(shape)

        block = ctx.enter_context(nc.Block())

        @block.sync
        def _(sp):
            t = Tally(sp)

            def chunk(first, second, words):
                s = t.take()
                if t.n[f"fill{s}"] > 1:
                    sp.wait_ge(slot_used[s], t.at(f"fill{s}", 1))
                h0 = words[0]
                sp.dma_start(RAW[s][:, 0:h0].rearrange("p (k n) -> p k n", n=first.shape[-1]), first)\
                    .then_inc(raw_loaded[s], 16)
                sp.dma_start(RAW[s][:, h0:h0 + words[1]].rearrange("p (k n) -> p k n", n=second.shape[-1]), second)\
                    .then_inc(raw_loaded[s], 16)

            def columns(w, c0):
                v = w.rearrange("(k p) n -> p k n", p=P)
                chunk(v[:, 0:4, c0:c0 + 256], v[:, 4:8, c0:c0 + 256], (1024, 1024))

            def ffn(l, gu, down):
                g = a[gu][l].rearrange("(k p) (t h n) -> p k t h n", p=P, t=2, h=2)
                w = a[down][l].rearrange("(h k p) n -> p h k n", p=P, h=2)
                with t.loop(2, ring_counts(t.pos, len(FFN_CHUNKS), "fill")) as half:
                    for j in range(FT_HALF):
                        chunk(g[:, :, 0, half, j * P:(j + 1) * P], g[:, :, 1, half, j * P:(j + 1) * P], (1024, 1024))
                    for m, k0, ks in DOWN_CHUNKS:
                        mid, to = k0 + (ks + 1) // 2, k0 + ks
                        chunk(w[:, half, k0:mid, m * P:(m + 1) * P], w[:, half, mid:to, m * P:(m + 1) * P],
                              ((mid - k0) * P, (to - mid) * P))

            x_v = a["x"][0].rearrange("(b p) d -> p b d", p=P)
            c_v = a["ctx_2"][0].rearrange("(b p) d -> p b d", p=P)
            sp.dma_start(XS[:, 0], x_v).then_inc(E["x_loaded"], 16)
            w_in = a["w_in"][0]
            for c in range(8):
                columns(w_in, 2 * D + 256 * c)
                if c == 0:
                    sp.wait_ge(E["rows_loaded"], dma_total["rows"])
                    sp.dma_start(XS[:, 1], c_v).then_inc(E["ctx_loaded"], 16)
                    sp.dma_start(WS[:], a["w_s"][0].rearrange("g t s -> t g s")).then_inc(E["ws_loaded"], 16)
            for c in range(4):
                columns(w_in, 4 * D + 256 * c)
            for c in range(4):
                columns(w_in, D + 256 * c)
            for c in range(4):
                columns(w_in, 256 * c)
            for c in range(4):
                columns(a["w_gate"][0], 256 * c)
                columns(a["w_gate"][0], D + 256 * c)
                columns(a["w_up_a"][0], 256 * c)
                columns(a["w_up_b"][0], 256 * c)
            for c in range(4):
                columns(a["w_out"][0], 256 * c)
            w1 = a["w1"][0].rearrange("e (k p) n -> p e k n", p=P)
            w3 = a["w3"][0].rearrange("e (k p) n -> p e k n", p=P)
            w2 = a["w2"][0].rearrange("e (k p) n -> p e k n", p=P)
            with t.loop(N_EXPERTS // 4, ring_counts(t.pos, 12, "fill")) as i:
                for which, e in MOE_ORDER:
                    if which == "w2":
                        chunk(w2[:, i * 4 + e, 0:1, :], w2[:, i * 4 + e, 1:2, :], (1024, 1024))
                    else:
                        v = w1 if which == "w1" else w3
                        chunk(v[:, i * 4 + e, 0:4, :], v[:, i * 4 + e, 4:8, :], (1024, 1024))
            for l in range(LAYERS):
                ffn(l, "ffn1_w_gu_2", "ffn1_w_down_2")
                for c in range(5):
                    columns(a["w_in_2"][l], 256 * c)
                for c in range(4):
                    columns(a["w_out_2"][l], 256 * c)
                ffn(l, "ffn2_w_gu_2", "ffn2_w_down_2")
            columns(w_in, 0)
            for j in range(4):
                half, blk = j // 2, j % 2
                cols = slice(half * D // 2, (half + 1) * D // 2)
                sp.wait_ge(E["outb_ready"], j + 1)
                sp.dma_start(out[0, blk * P:(blk + 1) * P, cols], OUTB[:, blk, cols]).then_inc(E["out_stored"], 16)
            sp.wait_ge(E["out_stored"], 64)

        @block.gpsimd
        def _(pool):
            t = Tally(pool)

            def link(ins):
                ins.then_inc(E["pool_step"], 1)
                pool.wait_ge(E["pool_step"], t.next("pool_step"))

            def squares(tiles, n, fresh, c0=0):
                for k in range(tiles):
                    fresh(k)
                    x = XC[:, k, c0:c0 + n]
                    acc, sq = ACC[:, c0:c0 + n], R[1][:, c0:c0 + n]
                    ins = nc.gpsimd.tensor_tensor(acc if k == 0 else sq, x, x, ALU.mult)
                    if k > 0:
                        link(ins)
                        ins = nc.gpsimd.tensor_tensor(acc, acc, sq, ALU.add)
                    if k < tiles - 1:
                        link(ins)
                ins.then_inc(E["acc_ready"], 1)

            def by_pair(k):
                if k % 2 == 0:
                    pool.wait_ge(E["x_ready"], t.next("x_ready"))

            def by_tile(k):
                pool.wait_ge(E["x_ready"], t.next("x_ready"))

            def normed(n):
                pool.wait_ge(E["r_ready"], t.next("r_ready"))
                for k in range(1, KT, 2):
                    nc.gpsimd.tensor_tensor(HF[:, k, :n], XC[:, k, :n], R[0][:, :n], ALU.mult).then_inc(E["xp_ready"], 1)

            def norm(n):
                squares(KT - 1, n, by_tile)
                t.next("x_ready")
                normed(n)

            def ada_weights(l, i0, i1, first, wait):
                v = a["ada_w_2"][l].rearrange("(h k p) (i b n) -> p h k i b n", p=P, h=2, b=2, n=S)

                def two_steps(i, fresh, wait):
                    for k in range(2):
                        if k and wait:
                            wait()
                        for half in range(2):
                            place = 2 * k + half
                            if not fresh:
                                pool.wait_ge(ada_used[place], t.next(f"ada_used{place}"))
                            for b in range(2):
                                pool.dma_start(ADW[l][place][:, :, b, :], v[:, half, :, i * 2 + k, b, :])\
                                    .then_inc(ada_loaded[place], 16)

                two_steps(i0, first, wait)
                if i1 - i0 > 1:
                    with t.loop(i1 - i0 - 1, {f"ada_used{place}": 1 for place in range(4)}) as i:
                        two_steps(i + (i0 + 1), False, None)

            def inputs_used():
                pool.wait_ge(E["ws_done"], 2)
                pool.wait_ge(E["h_ready"], KT)

            def yb_used():
                pool.wait_ge(E["merged_ready"], 4)

            for i, name in enumerate(("lambda_q1", "lambda_k1", "lambda_q2", "lambda_k2")):
                pool.dma_start(LV[:, i, :], a[name][0].partition_broadcast(P)).then_inc(E["misc_loaded"], 16)
            pool.dma_start(ND[:], a["neg_dist"]).then_inc(E["misc_loaded"], 16)
            pool.dma_start(BSB[:].rearrange("p g t -> p (g t)"), flat(a["b_s"]).partition_broadcast(P))\
                .then_inc(E["misc_loaded"], 16)
            pool.dma_start(BR[:, 0:N_GROUPS], a["b_rg"][0].partition_broadcast(P)).then_inc(E["misc_loaded"], 16)
            pool.dma_start(BR[:, N_GROUPS:], a["b_re"][0].partition_broadcast(P)).then_inc(E["misc_loaded"], 16)
            pool.dma_start(WR[:, :, 0:N_GROUPS], a["w_rg"][0].rearrange("(k p) n -> p k n", p=P))\
                .then_inc(E["misc_loaded"], 16)
            pool.dma_start(WR[:, :, N_GROUPS:], a["w_re"][0].rearrange("(k p) n -> p k n", p=P))\
                .then_inc(E["misc_loaded"], 16)
            pool.dma_start(DESC[:], a["descending"].partition_broadcast(P)).then_inc(E["misc_loaded"], 16)
            pool.dma_start(ASEL[:], a["ada_select"]).then_inc(E["misc_loaded"], 16)
            dma_total["misc"] = 16 * 12
            pool.wait_ge(E["ws_loaded"], 16)
            nc.gpsimd.affine_select(out=WS[:], in_=WS[:], compare_op=ALU.is_ge, fill=0.0, base=0,
                                    pattern=[[0, KT], [-1, P]], channel_multiplier=1).then_inc(E["ws_masked"], 1)
            ada_weights(0, 0, ADA_LATE // 2, True, inputs_used)
            ada_weights(0, ADA_LATE // 2, ADA_STEPS // 2 - 1, False, yb_used)
            squares(KT - 1, S, by_pair)
            ada_weights(0, ADA_STEPS // 2 - 1, ADA_STEPS // 2, False, None)
            pool.wait_ge(E["combT_ready"], 1)
            pool.dma_start(comb_rows, CT[:]).then_inc(E["comb_stored"], 16)
            pool.wait_ge(E["comb_stored"], 16)
            for e0, e1, done in ((0, 4, "comb_first"), (4, N_EXPERTS, "comb_loaded")):
                pool.dma_start(CB[:, e0:e1, :].rearrange("p e t -> p (e t)"),
                               comb_rows[e0:e1].rearrange("e t -> (e t)").partition_broadcast(P)).then_inc(E[done], 16)
            squares(KT, S, lambda k: None, S)
            for place in (2, 3):
                pool.wait_ge(ada_used[place], ADA_STEPS // 2)
            pool.dma_start(POOL[:], a["pool_mix"]).then_inc(E["mix_consts_loaded"], 16)
            pool.dma_start(DFT[:], a["dft"]).then_inc(E["mix_consts_loaded"], 16)
            pool.dma_start(TRIG[:], a["trig"]).then_inc(E["mix_consts_loaded"], 16)
            pool.dma_start(FW[:], a["fft_w_2"].rearrange("l (t p) n -> p l t n", p=P))\
                .then_inc(E["mix_consts_loaded"], 16)
            nc.gpsimd.memset(PWB[:], 0.0).then_inc(E["pwb_zero"], 1)
            pool.wait_ge(E["pwb_zero"], 1)
            for l in range(LAYERS):
                for g in range(4):
                    p0 = HD * (g % 2)
                    pool.dma_start(PWB[p0:p0 + HD, l, g // 2, p0:p0 + HD], a["pool_w_2"][l, g])\
                        .then_inc(E["mix_consts_loaded"], 16)
            dma_total["mix"] = 16 * (4 + 4 * LAYERS)
            t.n["x_ready"] += KT // 2
            normed(2 * S)
            for l in range(LAYERS):
                n = 2 * S if l + 1 < LAYERS else S
                t.n["x_ready"] += KT
                norm(2 * S)
                if l + 1 < LAYERS:
                    pool.wait_ge(E["pf_ready"], 4 * (l + 1))
                    ada_weights(l + 1, 0, ADA_STEPS // 2, False, None)
                norm(n)
                t.n["x_ready"] += KT
                if l + 1 < LAYERS:
                    norm(n)
            squares(KT - 1, S, by_tile)

        @block.vector
        def _(ve):
            t = Tally(ve)
            V = nc.vector

            def link(ins):
                ins.then_inc(E["vec_step"], 1)
                ve.wait_ge(E["vec_step"], t.next("vec_step"))

            def got(name):
                ve.wait_ge(E[name], t.next(name))

            def products():
                s, n = t.use()
                ve.wait_ge(slot_used[s], n)

            def prep(words=CHUNK):
                s = t.take()
                ve.wait_ge(hi_done[s], t.next(f"split{s}"))
                V.tensor_tensor(LO[s][:, :words], RAW[s][:, :words], HI[s % HI_SLOTS][:, :words].bitcast(F32),
                                ALU.subtract).then_inc(lo_done[s], 1)

            def split(hi, lo, x, done):
                link(V.tensor_copy(hi, x))
                V.tensor_tensor(lo, x, hi.bitcast(F32), ALU.subtract).then_inc(E[done], 1)

            def rstd(r):
                got("std_ready")
                link(V.reciprocal(r, r))

            V.memset(EPSC[:], EPS)
            V.memset(CS[:], 0.0).then_inc(E["silu_ready"], START["silu_ready"])
            V.memset(ZERO[:], 0.0).then_inc(E["gated"], START["gated"])
            got("params_done")
            V.tensor_copy(PT[:], B[0][:, 0:N_COLS])
            for l in range(LAYERS):
                ins = V.tensor_copy(ADB[:, l, :], B[0][:, P + l * P:P + l * P + MODT])
            link(ins)
            V.tensor_scalar(GQ[:, 0:1], PT[:, QN:QN + 1], HD ** -0.5, None, ALU.mult)
            V.tensor_scalar(GQ[:, 1:2], PT[:, SN:SN + 1], 1.0 - LAM_INIT, None, ALU.mult).then_inc(E["params_ready"], 1)
            def ada_read(n):
                l, tiles = n // ADA_STEPS, ADA_W // P
                m0 = n % ADA_STEPS * tiles
                got("ada_done")
                V.tensor_tensor(MOD[:, l, m0:m0 + tiles, :], B[7][:, 0:2 * tiles].rearrange("p (m v) -> p m v", v=2),
                                bc(ADB[:, l, m0:m0 + tiles], 2, [P, tiles, 2]), ALU.add).then_inc(E["mod_read"], 1)

            def ada_end(l):
                ada_read((l + 1) * ADA_STEPS - 1)
                ve.wait_ge(E["mod_read"], ADA_STEPS * (l + 1))
                for k in (1, 4, 7):
                    m = MOD[:, l, k * KT:(k + 1) * KT, :]
                    ins = V.tensor_scalar(m, m, 1.0, None, ALU.add)
                for k in (2, 8):
                    m = MOD[:, l, k * KT:(k + 1) * KT, :]
                    ins = V.tensor_scalar(m, m, 0.5, None, ALU.mult)
                link(ins)

            prep()

            def norm_first(hf, gain):
                rstd(R[0][:, :S])
                for k in range(KT + 2):
                    if k < KT:
                        V.scalar_tensor_tensor(hf[:, k, :], XC[:, k, 0:S], PT[:, gain + k:gain + k + 1], R[0][:, :S],
                                               ALU.mult, ALU.mult).then_inc(E["xn_ready"], 1)
                    if k >= 2:
                        got("hf_ready")
                        V.tensor_tensor(hL[:, k - 2, 0:S], hf[:, k - 2, :], hH[:, k - 2, 0:S].bitcast(F32), ALU.subtract)\
                            .then_inc(E["h_ready"], 1)

            norm_first(HF1, N1)

            for c in range(12):
                prep()
                t.use()
                if 1 <= c <= 8:
                    r = R[(c - 1) % 2][:]
                    rstd(r)
                    gain = GQ[:, 0:1] if c - 1 < 4 else PT[:, KN:KN + 1]
                    V.scalar_tensor_tensor(pair(QK, c - 1), pair(QK, c - 1), gain, r, ALU.mult, ALU.mult)\
                        .then_inc(E["qk_ready"], 1)
                if c in ADA_CHUNKS[1:]:
                    ada_read(c - ADA_CHUNKS[1])

            ve.wait_ge(E["misc_loaded"], dma_total["misc"])
            lv = LV[:].rearrange("p (a b) d -> p a b d", b=2)
            prod = T[1][:, 0:2 * HD].rearrange("p (a d) -> p a d", a=2)
            link(V.tensor_tensor(prod, lv[:, :, 0, :], lv[:, :, 1, :], ALU.mult))
            V.tensor_reduce(SM[:, 0:2], prod, AX, ALU.add).then_inc(E["lam_sums"], 1)
            got("lam_exps")
            link(V.tensor_tensor(SM[:, 4:5], SM[:, 3:4], SM[:, 2:3], ALU.subtract))
            link(V.tensor_scalar(SM[:, 5:6], SM[:, 4:5], -LAM_INIT, None, ALU.add))
            neg_lam = SM[:, 5:6]
            ss = SM[:, 8:24].rearrange("p (b g) -> p b g", b=TB)
            for h in range(HEADS):
                sc = SC[h % 2]
                got("scores_done")
                for i in range(TB):
                    nk = P * (i + 1)
                    col = 8 * (h % 2) + 4 * i
                    mx, nm = SM3[:, col:col + 2], SM3[:, col + 2:col + 4]
                    for c in range(2):
                        V.scalar_tensor_tensor(sc[i][:, c, :], ND[:, i, 0:nk], 2.0 ** -(h + 1), B[c][:, P * i:P * i + nk],
                                               ALU.mult, ALU.add).then_inc(E["sc_read"], 1)
                        t.next("sc_read")
                    ve.wait_ge(E["sc_read"], t.at("sc_read"))
                    link(V.tensor_reduce(mx, sc[i], AX, ALU.max))
                    V.tensor_scalar(nm, mx, -1.0, None, ALU.mult).then_inc(E["max_ready"], 1)
                sums, ri = (SM2[:, 8 * (h % 2):8 * (h % 2) + 8].rearrange("p (i a c) -> p i a c", i=TB, a=2)[:, :, k, :]
                            for k in range(2))
                ve.wait_ge(E["exp_ready"], t.next("exp_ready", TB))
                link(V.reciprocal(ri, sums))
                link(V.tensor_scalar(ri[:, :, 1:2], ri[:, :, 1:2], neg_lam, None, ALU.mult))
                for i in range(TB):
                    ins = V.tensor_scalar(sc[i][:, 0, :], sc[i][:, 0, :], ri[:, i, 0:1], None, ALU.mult)
                link(ins)
                for i in range(TB):
                    V.scalar_tensor_tensor(sc[i][:, 0, :], sc[i][:, 1, :], ri[:, i, 1:2], sc[i][:, 0, :],
                                           ALU.mult, ALU.add).then_inc(E["prob_ready"], 1)
                prep()
                ada_read(len(ADA_CHUNKS) + h - 1)
                if h < 4:
                    t.use()
                    got("va_copied")
                    va = VA[:, :, 256 * h:256 * (h + 1)]
                    sq = T[2][:].rearrange("p (b n) -> p b n", b=TB)
                    link(V.tensor_tensor(sq, va, va, ALU.mult))
                    for b in range(TB):
                        ins = V.tensor_reduce(ss[:, b, 2 * h:2 * h + 2],
                                              sq[:, b, :].rearrange("p (g n) -> p g n", g=2), AX, ALU.add)
                    if h < 3:
                        link(ins)
                    else:
                        link(ins)
                        link(V.tensor_scalar(SM[:, 8:24], SM[:, 8:24], 1.0 / P, EPS, ALU.mult, ALU.add))
                        V.tensor_copy(R[0][:, 0:16], SM[:, 8:24]).then_inc(E["var_ready"], 1)
                        got("std_ready")
                        link(V.reciprocal(R[0][:, 0:16], R[0][:, 0:16]))
                        for b in range(TB):
                            v = VA[:, b, :].rearrange("p (g n) -> p g n", g=KT)
                            ins = V.tensor_tensor(v, v, bc(R[0][:, KT * b:KT * b + KT], 2, [P, KT, P]), ALU.mult)
                        ins.then_inc(E["va_ready"], 1)
                        for g in range(KT):
                            if g % 2 == 0:
                                got("z_done")
                            ins = V.scalar_tensor_tensor(
                                ZB[:, g, :].rearrange("p (b n) -> p b n", b=TB),
                                bank2(6 + g // 2 % 2)[:, g % 2, :].rearrange("p (b n) -> p b n", b=TB),
                                PT[:, VG + g:VG + g + 1], bc(BSB[:, g, :], 1, [P, TB, P]), ALU.mult, ALU.add)
                            if g % 2:
                                ins.then_inc(E["zb_ready"], 1)
                        ve.wait_ge(E["zb_ready"], KT // 2)
                else:
                    j = h - 4
                    products()
                    V.tensor_tensor(T[2][:], B[4 + h % 2][:], pair(ZB, j), ALU.mult).then_inc(E["ya_ready"], 1)
                    ve.wait_ge(E["ya_ready"], 2 * j + 1)
                    split(pair(YAH, j), pair(YAL, j), T[2][:], "ya_ready")

            ada_read(ADA_LATE - 1)
            for j in range(4):
                rstd(R[j % 2][:])
                link(V.scalar_tensor_tensor(T[2 + j % 2][:], pair(QK, j), GQ[:, 1:2], R[j % 2][:], ALU.mult, ALU.mult))
                split(pair(YBH, j), pair(YBL, j), T[2 + j % 2][:], "yb_ready")
                if j in (0, 2):
                    prep()

            for j in range(4):
                b = 4 * (j % 2)
                for _ in range(2):
                    if j > 0:
                        prep()
                    t.use()
                gates = [T[2 * (j % 2)], T[2 * (j % 2) + 1]]
                for n in range(2):
                    prep()
                    products()
                    got("gate_ready")
                    V.tensor_tensor(T[4 + n][:], B[b + 2 + n][:], gates[n][:], ALU.mult).then_inc(E["up_read"], 1)
                ve.wait_ge(E["up_read"], 2 * (j + 1))
                link(V.tensor_tensor(T[4][:], T[4][:], T[5][:], ALU.add))
                split(pair(MH, j), pair(ML, j), T[4][:], "merged_ready")

            for j in range(4):
                prep()
                products()
                x = XC[:, 2 * j:2 * j + 2, 0:S]
                V.tensor_tensor(x, x, bank2(j), ALU.add).then_inc(E["x_ready"], 1)
                if j > 0:
                    ada_read(ADA_LATE + j - 1)

            norm_first(HF2, N2)
            got("logits_done")
            NR = N_GROUPS + N_EXPERTS

            def rt(i, *dims):
                n = 1
                for d in dims:
                    n *= d
                x = RT[:, i, 0:TB * n].rearrange("p (b n) -> p b n", b=TB)
                return x.rearrange("p b (g j) -> p b g j", g=dims[0]) if len(dims) == 2 else x

            def last(x, n):
                return x.to_broadcast([P, TB, n])

            logits = rt(0, NR)
            for b in range(TB):
                ins = V.tensor_tensor(logits[:, b, :], B[1 + b][:, 0:NR], BR[:], ALU.add)
            ins.then_inc(E["logits_read"], 1)
            ve.wait_ge(E["logits_read"], 1)
            gl = logits[:, :, 0:N_GROUPS]
            el = logits[:, :, N_GROUPS:].rearrange("p b (g j) -> p b g j", g=N_GROUPS)
            m, s4, gate, kmax = (SM2[:, 8 + 2 * i:10 + 2 * i].unsqueeze(2) for i in range(4))

            def first_max(x, is_max, n, desc, key):
                link(V.tensor_tensor(key, is_max, bc(desc, 1, [P, TB, n]), ALU.mult))
                link(V.tensor_reduce(kmax, key, AX, ALU.max))
                link(V.tensor_tensor(x, key, last(kmax, n), ALU.is_equal))

            d4, e4, oh4, key4 = rt(1, 4), rt(2, 4), rt(3, 4), rt(4, 4)
            link(V.tensor_reduce(m, gl, AX, ALU.max))
            V.tensor_tensor(d4, gl, last(m, 4), ALU.subtract).then_inc(E["top_ready"], 1)
            ve.wait_ge(E["top_ready"], 1)
            link(V.tensor_scalar(key4, d4, 0.0, None, ALU.is_ge))
            first_max(oh4, key4, 4, DESC[:, 0:N_GROUPS], key4)
            got("exp4_ready")
            link(V.tensor_reduce(s4, e4, AX, ALU.add))
            link(V.reciprocal(gate, s4))
            sel, e8 = rt(5, 4, 8), rt(6, 8)
            link(V.tensor_tensor(sel, el, oh4.unsqueeze(3).to_broadcast([P, TB, 4, 8]), ALU.mult))
            link(V.tensor_reduce(e8, sel.rearrange("p b g j -> p b j g"), AX, ALU.add))
            d8, key8, oh1, oh2, rest = rt(7, 8), rt(8, 8), rt(9, 8), rt(10, 8), rt(11, 8)
            link(V.tensor_reduce(m, e8, AX, ALU.max))
            link(V.tensor_tensor(d8, e8, last(m, 8), ALU.subtract))
            link(V.tensor_scalar(key8, d8, 0.0, None, ALU.is_ge))
            first_max(oh1, key8, 8, DESC[:, N_GROUPS:], key8)
            link(V.scalar_tensor_tensor(rest, oh1, -BIG, d8, ALU.mult, ALU.add))
            V.tensor_reduce(m, rest, AX, ALU.max).then_inc(E["m2_ready"], 1)
            ve.wait_ge(E["m2_ready"], 1)
            link(V.tensor_tensor(key8, rest, last(m, 8), ALU.is_equal))
            first_max(oh2, key8, 8, DESC[:, N_GROUPS:], key8)
            e2, w1_, w2_ = (SM2[:, 16 + 2 * i:18 + 2 * i].unsqueeze(2) for i in range(3))
            got("exp2_ready")
            link(V.tensor_scalar(s4, e2, 1.0, None, ALU.add))
            link(V.reciprocal(s4, s4))
            link(V.tensor_tensor(w1_, s4, gate, ALU.mult))
            link(V.tensor_tensor(w2_, w1_, e2, ALU.mult))
            link(V.tensor_tensor(oh1, oh1, last(w1_, 8), ALU.mult))
            link(V.tensor_tensor(oh2, oh2, last(w2_, 8), ALU.mult))
            link(V.tensor_tensor(oh1, oh1, oh2, ALU.add))
            for b in range(TB):
                ins = V.tensor_tensor(sel[:, b], bc(oh1[:, b, :], 1, [P, 4, 8]), bc(oh4[:, b, :], 2, [P, 4, 8]), ALU.mult)
            ins.then_inc(E["comb_ready"], 1)
            ada_read(ADA_STEPS - 3)
            got("combT_done")
            V.tensor_copy(CT[:], B[2][0:N_EXPERTS, 0:S]).then_inc(E["combT_ready"], 1)
            ada_read(ADA_STEPS - 2)
            ada_end(0)

            cb = CB[:].rearrange("p (i e) n -> p i e n", e=4)
            with t.loop(N_EXPERTS // 4, {**ring_counts(t.used, 12, "used", "fill", "split"), "silu_ready": 4, "gated": 4,
                                         "vec_step": 8}) as i:
                for which, e in MOE_ORDER:
                    prep()
                    if which != "w3":
                        t.use()
                        continue
                    products()
                    got("silu_ready")
                    V.tensor_tensor(T[2 + e % 2][:], B[2 * (e % 2) + 1][:], T[e % 2][:], ALU.mult).then_inc(E["gated"], 1)
                    got("gated")
                    x = T[2 + e % 2][:].rearrange("p (f n) -> p f n", f=2)
                    ve.wait_ge(E["comb_first"], 16)
                    for f in range(2):
                        ins = V.tensor_tensor(x[:, f, :], x[:, f, :], cb[:, i, e, :], ALU.mult)
                    link(ins)
                    split(HIDH[e % 2][:], HIDL[e % 2][:], x, "hid_ready")
                ve.wait_ge(E["comb_loaded"], 16)
            got("acc_done")
            for j in range(4):
                x = XC[:, 2 * j:2 * j + 2, 0:S]
                V.tensor_tensor(x, x, bank2(4 + j), ALU.add).then_inc(E["x_ready"], 1)

            def norm(n):
                got("std_ready")
                V.reciprocal(R[0][:, :n], R[0][:, :n]).then_inc(E["r_ready"], 1)
                got("r_ready")
                for k in range(KT):
                    if k == 0:
                        for m in (0, 2):
                            V.tensor_tensor(HF[:, m, :n], XC[:, m, :n], R[0][:, :n], ALU.mult).then_inc(E["xn_ready"], 1)
                    elif k % 2 == 0 and k + 2 < KT:
                        V.tensor_tensor(HF[:, k + 2, :n], XC[:, k + 2, :n], R[0][:, :n], ALU.mult)\
                            .then_inc(E["xn_ready"], 1)
                    got("hf_ready")
                    split(hH[:, k, :n], hL[:, k, :n], HF[:, k, :n], "h_ready")

            def residual(l, gate, m, b, n):
                for v in range(n // S):
                    x = XC[:, m, v * S:(v + 1) * S]
                    ins = V.scalar_tensor_tensor(x, B[b][:, v * S:(v + 1) * S], MOD[:, l, gate * KT + m, v:v + 1], x,
                                                 ALU.mult, ALU.add)
                ins.then_inc(E["x_ready"], 1)

            def ffn(l, gate, n):
                counts = {**ring_counts(t.used, len(FFN_CHUNKS), "used", "fill", "split"), "silu_ready": FT_HALF,
                          "gated": FT_HALF, "vec_step": FT_HALF}
                with t.loop(2, counts):
                    for j in range(FT_HALF):
                        prep(FFN_CHUNKS[j + 1])
                        products()
                        got("silu_ready")
                        V.tensor_tensor(T[2 + j % 2][:, :n], B[2 * (j % 2) + 1][:, :n], T[j % 2][:, :n], ALU.mult)\
                            .then_inc(E["gated"], 1)
                        got("gated")
                        split(aH[:, j, :n], aL[:, j, :n], T[2 + j % 2][:, :n], "hid_ready")
                    for (m, k0, ks), words in zip(DOWN_CHUNKS, FFN_CHUNKS[FT_HALF + 1:] + [CHUNK]):
                        prep(words)
                        products()
                        if k0 + ks == FT_HALF:
                            residual(l, gate, m, 4 + m % 4, n)

            def mix_split(x, m, p0, np_, c0, n):
                got("mix_hi")
                V.tensor_tensor(XL[p0:p0 + np_, m, c0:c0 + n], x, XH[p0:p0 + np_, m, c0:c0 + n].bitcast(F32),
                                ALU.subtract).then_inc(E["mix_ready"], 1)

            def mixers(l):
                n = 2 * S if l + 1 < LAYERS else S
                for c in range(5):
                    prep()
                    t.use()
                if l == 0:
                    ve.wait_ge(E["mix_consts_loaded"], dma_total["mix"])
                step = ADA_STEPS * (l + 1) - 1
                for i in range(6):
                    if l + 1 < LAYERS and 1 <= i <= 4:
                        if step >= ADA_STEPS * (l + 1):
                            ada_read(step)
                        step += 1
                    if 1 <= i <= 2:
                        p = i - 1
                        got("mix_hi")
                        V.scalar_tensor_tensor(XL[:, 4 + p, :n], B[1][:, :n], PT[:, PS + 2 * l + p:PS + 2 * l + p + 1],
                                               XH[:, 4 + p, :n].bitcast(F32), ALU.mult, ALU.subtract)\
                            .then_inc(E["mix_ready"], 1)
                    elif i == 5:
                        for d in range(2):
                            mix_split(B[2 + d][:, :n], 6 + d, 0, P, 0, n)
                    if i < 5:
                        w = n if i < 4 else 2 * S
                        rstd(R[i % 2][:, :w])
                        gain = PT[:, QG2 + l:QG2 + l + 1] if i < 4 else PT[:, KG2 + l:KG2 + l + 1]
                        V.scalar_tensor_tensor(QQ[:, i, :w], QQ[:, i, :w], gain, R[i % 2][:, :w], ALU.mult, ALU.mult)\
                            .then_inc(E["qn_ready"], 1)
                        t.next("qn_ready")
                    if i >= 1:
                        x = QQ[:, i - 1, 0:S]
                        got("rot_done")
                        c, s = T[i % 2][:, 0:S], T[i % 2][:, S:2 * S]
                        V.tensor_tensor(c, x, TRIG[:, 0, :], ALU.mult)
                        link(V.tensor_tensor(s, B[4][:, :S], TRIG[:, 1, :], ALU.mult))
                        V.tensor_tensor(x, c, s, ALU.add).then_inc(E["q_ready"], 1)
                pairs = attention_pairs(l)
                for u in range(len(pairs) + 2):
                    i = 2 * u % 4
                    if u < len(pairs):
                        h, q0, k0, nk = pairs[u]
                        got("scores_done")
                        mx, nm = SM[:, 8 + i:10 + i], SM[:, 12 + i:14 + i]
                        for c in range(2):
                            ins = V.tensor_reduce(mx[:, c:c + 1], B[SCORE_BANKS[(2 * u + c) % 3]][:, :nk], AX, ALU.max)
                        link(ins)
                        V.tensor_scalar(nm, mx, -(HD ** -0.5), None, ALU.mult).then_inc(E["max_ready"], 1)
                    if u >= 2:
                        h, q0, k0, nk = pairs[u - 2]
                        mix_split(B[4][:, 0:P], h // 2, 0, P, q0, P)
                    if u < len(pairs):
                        h, q0, k0, nk = pairs[u]
                        sums, ri = SM2[:, i:i + 2], SM2[:, 4 + i:6 + i]
                        ve.wait_ge(E["exp_ready"], t.next("exp_ready", 2))
                        link(V.reciprocal(ri, sums))
                        for c in range(2):
                            e = PROBS[i + c][:, :nk]
                            ins = V.tensor_scalar(e, e, ri[:, c:c + 1], None, ALU.mult)
                        ins.then_inc(E["prob_ready"], 1)
                    if ada_beside(l, u) is not None:
                        ada_read(ada_beside(l, u) - 1)
                if l + 1 < LAYERS:
                    ada_end(l + 1)
                for j in range(4):
                    prep()
                    products()
                    for m in (2 * j, 2 * j + 1):
                        residual(l, 5, m, m, n)

            for l in range(LAYERS):
                n = 2 * S if l + 1 < LAYERS else S
                norm(2 * S)
                ffn(l, 2, 2 * S)
                norm(2 * S)
                mixers(l)
                norm(n)
                ffn(l, 8, n)

            rstd(R[0][:, :S])
            for k in range(KT):
                ins = V.scalar_tensor_tensor(HF[:, k, :S], XC[:, k, :S], PT[:, FG + k:FG + k + 1], R[0][:, :S],
                                             ALU.mult, ALU.mult)
                ins.then_inc(E["hf_done"], 1)

        @block.scalar
        def _(act):
            t = Tally(act)
            A = nc.scalar

            def got(name):
                act.wait_ge(E[name], t.next(name))

            def products():
                s, n = t.use()
                act.wait_ge(slot_used[s], n)

            def prep(words=CHUNK):
                s = t.take()
                before = (s + HI_SLOTS) % RAW_SLOTS
                act.wait_ge(raw_loaded[s], t.at(f"fill{s}") * 32)
                if t.n[f"fill{before}"]:
                    act.wait_ge(slot_used[before], t.at(f"fill{before}"))
                A.activation(HI[s % HI_SLOTS][:, :words], RAW[s][:, :words], ACT.Copy).then_inc(hi_done[s], 1)

            def root(mean, r):
                got("stats_done")
                A.activation(r, mean, ACT.Sqrt, bias=EPSC[:]).then_inc(E["std_ready"], 1)

            def squares(fresh):
                for k in range(KT):
                    fresh(k)
                    if k >= 2:
                        got("sq_used")
                    A.activation(SQ[k % 2][:, :S], XC[:, k, :S], ACT.Square).then_inc(E["sq_ready"], 1)

            def first_high(hf):
                for k in range(KT):
                    got("xn_ready")
                    A.activation(hH[:, k, 0:S], hf[:, k, :], ACT.Copy).then_inc(E["hf_ready"], 1)

            def last_square(n, residuals):
                t.n["x_ready"] += residuals
                act.wait_ge(E["x_ready"], t.n["x_ready"])
                A.activation(SQ[1][:, :n], XC[:, KT - 1, :n], ACT.Square).then_inc(E["sq_ready"], 1)
                root(B[0][:, :n], R[0][:, :n])

            act.dma_start(MATS[:], a["mats"]).then_inc(E["mats_loaded"], 16)
            for src, dst in vectors:
                act.dma_start(dst, src).then_inc(E["rows_loaded"], 16)

            def to_features(v):
                for c in range(4):
                    got("x_done")
                    A.activation(XC[:, 2 * c:2 * c + 2, v * S:(v + 1) * S], bank2((4 * v + c + 1) % 8), ACT.Copy)\
                        .then_inc(E["x_copied"], 1)

            def from_start(k):
                act.wait_ge(E["x_copied"], 4)

            to_features(0)
            prep()
            squares(from_start)
            root(B[0][:, :S], R[0][:, :S])
            first_high(HF1)
            def ada_copy(n):
                act.wait_ge(ada_used[2 * (n % 2) + 1], n // 2 + 1)
                A.activation(adt(n)[:], B[6][:], ACT.Copy).then_inc(E["ada_copied"], 1)

            def other_inputs():
                to_features(1)
                got("params_ready")
                for v in range(2):
                    A.activation(CS[:, :, v], PT[:, CV + v * KT:CV + (v + 1) * KT], ACT.Silu).then_inc(E["cs_ready"], 1)
                for i in range(2):
                    got("ws_done")
                    A.activation(WST[:, 4 * i:4 * i + 4, :].rearrange("p g t -> p (g t)"), B[1 + i][:], ACT.Copy)\
                        .then_inc(E["wst_ready"], 1)

            for c in range(12):
                prep()
                if c == 0:
                    other_inputs()
                products()
                if c < 8:
                    A.activation(pair(QK, c), B[4 + c % 2][:], ACT.Copy)
                    A.activation(SQ[c % 2][:], B[4 + c % 2][:], ACT.Square).then_inc(E["sq_ready"], 1)
                else:
                    A.activation(VB[:, :, 256 * (c - 8):256 * (c - 7)], bank2(4 + c % 2), ACT.Copy)\
                        .then_inc(E["vb_ready"], 1)
                if 1 <= c <= 8:
                    if c >= 3:
                        act.wait_ge(E["qk_ready"], c - 2)
                    root(B[2 + (c - 1) % 2][:], R[(c - 1) % 2][:])
                if c in ADA_CHUNKS:
                    ada_copy(c - ADA_CHUNKS[0])

            got("lam_sums")
            A.activation(SM[:, 2:4], SM[:, 0:2], ACT.Exp).then_inc(E["lam_exps"], 1)

            def head_probs(h):
                got("probT_done")
                A.activation(T[3][:, 0:3 * P], B[2][:, 0:3 * P], ACT.Copy).then_inc(E["probT_ready"], 1)

            def head_out(h):
                got("pv_done")
                A.activation(QK[:, h, :], B[3][:, 0:S], ACT.Copy).then_inc(E["o_ready"], 1)

            for h in range(HEADS):
                if h >= 1:
                    head_probs(h - 1)
                for i in range(TB):
                    got("max_ready")
                    for c in range(2):
                        col = 8 * (h % 2) + 4 * i + c
                        ins = A.activation(SC[h % 2][i][:, c, :], SC[h % 2][i][:, c, :], ACT.Exp,
                                           bias=SM3[:, col + 2:col + 3], accum_out=SM2[:, col:col + 1])
                    ins.then_inc(E["exp_ready"], 1)
                ada_copy(len(ADA_CHUNKS) + h)
                if h >= 1:
                    head_out(h - 1)
                prep()
                if h < 4:
                    products()
                    A.activation(VA[:, :, 256 * h:256 * (h + 1)], bank2(4 + h % 2), ACT.Copy).then_inc(E["va_copied"], 1)
                else:
                    t.use()
                if h == 3:
                    got("var_ready")
                    A.activation(R[0][:, 0:16], R[0][:, 0:16], ACT.Sqrt).then_inc(E["std_ready"], 1)
            head_probs(HEADS - 1)
            head_out(HEADS - 1)
            act.wait_ge(E["mod_read"], ADA_LATE)
            act.wait_ge(E["o_ready"], HEADS)
            for j in range(4):
                A.activation(SQ[j % 2][:], pair(QK, j), ACT.Square).then_inc(E["sq_ready"], 1)
                if j >= 1:
                    if j >= 3:
                        act.wait_ge(E["yb_ready"], j - 2)
                    root(B[4 + j - 1][:], R[(j - 1) % 2][:])
                if j in (1, 3):
                    prep()
            act.wait_ge(E["yb_ready"], 2)
            root(B[7][:], R[1][:])

            for j in range(4):
                if j == 1:
                    act.wait_ge(E["yb_ready"], 4)
                if j >= 2:
                    act.wait_ge(E["up_read"], 2 * (j - 1))
                for n in range(2):
                    if j > 0:
                        prep()
                    products()
                    for m in range(2):
                        col = BG + KT * n + 2 * j + m
                        ins = A.activation(T[2 * (j % 2) + n][:, m * S:(m + 1) * S], bank2(4 * (j % 2) + n)[:, m, :],
                                           ACT.Sigmoid, bias=PT[:, col:col + 1])
                    ins.then_inc(E["gate_ready"], 1)
                for n in range(2):
                    prep()
                    t.use()
            for j in range(4):
                prep()
                t.use()
                ada_copy(ADA_LATE + j)

            def by_pair(k):
                if k % 2 == 0:
                    got("x_ready")

            last_square(S, KT // 2)
            first_high(HF2)

            def rt(i, n):
                return RT[:, i, 0:TB * n]
            got("top_ready")
            A.activation(rt(2, 4), rt(1, 4), ACT.Exp).then_inc(E["exp4_ready"], 1)
            got("m2_ready")
            A.activation(SM2[:, 16:18], SM2[:, 8:10], ACT.Exp).then_inc(E["exp2_ready"], 1)
            for n in range(ADA_STEPS - 2, ADA_STEPS):
                ada_copy(n)

            with t.loop(N_EXPERTS // 4, {**ring_counts(t.used, 12, "used", "fill"), "silu_ready": 0, "gated": 4}) as i:
                for which, e in MOE_ORDER:
                    prep()
                    if which != "w1":
                        t.use()
                        if which == "w3":
                            t.next("gated")
                        continue
                    products()
                    if e >= 2:
                        act.wait_ge(E["gated"], t.at("gated", 1))
                    else:
                        act.wait_ge(E["gated"], t.at("gated", e))
                    A.activation(T[e % 2][:], B[2 * (e % 2)][:], ACT.Silu).then_inc(E["silu_ready"], 1)

            def norm(l, shift, scale, n):
                for k in range(KT):
                    got("xp_ready" if k % 2 else "xn_ready")
                    for v in range(n // S):
                        h = HF[:, k, v * S:(v + 1) * S]
                        ins = A.activation(h, h, ACT.Identity, bias=MOD[:, l, shift * KT + k, v:v + 1],
                                           scale=MOD[:, l, scale * KT + k, v:v + 1])
                    ins.then_inc(E["hf_ready"], 1)

            def ffn(n):
                counts = {**ring_counts(t.used, len(FFN_CHUNKS), "used", "fill"), "gated": FT_HALF, "gate_done": FT_HALF}
                with t.loop(2, counts):
                    for j in range(FT_HALF):
                        prep(FFN_CHUNKS[j + 1])
                        got("gate_done")
                        act.wait_ge(E["gated"], t.at("gated", min(j, 1)))
                        A.activation(T[j % 2][:, :n], B[2 * (j % 2)][:, :n], ACT.Silu).then_inc(E["silu_ready"], 1)
                        t.next("gated")
                        t.use()
                    for words in FFN_CHUNKS[FT_HALF + 1:] + [CHUNK]:
                        prep(words)
                        t.use()
                t.n["x_ready"] += KT

            def mix_high(x, m, p0, np_, c0, n, **scale):
                A.activation(XH[p0:p0 + np_, m, c0:c0 + n], x, ACT.Copy, **scale).then_inc(E["mix_hi"], 1)

            def mixers(l):
                n = 2 * S if l + 1 < LAYERS else S
                sets = n // S
                for c in range(5):
                    prep()
                    products()
                    if c < 2:
                        for i in (2 * c, 2 * c + 1):
                            A.activation(QQ[:, i, :n], B[i][:, :n], ACT.Copy).then_inc(E["q_copied"], 1)
                    elif c == 2:
                        A.activation(QQ[:, 4, :], B[4][:], ACT.Copy).then_inc(E["q_copied"], 1)
                        for kv in range(2):
                            src = B[5][:].rearrange("p (b n) -> p b n", b=4)[:, :, kv * HD:(kv + 1) * HD]
                            ins = A.activation(VD[:, :, kv], src, ACT.Copy)
                        ins.then_inc(E["v_ready"], 1)
                    else:
                        for s in range(sets):
                            ins = A.activation(PF[:, 2 * s:2 * s + 2, c - 3, :], bank2([6, 0][c - 3] + s), ACT.Copy)
                            ins.then_inc(E["pf_ready"], 1)
                act.wait_ge(E["q_copied"], 5 * (l + 1))
                for i in range(6):
                    if i < 5:
                        w = n if i < 4 else 2 * S
                        A.activation(SQ[i % 2][:, :w], QQ[:, i, :w], ACT.Square).then_inc(E["sq_ready"], 1)
                    if i >= 1:
                        w = n if i < 5 else 2 * S
                        if i >= 3:
                            act.wait_ge(E["qn_ready"], 5 * l + i - 2)
                        root(B[2 + (i - 1) % 2][:, :w], R[(i - 1) % 2][:, :w])
                    if 1 <= i <= 2:
                        p = i - 1
                        for s in range(sets):
                            got("pool_done")
                            for g in range(2):
                                rows = slice(HD * g, HD * (g + 1))
                                ins = A.activation(T[2 + p][rows, s * S:(s + 1) * S],
                                                   bank2(MIX_BANKS[s])[rows, g, :], ACT.Copy)
                            ins.then_inc(E["pm_ready"], 1)
                        if l + 1 < LAYERS:
                            ada_copy(ADA_STEPS * (l + 1) + p)
                        got("pwb_done")
                        col = PS + 2 * l + p
                        mix_high(B[1][:, :n], 4 + p, 0, P, 0, n, scale=PT[:, col:col + 1])
                    elif 3 <= i <= 4:
                        p = i - 3
                        for s in range(sets):
                            got("fftab_done")
                            A.activation(AB[:], B[MIX_BANKS[s]][:], ACT.Copy).then_inc(E["ab_ready"], 1)
                            if l + 1 < LAYERS and s == 0:
                                ada_copy(ADA_STEPS * (l + 1) + 2 + p)
                            got("fft_done")
                            A.activation(T[2 + p][:, s * S:(s + 1) * S], B[1][:, :S], ACT.Copy).then_inc(E["ft_ready"], 1)
                    elif i == 5:
                        for d in range(2):
                            got("yf_done")
                            mix_high(B[2 + d][:, :n], 6 + d, 0, P, 0, n)
                for kv in range(2):
                    got("dup_done")
                    A.activation(KD[:, kv, :], B[4 + kv][:], ACT.Copy).then_inc(E["kd_ready"], 1)
                pairs = attention_pairs(l)
                for u in range(len(pairs) + 2):
                    if u < len(pairs):
                        h, q0, k0, nk = pairs[u]
                        got("max_ready")
                        for c in range(2):
                            i = (2 * u + c) % 4
                            A.activation(PROBS[i][:, :nk], B[SCORE_BANKS[(2 * u + c) % 3]][:, :nk], ACT.Exp,
                                         bias=SM[:, 12 + i:13 + i], scale=HD ** -0.5, accum_out=SM2[:, i:i + 1])\
                                .then_inc(E["exp_ready"], 1)
                    if u >= 2:
                        h, q0, k0, nk = pairs[u - 2]
                        got("pv_done")
                        mix_high(B[4][:, 0:P], h // 2, 0, P, q0, P)
                    if 1 <= u <= len(pairs):
                        h, q0, k0, nk = pairs[u - 1]
                        got("probT_done")
                        for c in range(2):
                            A.activation(T[2 + c][:, :nk], B[2 + c][:, :nk], ACT.Copy).then_inc(E["probT_ready"], 1)
                    if ada_beside(l, u) is not None:
                        ada_copy(ada_beside(l, u))
                for j in range(4):
                    prep()
                    t.use()

            for l in range(LAYERS):
                n = 2 * S if l + 1 < LAYERS else S
                if l == 0:
                    squares(by_pair)
                    root(B[0][:], R[0][:])
                else:
                    last_square(2 * S, KT)
                norm(l, 0, 1, 2 * S)
                ffn(2 * S)
                last_square(2 * S, KT)
                norm(l, 3, 4, 2 * S)
                mixers(l)
                last_square(n, KT)
                norm(l, 6, 7, n)
                ffn(n)
            last_square(S, KT)

            for j in range(4):
                got("fin_done")
                half, b = j // 2, j % 2
                A.activation(OUTB[:, b, 512 * half:512 * (half + 1)], B[1 + j][:], ACT.Copy).then_inc(E["outb_ready"], 1)

        @block.tensor
        def _(pe):
            t = Tally(pe)
            mm = nc.tensor.matmul
            release = {}
            turn_start = {}

            def got(name):
                pe.wait_ge(E[name], t.next(name))

            def claim(b, reader, count=None):
                if b in release:
                    name, n = release[b]
                    pe.wait_ge(E[name], n)
                elif t.turn is not None:
                    pe.wait_ge(E[reader], turn_start[reader])
                release[b] = (reader, count or t.next(reader))

            @contextmanager
            def turns(n, counts, events):
                for name, v in release.values():
                    pe.wait_ge(E[name], v)
                release.clear()
                with t.loop(n, counts) as i:
                    for e in events:
                        turn_start[e] = t.at(e)
                    yield i
                for b, (name, _) in release.items():
                    release[b] = (name, t.n[name])

            def chunk():
                s = t.take()
                pe.wait_ge(lo_done[s], t.next(f"split{s}"))
                return s

            def used(ins, s):
                ins.then_inc(slot_used[s], 1)

            def exact(o, wh, wl, xh, xl, first=True, last=True, **more):
                mm(o, wh, xh, start=first, stop=False, **more)
                mm(o, wh, xl, start=False, stop=False, **more)
                return mm(o, wl, xh, start=False, stop=last, **more)

            def slot(s, **dims):
                v = "p (k n) -> p k n"
                return HI[s % HI_SLOTS][:].rearrange(v, **dims), LO[s][:].rearrange(v, **dims)

            def features(s, col, o, xh, xl, n, wait=None):
                wh, wl = slot(s, k=KT)
                for k in range(KT):
                    if wait:
                        wait(k)
                    ins = exact(o, wh[:, k, col:col + P], wl[:, k, col:col + P], xh[:, k, :n], xl[:, k, :n],
                                k == 0, k == KT - 1)
                return ins

            def tokens(s, block, o, col=0, w=256):
                wh, wl = slot(s, k=KT)
                rows = slice(P * block, P * (block + 1))
                for k in range(KT):
                    ins = exact(o, hH[:, k, rows], hL[:, k, rows], wh[:, k, col:col + w], wl[:, k, col:col + w],
                                k == 0, k == KT - 1)
                return ins

            def mean_of_squares():
                claim(0, "std_ready")
                for k in range(KT):
                    got("sq_ready")
                    ins = mm(B[0][:, :S], mat(MEAN_D), SQ[k % 2][:, :S], start=(k == 0), stop=(k == KT - 1))
                    if k < KT - 2:
                        ins.then_inc(E["sq_used"], 1)
                return ins

            def mean_of_sums(n):
                claim(0, "std_ready")
                got("acc_ready")
                mm(B[0][:, :n], mat(MEAN_D), ACC[:, :n], start=True, stop=False)
                got("sq_ready")
                mm(B[0][:, :n], mat(MEAN_D), SQ[1][:, :n], start=False, stop=True).then_inc(E["stats_done"], 1)

            def stats(m, i, b, n=512):
                claim(b, "std_ready")
                got("sq_ready")
                mm(B[b][:, :n], mat(m), SQ[i % 2][:, :n], start=True, stop=True).then_inc(E["stats_done"], 1)

            def wait_h(k):
                got("h_ready")

            pe.wait_ge(E["mats_loaded"], 16)

            def to_features(v):
                for c in range(4):
                    b = (4 * v + c + 1) % 8
                    claim(b, "x_copied")
                    for m in range(2):
                        for blk in range(TB):
                            ins = nc.tensor.transpose(bank2(b)[:, m, blk * P:(blk + 1) * P],
                                                      XS[:, v, blk, (2 * c + m) * P:(2 * c + m + 1) * P], mat(IDENT))
                    ins.then_inc(E["x_done"], 1)

            pe.wait_ge(E["x_loaded"], 16)
            to_features(0)
            pe.wait_ge(E["rows_loaded"], dma_total["rows"])
            claim(0, "params_ready")
            nc.tensor.transpose(B[0][:, 0:N_COLS], PA[:], mat(IDENT)[0:N_COLS, 0:N_COLS])
            for l in range(LAYERS):
                ins = nc.tensor.transpose(B[0][:, P + l * P:P + l * P + MODT], PB[:, l, :], mat(IDENT)[0:MODT, 0:MODT])
            ins.then_inc(E["params_done"], 1)
            mean_of_squares().then_inc(E["stats_done"], 1)
            pe.wait_ge(E["ctx_loaded"], 16)
            to_features(1)
            pe.wait_ge(E["ws_masked"], 1)
            for i in range(2):
                claim(1 + i, "wst_ready")
                for g in range(4):
                    ins = nc.tensor.transpose(B[1 + i][:, g * P:(g + 1) * P], WS[:, 4 * i + g, :], mat(IDENT))
                ins.then_inc(E["ws_done"], 1)

            def ada_finish(n):
                got("ada_copied")
                claim(7, "mod_read")
                for m in range(ADA_W // P):
                    ins = mm(B[7][:, 2 * m:2 * m + 2], adt(n)[:, m * P:(m + 1) * P], ASEL[:],
                             start=True, stop=True)
                ins.then_inc(E["ada_done"], 1)

            def ada(n):
                if n % ADA_STEPS and n != ADA_LATE:
                    ada_finish(n - 1)
                claim(6, "ada_copied", n + 1)
                for half in range(2):
                    place = 2 * (n % 2) + half
                    pe.wait_ge(ada_loaded[place], 32 * (n // 2 + 1))
                    for j in range(COL_TILES):
                        ins = mm(bank2(6)[CT_W * j:CT_W * (j + 1)], CS[:, COL_TILES * half + j, :],
                                 ADW[n // ADA_STEPS][place][:, j],
                                 start=(half == 0), stop=(half == 1))
                    ins.then_inc(ada_used[place], 1)

            for c in range(12):
                s = chunk()
                b = 4 + c % 2
                if c < 8:
                    claim(b, "sq_ready", KT + c + 1)
                    for m in range(2):
                        ins = features(s, m * P, bank2(b)[:, m, :], hH, hL, S, wait_h if c == 0 and m == 0 else None)
                else:
                    claim(b, "vb_ready")
                    for blk in range(TB):
                        ins = tokens(s, blk, bank2(b)[:, blk, :])
                used(ins, s)
                if 1 <= c <= 8:
                    stats(MEAN_HD, c - 1, 2 + (c - 1) % 2)
                if c == ADA_CHUNKS[0]:
                    pe.wait_ge(E["cs_ready"], 2)
                    pe.wait_ge(E["misc_loaded"], dma_total["misc"])
                if c in ADA_CHUNKS:
                    ada(c - ADA_CHUNKS[0])

            pe.wait_ge(E["qk_ready"], 8)
            pe.wait_ge(E["vb_ready"], 4)
            def head_probs(h):
                claim(2, "probT_ready", h + 1)
                got("prob_ready")
                sc = SC[h % 2]
                nc.tensor.transpose(B[2][:, 0:P], sc[0][:, 0, :], mat(IDENT))
                got("prob_ready")
                nc.tensor.transpose(B[2][:, P:2 * P], sc[1][:, 0, 0:P], mat(IDENT))
                nc.tensor.transpose(B[2][:, 2 * P:3 * P], sc[1][:, 0, P:S], mat(IDENT)).then_inc(E["probT_done"], 1)

            def head_out(h):
                claim(3, "o_ready")
                got("probT_ready")
                v = VB[:, :, h * P:(h + 1) * P]
                pT = T[3]
                mm(B[3][:, 0:P], v[:, 0, :], pT[:, 0:P], start=True, stop=True)
                mm(B[3][:, P:S], v[:, 0, :], pT[:, P:2 * P], start=True, stop=False)
                mm(B[3][:, P:S], v[:, 1, :], pT[:, 2 * P:3 * P], start=False, stop=True).then_inc(E["pv_done"], 1)

            for h in range(HEADS):
                for i in range(TB):
                    nk = P * (i + 1)
                    for c in range(2):
                        rows = slice(HD * c, HD * (c + 1))
                        if i == 0:
                            claim(c, "sc_read", 2 * TB * (h + 1))
                        ins = mm(B[c][:, P * i:P * i + nk], QK[rows, h, i * P:(i + 1) * P], QK[rows, HEADS + h, 0:nk],
                                 start=True, stop=True)
                ins.then_inc(E["scores_done"], 1)
                if h >= 1:
                    head_probs(h - 1)
                ada(len(ADA_CHUNKS) + h)
                if h >= 1:
                    head_out(h - 1)
                s = chunk()
                b = 4 + h % 2
                if h < 4:
                    claim(b, "va_copied")
                    for blk in range(TB):
                        ins = tokens(s, blk, bank2(b)[:, blk, :])
                else:
                    claim(b, "ya_ready", 2 * (h - 4) + 1)
                    for m in range(2):
                        ins = features(s, m * P, bank2(b)[:, m, :], hH, hL, S)
                used(ins, s)
                if h == 3:
                    got("va_ready")
                    t.next("std_ready")
                    pe.wait_ge(E["wst_ready"], 2)
                    for g in range(KT):
                        if g % 2 == 0:
                            claim(6 + g // 2 % 2, "zb_ready")
                        for blk in range(TB):
                            ins = mm(bank2(6 + g // 2 % 2)[:, g % 2, blk * P:(blk + 1) * P], VA[:, blk, g * P:(g + 1) * P],
                                     WST[:, g, :], start=True, stop=True)
                        if g % 2:
                            ins.then_inc(E["z_done"], 1)
            head_probs(HEADS - 1)
            ada_finish(ADA_LATE - 1)
            head_out(HEADS - 1)
            for j in range(4):
                stats(MEAN_P, j, 4 + j)

            for j in range(4):
                b = 4 * (j % 2)
                for n in range(4):
                    s = chunk()
                    claim(b + n, "gate_ready" if n < 2 else "up_read")
                    if j == 0 and n == 2:
                        pe.wait_ge(E["ya_ready"], 8)
                    if j == 0 and n == 3:
                        pe.wait_ge(E["yb_ready"], 4)
                    xh, xl = ((hH, hL), (hH, hL), (YAH, YAL), (YBH, YBL))[n]
                    for m in range(2):
                        ins = features(s, m * P, bank2(b + n)[:, m, :], xh, xl, S)
                    used(ins, s)
            pe.wait_ge(E["merged_ready"], 4)
            for j in range(4):
                s = chunk()
                claim(j, "x_ready")
                for m in range(2):
                    ins = features(s, m * P, bank2(j)[:, m, :], MH, ML, S)
                used(ins, s)
                ada(ADA_LATE + j)

            mean_of_sums(S)
            claim(1, "logits_read")
            claim(2, "logits_read", 1)
            NR = N_GROUPS + N_EXPERTS
            for k in range(KT):
                got("h_ready")
                for blk in range(TB):
                    ins = mm(B[1 + blk][:, 0:NR], HF2[:, k, blk * P:(blk + 1) * P], WR[:, k, :],
                             start=(k == 0), stop=(k == KT - 1))
            ins.then_inc(E["logits_done"], 1)
            ada(ADA_STEPS - 2)
            got("comb_ready")
            claim(2, "combT_ready")
            comb = RT[:, 5, 0:TB * N_EXPERTS].rearrange("p (b e) -> p b e", b=TB)
            for blk in range(TB):
                ins = nc.tensor.transpose(B[2][0:N_EXPERTS, blk * P:(blk + 1) * P], comb[:, blk, :], mat(IDENT))
            ins.then_inc(E["combT_done"], 1)
            ada(ADA_STEPS - 1)
            ada_finish(ADA_STEPS - 1)

            zeros = ZERO[:]
            pe.wait_ge(E["gated"], START["gated"])
            for b in range(4, 8):
                claim(b, "x_ready")
                mm(B[b][:], zeros[:, 0:P], zeros[:], start=True, stop=False, skip_group_check=True)
            acc_release = {b: release.pop(b) for b in range(4, 8)}
            counts = {**ring_counts(t.pos, 12, "fill", "split"), "silu_ready": 4, "gated": 4, "hid_ready": 4}
            with turns(N_EXPERTS // 4, counts, ["silu_ready", "gated"]):
                for which, e in MOE_ORDER:
                    s = chunk()
                    if which == "w2":
                        got("hid_ready")
                        wh, wl = slot(s, k=2)
                        for m in range(KT):
                            for f in range(2):
                                ins = exact(bank2(4 + m // 2)[:, m % 2, :], wh[:, f, m * P:(m + 1) * P],
                                            wl[:, f, m * P:(m + 1) * P], HIDH[e % 2][:, f, :], HIDL[e % 2][:, f, :],
                                            False, False, skip_group_check=True)
                    else:
                        b = 2 * (e % 2) + (which == "w3")
                        claim(b, "gated" if which == "w3" else "silu_ready")
                        for f in range(2):
                            ins = features(s, f * P, bank2(b)[:, f, :], hH, hL, S)
                    used(ins, s)
            for b in range(4, 8):
                ins = mm(B[b][:, 0:2], zeros[:, 0:P], zeros[:, 0:2], start=False, stop=True, skip_group_check=True)
            ins.then_inc(E["acc_done"], 1)
            release.update(acc_release)

            def ffn(n):
                counts = {**ring_counts(t.pos, len(FFN_CHUNKS), "fill", "split"), "silu_ready": FT_HALF, "gated": FT_HALF,
                          "hid_ready": FT_HALF, "x_ready": KT}
                normed = t.n["h_ready"]
                t.n["h_ready"] += KT
                with turns(2, counts, ["silu_ready", "gated", "x_ready"]):
                    for j in range(FT_HALF):
                        s = chunk()
                        wh, wl = slot(s, k=2 * KT)
                        for which in range(2):
                            b = 2 * (j % 2) + which
                            claim(b, ("silu_ready", "gated")[which])
                            for k in range(KT):
                                if j == 0 and which == 0:
                                    pe.wait_ge(E["h_ready"], normed + k + 1)
                                ins = exact(B[b][:, :n], wh[:, which * KT + k, :], wl[:, which * KT + k, :], hH[:, k, :n],
                                            hL[:, k, :n], k == 0, k == KT - 1)
                            if which == 0:
                                ins.then_inc(E["gate_done"], 1)
                        used(ins, s)
                    for m, k0, ks in DOWN_CHUNKS:
                        s = chunk()
                        b = 4 + m % 4
                        if k0 == 0:
                            claim(b, "x_ready")
                        wh = HI[s % HI_SLOTS][:, :ks * P].rearrange("p (k n) -> p k n", n=P)
                        wl = LO[s][:, :ks * P].rearrange("p (k n) -> p k n", n=P)
                        for k in range(k0, k0 + ks):
                            if m == 0:
                                got("hid_ready")
                            ins = exact(B[b][:, :n], wh[:, k - k0, :], wl[:, k - k0, :], aH[:, k, :n], aL[:, k, :n], k == 0,
                                        k == FT_HALF - 1)
                        used(ins, s)

            def mixers(l):
                n = 2 * S if l + 1 < LAYERS else S
                sets = n // S
                for c in range(5):
                    s = chunk()
                    if c < 2:
                        for m in range(2):
                            claim(2 * c + m, "q_copied")
                            ins = features(s, m * P, B[2 * c + m][:, :n], hH, hL, n, wait_h if c == 0 and m == 0 else None)
                    elif c == 2:
                        claim(4, "q_copied")
                        features(s, 0, B[4][:], hH, hL, 2 * S)
                        claim(5, "v_ready")
                        for blk in range(2 * TB):
                            ins = tokens(s, blk, B[5][:, blk * P:(blk + 1) * P], P, P)
                    else:
                        for blk in range(sets * TB):
                            b = [6, 0][c - 3] + blk // TB
                            if blk % TB == 0:
                                claim(b, "pf_ready")
                            ins = tokens(s, blk, bank2(b)[:, blk % TB, :])
                    used(ins, s)
                pe.wait_ge(E["pf_ready"], t.n["pf_ready"])
                if l == 0:
                    pe.wait_ge(E["mix_consts_loaded"], dma_total["mix"])

                def pooled(p):
                    for s in range(sets):
                        b = MIX_BANKS[s]
                        claim(b, "pm_ready")
                        for g in range(2):
                            for blk in range(TB):
                                ins = mm(bank2(b)[:, g, :], PF[:, 2 * s + blk, 0, p * P:(p + 1) * P],
                                         POOL[:, 2 * p + g, blk, :],
                                         start=(blk == 0), stop=(blk == TB - 1))
                        ins.then_inc(E["pool_done"], 1)
                    if l + 1 < LAYERS:
                        ada(ADA_STEPS * (l + 1) + p)
                    pe.wait_ge(E["pm_ready"], t.n["pm_ready"])
                    claim(1, "mix_ready")
                    mm(B[1][:, :n], PWB[:, l, p, :], T[2 + p][:, :n], start=True, stop=True).then_inc(E["pwb_done"], 1)

                def fourier(p):
                    before = t.n["ab_ready"]
                    for s in range(sets):
                        b = MIX_BANKS[s]
                        claim(b, "ab_ready")
                        for f in range(2):
                            for blk in range(TB):
                                ins = mm(bank2(b)[:, f, :], PF[:, 2 * s + blk, 1, p * P:(p + 1) * P], DFT[:, f, blk, :],
                                         start=(blk == 0), stop=(blk == TB - 1))
                        ins.then_inc(E["fftab_done"], 1)
                    if l + 1 < LAYERS:
                        ada(ADA_STEPS * (l + 1) + 2 + p)
                    for s in range(sets):
                        pe.wait_ge(E["ab_ready"], before + s + 1)
                        claim(1, "ft_ready")
                        mm(B[1][:, :S], mat(DFT_C), AB[:, 0:S], start=True, stop=False)
                        mm(B[1][:, :S], mat(DFT_S), AB[:, S:2 * S], start=False, stop=True).then_inc(E["fft_done"], 1)

                for i in range(6):
                    if i < 5:
                        stats(MEAN_HD, i, 2 + i % 2, n if i < 4 else 2 * S)
                    if 1 <= i <= 2:
                        pooled(i - 1)
                    elif 3 <= i <= 4:
                        fourier(i - 3)
                    elif i == 5:
                        pe.wait_ge(E["ft_ready"], t.n["ft_ready"])
                        for d in range(2):
                            claim(2 + d, "mix_ready")
                            for p in range(2):
                                ins = mm(B[2 + d][:, :n], FW[:, l, p, d * P:(d + 1) * P], T[2 + p][:, :n], start=(p == 0),
                                         stop=(p == 1))
                            ins.then_inc(E["yf_done"], 1)
                    if i >= 1:
                        got("qn_ready")
                        claim(4, "q_ready")
                        mm(B[4][:, :S], mat(ROT), QQ[:, i - 1, 0:S], start=True, stop=True)\
                            .then_inc(E["rot_done"], 1)
                pe.wait_ge(E["q_ready"], 5 * (l + 1))
                for kv in range(2):
                    claim(4 + kv, "kd_ready")
                    mm(B[4 + kv][:], mat(DUP0 + kv), QQ[:, 4, :], start=True, stop=True).then_inc(E["dup_done"], 1)
                pe.wait_ge(E["kd_ready"], t.n["kd_ready"])
                pe.wait_ge(E["v_ready"], l + 1)
                if l == 0:
                    t.n["exp_ready"] += HEADS * TB
                pairs = attention_pairs(l)
                before = t.n["probT_ready"]
                for u in range(len(pairs) + 2):
                    if u < len(pairs):
                        h, q0, k0, nk = pairs[u]
                        banks = [SCORE_BANKS[(2 * u + c) % 3] for c in range(2)]
                        for b in banks:
                            claim(b, "exp_ready")
                        for c, b in enumerate(banks):
                            rows = slice(HD * c, HD * (c + 1))
                            ins = mm(B[b][:, :nk], QQ[rows, h // 2, q0:q0 + P], KD[rows, h // 4, k0:k0 + nk], start=True,
                                     stop=True)
                        ins.then_inc(E["scores_done"], 1)
                    if u >= 2:
                        h, q0, k0, nk = pairs[u - 2]
                        pe.wait_ge(E["probT_ready"], t.next("probT_ready", 2))
                        claim(4, "mix_ready")
                        for kb in range(nk // P):
                            for c in range(2):
                                ins = mm(B[4][HD * c:HD * (c + 1), 0:P], VD[:, k0 // P + kb, h // 4, :],
                                         T[2 + c][:, kb * P:(kb + 1) * P], start=(kb == 0), stop=(kb == nk // P - 1))
                        ins.then_inc(E["pv_done"], 1)
                    if 1 <= u <= len(pairs):
                        h, q0, k0, nk = pairs[u - 1]
                        got("prob_ready")
                        for c in range(2):
                            claim(2 + c, "probT_ready", before + 2 * (u - 1) + c + 1)
                            for kb in range(nk // P):
                                ins = nc.tensor.transpose(B[2 + c][:, kb * P:(kb + 1) * P],
                                                          PROBS[(2 * (u - 1) + c) % 4][:, kb * P:(kb + 1) * P], mat(IDENT))
                        ins.then_inc(E["probT_done"], 1)
                    if ada_beside(l, u) is not None:
                        ada(ada_beside(l, u))
                if l + 1 < LAYERS:
                    ada_finish(ADA_STEPS * (l + 2) - 1)
                pe.wait_ge(E["mix_ready"], t.n["mix_ready"])
                for j in range(4):
                    s = chunk()
                    for m in (2 * j, 2 * j + 1):
                        claim(m, "x_ready")
                        ins = features(s, (m % 2) * P, B[m][:, :n], XH, XL, n)
                    used(ins, s)

            for l in range(LAYERS):
                n = 2 * S if l + 1 < LAYERS else S
                if l == 0:
                    mean_of_squares()
                    got("acc_ready")
                    mm(B[0][:, S:], mat(MEAN_D), ACC[:, S:], start=True, stop=True).then_inc(E["stats_done"], 1)
                else:
                    mean_of_sums(2 * S)
                ffn(2 * S)
                mean_of_sums(2 * S)
                mixers(l)
                mean_of_sums(n)
                ffn(n)

            mean_of_sums(S)
            for j in range(4):
                half, blk = j // 2, j % 2
                pe.wait_ge(E["hf_done"], KT // 2 * (half + 1))
                claim(1 + j, "outb_ready")
                for k in range(4):
                    ins = nc.tensor.transpose(B[1 + j][:, k * P:(k + 1) * P], HF[:, 4 * half + k, blk * P:(blk + 1) * P],
                                              mat(IDENT))
                ins.then_inc(E["fin_done"], 1)


INPUTS = ("x norm1_g w_in v_norm_g w_s b_s q_norm_g k_norm_g lambda_q1 lambda_k1 lambda_q2 lambda_k2 sub_norm_g w_up_a "
          "w_up_b w_gate b_gate w_out norm2_g w_rg b_rg w_re b_re w1 w3 w2 c_2 ctx_2 c_ctx_2 ada_w_2 ada_b_2 ffn1_w_gu_2 "
          "ffn1_w_down_2 w_in_2 q_gain_2 k_gain_2 pool_w_2 pool_scale_2 fft_w_2 w_out_2 ffn2_w_gu_2 ffn2_w_down_2 "
          "final_gain_2").split()


def constants():
    import numpy as np

    i = np.arange(P)
    mats = np.zeros((P, N_MATS, P))
    mats[:, IDENT] = np.eye(P)
    mats[:, MEAN_D] = 1.0 / D
    mats[:, MEAN_P] = 1.0 / P
    half = i // HD
    mats[:, MEAN_HD] = (half[:, None] == half[None, :]) / HD
    q = HD // 2
    for d in range(P):
        if d % HD < q:
            mats[d + q, ROT, d] = -1.0
        else:
            mats[d - q, ROT, d] = 1.0
    for kv in range(2):
        for d in range(P):
            mats[HD * kv + d % HD, DUP0 + kv, d] = 1.0
    group = (half[:, None] == half[None, :])
    angle = 2 * np.pi * np.outer(i % HD, i % HD) / HD
    norm = 1.0 / math.sqrt(S * HD)
    mats[:, DFT_C] = group * np.cos(angle) * norm
    mats[:, DFT_S] = group * -np.sin(angle) * norm
    s = np.arange(S)
    tok = 2 * np.pi * (np.outer(s, s) % S) / S
    dft = np.stack([np.cos(tok), np.sin(tok)]).reshape(2, TB, P, S).transpose(2, 0, 1, 3)
    pool = np.zeros((4, S, S))
    for g, w in enumerate((2, 4, 8, 16)):
        for to in range(S):
            lo, hi = max(to - w // 2, 0), min(to + w - w // 2, S)
            pool[g, lo:hi, to] = 1.0 / (hi - lo)
        pool[g] -= np.eye(S)
    pool = pool.reshape(4, TB, P, S).transpose(2, 0, 1, 3)
    n_freq = HD // 4
    inv = 10000.0 ** (-np.arange(n_freq) / n_freq)
    ang = np.concatenate([(s // 64)[:, None] * inv, (s % 64)[:, None] * inv], axis=1)
    trig = np.stack([np.cos(ang), np.sin(ang)])[:, :, i % q].transpose(2, 0, 1)
    dist = s[:, None] - s[None, :]
    neg = np.where(dist >= 0, -dist, -BIG).reshape(TB, P, S).transpose(1, 0, 2)
    falling = np.concatenate([np.arange(n, 0, -1) for n in (N_GROUPS, PER_GROUP)])
    select = np.zeros((P, 2))
    for v in range(2):
        select[v::CT_W, v] = 1.0
    tables = {"ada_select": select, "mats": mats, "dft": dft, "pool_mix": pool, "trig": trig, "neg_dist": neg,
              "descending": falling}
    return {k: np.ascontiguousarray(v, dtype=np.float32) for k, v in tables.items()}


def kernel(**inputs):
    import numpy as np
    import concourse.bacc as bacc
    from concourse.bass_utils import run_bass_kernel_spmd

    nc = bacc.Bacc("TRN2", target_bir_lowering=False, num_devices=1)
    given = {f"in_{n}": np.ascontiguousarray(inputs[n]) for n in INPUTS}
    given.update({f"in_{n}": v for n, v in constants().items()})
    handles = {n[3:]: nc.dram_tensor(n, v.shape, F32, kind="ExternalInput").ap() for n, v in given.items()}
    out = nc.dram_tensor("out", (1, S, D), F32, kind="ExternalOutput").ap()
    comb_rows = nc.dram_tensor("comb_rows", (N_EXPERTS, S), F32, kind="Internal").ap()
    build(nc, handles, out, comb_rows)
    got = run_bass_kernel_spmd(nc, [given], core_ids=[0])
    return got.results[0]["out"]
```
